# Optimizing a Trainium2 kernel written in Bass

```python
import jax, jax.numpy as jnp
from jax import lax
import numpy as np

D_MODEL = 1024
BATCH = 1
SEQ = 512
DEPTH = 2
DEC_BATCH = 1
DEC_SEQ = 32
PAST_LEN = 512

CHUNK = 64
D_PLE = 256
D_MIX = D_MODEL
LRU_WIDTH = D_MIX // 2
LRU_BLOCKS = 4
LRU_BLOCK = LRU_WIDTH // LRU_BLOCKS
CONV_W = 4
LRU_C = 8.0
RWKV_WIDTH = D_MIX - LRU_WIDTH
RWKV_HEAD = 64
RWKV_HEADS = RWKV_WIDTH // RWKV_HEAD
W_LORA = 64
A_LORA = 64
G_LORA = 128
RWKV_COLS = 3 * RWKV_WIDTH + W_LORA + A_LORA + G_LORA
IN_COLS = 2 * LRU_WIDTH + RWKV_COLS
PEER_HEADS = 8
N_KEYS = 128
N_EXPERTS = N_KEYS * N_KEYS
PEER_QDIM = 256
PEER_HALF = PEER_QDIM // 2
PEER_TOPK = 16
PEER_BLOCK = 128
EPS = 1e-6
GN_EPS = 64e-5

kernel_name = 'hymba_rglru_rwkv7_peer_stream_step'

def rms_norm(x, g):
    xf = x.astype(jnp.float32)
    y = xf * lax.rsqrt(jnp.mean(xf * xf, axis=-1, keepdims=True) + EPS)
    return (y * g.astype(jnp.float32)).astype(x.dtype)

def rglru_mixer(xb, gb, conv_buf, h0, cw, cb, wa, ba, wx, bx, lam, first):
    B, T, W = xb.shape
    full = jnp.concatenate([conv_buf.astype(xb.dtype), xb], axis=1)
    xc = cb + sum(full[:, j:j + T] * cw[j] for j in range(CONV_W))
    new_buf = full[:, T:]
    xblk = xc.reshape(B, T, LRU_BLOCKS, LRU_BLOCK)
    r = jax.nn.sigmoid(jnp.einsum('btni,nij->btnj', xblk, wa).reshape(B, T, W) + ba)
    ig = jax.nn.sigmoid(jnp.einsum('btni,nij->btnj', xblk, wx).reshape(B, T, W) + bx)
    log_a = (-LRU_C * r * jax.nn.softplus(-lam)).astype(jnp.float32)
    a = jnp.exp(log_a)
    mult = jnp.sqrt(-jnp.expm1(2.0 * log_a))
    if first:
        mult = mult.at[:, 0].set(1.0)
    b = mult * (ig * xc).astype(jnp.float32)
    b = b.at[:, 0].add(a[:, 0] * h0.astype(jnp.float32))

    def comb(left, right):
        a_l, b_l = left
        a_r, b_r = right
        return a_l * a_r, a_r * b_l + b_r

    _, h = lax.associative_scan(comb, (a, b), axis=1)
    y = h.astype(xb.dtype) * jax.nn.gelu(gb)
    return y, new_buf, h[:, -1]

def rwkv7_mixer(z, shift_prev, S0, mu, w0, w2, a0, a2, g2, k_k, k_a, r_k, ln_w, ln_b):
    B, T, _ = z.shape
    f32 = jnp.float32
    z_prev = jnp.concatenate([shift_prev[:, None].astype(z.dtype), z[:, :-1]], axis=1)
    zs = z + (z_prev - z) * mu
    W = RWKV_WIDTH
    r, k, v, zw, za, zg = jnp.split(zs, [W, 2 * W, 3 * W, 3 * W + W_LORA, 3 * W + W_LORA + A_LORA], axis=-1)
    w_log = -jax.nn.softplus(-(w0 + jnp.tanh(zw) @ w2)) - 0.5
    decay = jnp.exp(-jnp.exp(w_log.astype(f32)))
    iclr = jax.nn.sigmoid(a0 + za @ a2)
    g = jax.nn.sigmoid(zg) @ g2

    def heads(t):
        return t.reshape(B, T, RWKV_HEADS, RWKV_HEAD)

    kk = heads(k * k_k).astype(f32)
    kk = kk / jnp.maximum(jnp.sqrt(jnp.sum(kk * kk, axis=-1, keepdims=True)), 1e-12)
    k = k * (1.0 + (iclr - 1.0) * k_a)
    rh, kh, vh, ah = heads(r), heads(k), heads(v), heads(iclr)
    wh = heads(decay)
    a_vec = -kk
    b_vec = kk * ah.astype(f32)

    def step(S, inp):
        r_t, w_t, k_t, v_t, a_t, b_t = inp
        sa = jnp.einsum('bhij,bhj->bhi', S, a_t)
        S = S * w_t[:, :, None, :] + sa[..., None] * b_t[:, :, None, :] + v_t[..., None] * k_t[:, :, None, :]
        return S, jnp.einsum('bhij,bhj->bhi', S, r_t)

    def tm(t):
        return jnp.moveaxis(t.astype(f32), 1, 0)

    S_T, o = lax.scan(step, S0.astype(f32), (tm(rh), tm(wh), tm(kh), tm(vh), tm(a_vec), tm(b_vec)))
    o = jnp.moveaxis(o, 0, 1)
    mean = jnp.mean(o, axis=-1, keepdims=True)
    var = jnp.mean(jnp.square(o - mean), axis=-1, keepdims=True)
    o = ((o - mean) * lax.rsqrt(var + GN_EPS)).reshape(B, T, W) * ln_w + ln_b
    bonus = jnp.sum((rh * kh * r_k).astype(f32), axis=-1, keepdims=True) * vh.astype(f32)
    o = (o + bonus.reshape(B, T, W)) * g
    return o.astype(z.dtype), z[:, -1], S_T

def peer_ffn(xn, wq, keys, u, v):
    B, T, D = xn.shape
    n = B * T
    nblk = -(-n // PEER_BLOCK)
    xf = jnp.pad(xn.reshape(n, D), ((0, nblk * PEER_BLOCK - n), (0, 0))).reshape(nblk, PEER_BLOCK, D)

    def block(xb):
        q = (xb @ wq).reshape(PEER_BLOCK, PEER_HEADS, 2, PEER_HALF)
        s = jnp.einsum('thsc,hskc->thsk', q, keys).astype(jnp.float32)
        top_s, top_i = lax.top_k(s, PEER_TOPK)
        cand = top_s[:, :, 0, :, None] + top_s[:, :, 1, None, :]
        best_s, best_c = lax.top_k(cand.reshape(PEER_BLOCK, PEER_HEADS, PEER_TOPK * PEER_TOPK), PEER_TOPK)
        i1 = jnp.take_along_axis(top_i[:, :, 0], best_c // PEER_TOPK, axis=-1)
        i2 = jnp.take_along_axis(top_i[:, :, 1], best_c % PEER_TOPK, axis=-1)
        e = (i1 * N_KEYS + i2).reshape(PEER_BLOCK, PEER_HEADS * PEER_TOPK)
        gate = jax.nn.softmax(best_s, axis=-1).reshape(PEER_BLOCK, PEER_HEADS * PEER_TOPK)
        hid = jnp.einsum('td,tkd->tk', xb, jnp.take(u, e, axis=0)).astype(jnp.float32)
        wgt = (gate * jax.nn.gelu(hid)).astype(xb.dtype)
        return jnp.einsum('tk,tkd->td', wgt, jnp.take(v, e, axis=0))

    out = lax.map(block, xf).reshape(nblk * PEER_BLOCK, D)[:n]
    return out.reshape(B, T, D)

def _trunk(x, p, conv_st, lru_st, shift_st, wkv_st, first, params):
    (norm1_g, w_in, conv_w, conv_b, lru_wa, lru_ba, lru_wx, lru_bx, lru_lambda,
     rwkv_mu, rwkv_w0, rwkv_w2, rwkv_a0, rwkv_a2, rwkv_g2, rwkv_kk, rwkv_ka, rwkv_rk,
     rwkv_ln_w, rwkv_ln_b, w_out, norm2_g, peer_wq, peer_keys, peer_u, peer_v,
     norm3_g, ple_w, ple_gate, final_g) = params
    h = x
    convs, lrus, shifts, wkvs = [], [], [], []
    for i in range(DEPTH):
        xn = rms_norm(h, norm1_g[i])
        zin = xn @ w_in[i]
        xb = zin[..., :LRU_WIDTH]
        gb = zin[..., LRU_WIDTH:2 * LRU_WIDTH]
        z = zin[..., 2 * LRU_WIDTH:]
        y_lru, cbuf, h_lru = rglru_mixer(xb, gb, conv_st[i], lru_st[i], conv_w[i], conv_b[i],
                                         lru_wa[i], lru_ba[i], lru_wx[i], lru_bx[i], lru_lambda[i], first)
        y_rw, sh, S = rwkv7_mixer(z, shift_st[i], wkv_st[i], rwkv_mu[i], rwkv_w0[i], rwkv_w2[i],
                                  rwkv_a0[i], rwkv_a2[i], rwkv_g2[i], rwkv_kk[i], rwkv_ka[i],
                                  rwkv_rk[i], rwkv_ln_w[i], rwkv_ln_b[i])
        h = h + jnp.concatenate([y_lru, y_rw], axis=-1) @ w_out[i]
        h = h + peer_ffn(rms_norm(h, norm2_g[i]), peer_wq[i], peer_keys[i], peer_u[i], peer_v[i])
        h = h + (p[i] @ ple_w[i]) * jax.nn.sigmoid(rms_norm(h, norm3_g[i]) @ ple_gate[i])
        convs.append(cbuf)
        lrus.append(h_lru)
        shifts.append(sh)
        wkvs.append(S)
    y = rms_norm(h, final_g)
    return (y, jnp.stack(convs).astype(x.dtype), jnp.stack(lrus).astype(x.dtype),
            jnp.stack(shifts).astype(x.dtype), jnp.stack(wkvs).astype(x.dtype))

def setup_inputs(seed: int = 0) -> dict:
    key = jax.random.key(seed)
    ks = iter(jax.random.split(key, 48))

    def nrm(shape, scale):
        return jax.random.normal(next(ks), shape, jnp.float32) * scale

    def unif(shape, lo, hi):
        return jax.random.uniform(next(ks), shape, jnp.float32, lo, hi)

    L = DEPTH
    a_base = unif((L, LRU_WIDTH), 0.9, 0.999)
    s = a_base ** (1.0 / LRU_C)
    lru_lambda = jnp.log(s) - jnp.log1p(-s)
    return {
        'x_prompt': nrm((BATCH, SEQ, D_MODEL), 1.0),
        'x_sample': nrm((DEC_BATCH, DEC_SEQ, D_MODEL), 1.0),
        'p_prompt': nrm((L, BATCH, SEQ, D_PLE), 1.0),
        'p_sample': nrm((L, DEC_BATCH, DEC_SEQ, D_PLE), 1.0),
        'state_conv': nrm((L, DEC_BATCH, CONV_W - 1, LRU_WIDTH), 1.0),
        'state_lru': nrm((L, DEC_BATCH, LRU_WIDTH), 0.5),
        'state_shift': nrm((L, DEC_BATCH, RWKV_COLS), 1.0),
        'state_wkv': nrm((L, DEC_BATCH, RWKV_HEADS, RWKV_HEAD, RWKV_HEAD), 1.0),
        'norm1_g': 1.0 + nrm((L, D_MODEL), 0.05),
        'w_in': nrm((L, D_MODEL, IN_COLS), D_MODEL ** -0.5),
        'conv_w': nrm((L, CONV_W, LRU_WIDTH), CONV_W ** -0.5),
        'conv_b': nrm((L, LRU_WIDTH), 0.02),
        'lru_wa': nrm((L, LRU_BLOCKS, LRU_BLOCK, LRU_BLOCK), LRU_BLOCK ** -0.5),
        'lru_ba': nrm((L, LRU_WIDTH), 0.02),
        'lru_wx': nrm((L, LRU_BLOCKS, LRU_BLOCK, LRU_BLOCK), LRU_BLOCK ** -0.5),
        'lru_bx': nrm((L, LRU_WIDTH), 0.02),
        'lru_lambda': lru_lambda,
        'rwkv_mu': unif((L, RWKV_COLS), 0.0, 1.0),
        'rwkv_w0': unif((L, RWKV_WIDTH), -6.0, -1.0),
        'rwkv_w2': nrm((L, W_LORA, RWKV_WIDTH), 0.1 * W_LORA ** -0.5),
        'rwkv_a0': nrm((L, RWKV_WIDTH), 0.1),
        'rwkv_a2': nrm((L, A_LORA, RWKV_WIDTH), 0.1 * A_LORA ** -0.5),
        'rwkv_g2': nrm((L, G_LORA, RWKV_WIDTH), G_LORA ** -0.5),
        'rwkv_kk': 0.85 + nrm((L, RWKV_WIDTH), 0.02),
        'rwkv_ka': 1.0 + nrm((L, RWKV_WIDTH), 0.02),
        'rwkv_rk': nrm((L, RWKV_HEADS, RWKV_HEAD), 0.1),
        'rwkv_ln_w': 1.0 + nrm((L, RWKV_WIDTH), 0.05),
        'rwkv_ln_b': nrm((L, RWKV_WIDTH), 0.02),
        'w_out': nrm((L, D_MIX, D_MODEL), D_MIX ** -0.5),
        'norm2_g': 1.0 + nrm((L, D_MODEL), 0.05),
        'peer_wq': nrm((L, D_MODEL, PEER_HEADS * PEER_QDIM), D_MODEL ** -0.5),
        'peer_keys': nrm((L, PEER_HEADS, 2, N_KEYS, PEER_HALF), PEER_HALF ** -0.5),
        'peer_u': nrm((L, N_EXPERTS, D_MODEL), D_MODEL ** -0.5),
        'peer_v': nrm((L, N_EXPERTS, D_MODEL), PEER_HEADS ** -0.5),
        'norm3_g': 1.0 + nrm((L, D_MODEL), 0.05),
        'ple_w': nrm((L, D_PLE, D_MODEL), D_PLE ** -0.5),
        'ple_gate': nrm((L, D_MODEL, D_MODEL), D_MODEL ** -0.5),
        'final_g': 1.0 + nrm((D_MODEL,), 0.05),
    }

def reference(x_prompt, x_sample, p_prompt, p_sample, state_conv, state_lru, state_shift, state_wkv,
              norm1_g, w_in, conv_w, conv_b, lru_wa, lru_ba, lru_wx, lru_bx, lru_lambda,
              rwkv_mu, rwkv_w0, rwkv_w2, rwkv_a0, rwkv_a2, rwkv_g2, rwkv_kk, rwkv_ka, rwkv_rk,
              rwkv_ln_w, rwkv_ln_b, w_out, norm2_g, peer_wq, peer_keys, peer_u, peer_v,
              norm3_g, ple_w, ple_gate, final_g):
    params = (norm1_g, w_in, conv_w, conv_b, lru_wa, lru_ba, lru_wx, lru_bx, lru_lambda,
              rwkv_mu, rwkv_w0, rwkv_w2, rwkv_a0, rwkv_a2, rwkv_g2, rwkv_kk, rwkv_ka, rwkv_rk,
              rwkv_ln_w, rwkv_ln_b, w_out, norm2_g, peer_wq, peer_keys, peer_u, peer_v,
              norm3_g, ple_w, ple_gate, final_g)
    bp = x_prompt.shape[0]
    dt = x_prompt.dtype
    zc = jnp.zeros((DEPTH, bp, CONV_W - 1, LRU_WIDTH), dt)
    zl = jnp.zeros((DEPTH, bp, LRU_WIDTH), dt)
    zs = jnp.zeros((DEPTH, bp, RWKV_COLS), dt)
    zw = jnp.zeros((DEPTH, bp, RWKV_HEADS, RWKV_HEAD, RWKV_HEAD), dt)
    y_prompt, conv_p, lru_p, shift_p, wkv_p = _trunk(x_prompt, p_prompt, zc, zl, zs, zw, True, params)
    y_sample, conv_s, lru_s, shift_s, wkv_s = _trunk(x_sample, p_sample, state_conv, state_lru,
                                                     state_shift, state_wkv, False, params)
    return (y_prompt, y_sample, conv_p, lru_p, shift_p, wkv_p, conv_s, lru_s, shift_s, wkv_s)


_drawn_inputs = setup_inputs


def setup_inputs(seed=0):
    import zlib

    import numpy as np

    out = dict(_drawn_inputs(seed))
    spreads = {}
    factors = {'lru_ba': 5.197, 'lru_bx': 4.032, 'rwkv_w2': 4.299, 'norm3_g': 2.981}
    for name, (base, spread) in spreads.items():
        noise = np.random.default_rng([zlib.crc32(name.encode()), seed]).standard_normal(out[name].shape)
        drawn = base * np.exp(spread * noise) if base else spread * noise
        out[name] = __import__('jax').numpy.asarray(drawn.astype(out[name].dtype))
    for name, factor in factors.items():
        out[name] = (out[name] * factor).astype(out[name].dtype)
    return out
```

```python
from contextlib import ExitStack

import numpy as np

import concourse.bass as bass
from concourse import mybir

F32 = mybir.dt.float32
F32R = mybir.dt.float32r
U32 = mybir.dt.uint32
ALU = mybir.AluOpType
ACT = mybir.ActivationFunctionType
AX = mybir.AxisListType

P = 128
DEPTH, D, SEQ, DEC = 2, 1024, 512, 32
KD = D // P
T = SEQ + DEC
HALF = T // 2
LW = 512
NT = LW // P
RCOLS = 1792
ZT = 2 * NT + RCOLS // P
ZR = RCOLS // P
LEAD = 3
ZW = SEQ + DEC + 2 * LEAD
DEC0 = SEQ + LEAD
EW = DEC0 + DEC
MW = 580
MH = MW // 2
C = 64
NCH = SEQ // C
HEADS = 8
HD = 64
LEVELS = 6
QH = 16
NK = 128
PH = 8
TOPK = 16
EPS, GN_EPS = 1e-6, 64e-5
NEG = -3.0e38

IN_T, OUT_T, Q_T, PLE_T = ZT, KD, QH, KD
OUT_0, Q_0, PLE_0 = IN_T, IN_T + OUT_T, IN_T + OUT_T + Q_T
TILES = IN_T + OUT_T + Q_T + PLE_T
WK = KD + 2

SM = {}
_at = 0
for _name, _n in [("n1", 8), ("n2", 8), ("n3", 8), ("fin", 8), ("cw", 16), ("cb", 4), ("ba", 4), ("bx", 4),
                  ("lam", 4), ("mu", 14), ("w0", 4), ("a0", 4), ("kk", 4), ("ka", 4), ("rk", 4),
                  ("lnw", 4), ("lnb", 4), ("cst", 12), ("lst", 4), ("sst", 14)]:
    SM[_name] = _at
    _at += _n
NSM = _at
CN = {}
_at = 0
for _name, _n in [("ident", P), ("ones", P), ("heads", P), ("iota", P), ("causal", P),
                  ("level", LEVELS * C), ("reset", MW)]:
    CN[_name] = _at
    _at += _n
NCN = _at
SO = {"conv": (0, 12), "lru": (24, 4), "shift": (32, 14)}
NSO = 60

BLK = 128
NB = SEQ // BLK
GT = 4
GROUPS = T // GT
EC = 4
ESTEPS = NK // EC


def constants():
    c = np.zeros((P, NCN), np.float32)
    i = np.arange(P)
    c[:, CN["ident"]:CN["ident"] + P] = np.eye(P)
    c[:, CN["ones"]:CN["ones"] + P] = 1.0
    c[:, CN["heads"]:CN["heads"] + P] = (i[:, None] // HD == i[None] // HD)
    c[:, CN["iota"]:CN["iota"] + P] = i[None]
    s, t = i[:, None] % C, np.arange(C)[None]
    c[:, CN["causal"]:CN["causal"] + C] = s < t
    c[:, CN["causal"] + C:CN["causal"] + P] = s <= t
    for k in range(LEVELS):
        b = 1 << k
        off = (s // (2 * b) == t // (2 * b)) & (s // b % 2 == 0) & (t // b % 2 == 1)
        c[:, CN["level"] + k * C:CN["level"] + (k + 1) * C] = off
    r = np.ones(MW)
    r[[k * C for k in range(NCH)] + [DEC0]] = 0.0
    c[:, CN["reset"]:CN["reset"] + MW] = r[None]
    return c


def trunk(nc, x, p, small, const, mixw, wkv0, w_in, w_out, wq, keys, ut, v, wple, y, small_out, wkv_out,
          do_peer=True):
    ctx = ExitStack()
    with ctx:
        def sem(name):
            return ctx.enter_context(nc.semaphore(name))

        words = 53215
        names = []
        RESERVED = 16512
        ps = ctx.enter_context(nc.psum_tensor("ps", [P, 8, 512], F32))
        top = [0]

        def aligned(at):
            return -(-at // 8) * 8

        def take(n, at=None, kind=F32):
            if at is None:
                at = aligned(top[0])
                top[0] = at + n
            assert at + n <= words, (at, n)
            names.append(f"m{len(names)}")
            return nc.alloc_sbuf_tensor_at(names[-1], [P, n], kind, offset=RESERVED + 4 * at)[:, :]

        def split(n):
            return take(n, kind=F32R)

        h = take(KD * T).rearrange("p (k t) -> p k t", k=KD)
        xn = take(KD * T).rearrange("p (k t) -> p k t", k=KD)
        ymix = xn
        wslot = take(2 * WK * P).rearrange("p (s k n) -> p s k n", s=2, k=WK)
        sm = take(NSM)
        cn = take(NCN)
        rms = take(T)
        sout = take(NSO)
        sp = take(40)
        epst = take(2)
        A0 = aligned(top[0])

        def const_of(name, n):
            return cn[:, CN[name]:CN[name] + n]

        def small_of(name, i, n=1):
            return sm[:, SM[name] + i:SM[name] + i + n]

        ident, ones, hones, iota = (const_of(n, P) for n in ("ident", "ones", "heads", "iota"))
        causal, reset = const_of("causal", P), const_of("reset", MW)
        eye = ident[0:C, 0:C]

        z_at = A0
        zin = take(ZT * ZW, z_at).rearrange("p (k t) -> p k t", k=ZT)
        zs_at = aligned(z_at + ZT * ZW)
        zs = take(ZR * MW, zs_at).rearrange("p (k t) -> p k t", k=ZR)
        sq = take(KD * T, zs_at).rearrange("p (k t) -> p k t", k=KD)
        mw_at = zs_at + ZR * MW
        mw = take(4 * LW, mw_at).rearrange("p (w n) -> p w n", w=4)
        t_at = mw_at + 4 * LW
        TB = [take(NT * MW, t_at + i * NT * MW).rearrange("p (k t) -> p k t", k=NT) for i in range(7)]
        assert t_at + 7 * NT * MW <= words
        top[0] = z_at
        bk = take(NT * P).rearrange("p (m t) -> p m t", m=NT)
        ar = take(NT * P).rearrange("p (m t) -> p m t", m=NT)
        vc = take(NT * P).rearrange("p (m t) -> p m t", m=NT)
        gm = take(HEADS * P).rearrange("p (h t) -> p h t", h=HEADS)
        bkT = take(LW)
        sav = take(LW)
        fs = take(LW)
        xi = take(LW).rearrange("p (h t) -> p h t", h=HEADS)
        xt = take(LW).rearrange("p (h t) -> p h t", h=HEADS)
        ys = take(LW).rearrange("p (h t) -> p h t", h=HEADS)
        ml = [take(LW).rearrange("p (h t) -> p h t", h=HEADS) for _ in range(2)]
        st = take(NT * P).rearrange("p (m v) -> p m v", m=NT)
        vz = take(LW)
        stp = take(NT * HD).rearrange("p (m v) -> p m v", m=NT)
        sts = take(NT * HD).rearrange("p (m v) -> p m v", m=NT)
        o = take(NT * MW).rearrange("p (m t) -> p m t", m=NT)
        assert top[0] <= zs_at

        top[0] = A0
        qT = take(QH * T).rearrange("p (q t) -> p q t", q=QH)
        qb = take(QH * BLK).rearrange("p (q t) -> p q t", q=QH)
        kT = take(QH * NK).rearrange("p (q n) -> p q n", q=QH)
        s1 = take(2048)
        s2 = take(2048)
        e_top = aligned(top[0])
        stage = take(NK * BLK).rearrange("p (n t) -> p n t", n=NK)
        sq2 = take(KD * T, e_top).rearrange("p (k t) -> p k t", k=KD)
        oneA = take(2 * GT * P).rearrange("p (s j n) -> p s j n", s=2, j=GT)
        oneB = take(2 * GT * P).rearrange("p (s j n) -> p s j n", s=2, j=GT)
        sel = take(3 * P).rearrange("p (w t) -> p w t", w=3)
        sel_t = take(3 * P).rearrange("p (w k) -> p w k", w=3)
        tv = take(QH * TOPK).rearrange("p (q k) -> p q k", q=QH)
        ti = take(QH * TOPK).rearrange("p (q k) -> p q k", q=QH)
        tf = take(QH * TOPK).rearrange("p (q k) -> p q k", q=QH)
        bv = take(PH * TOPK).rearrange("p (q k) -> p q k", q=PH)
        bi = take(PH * TOPK).rearrange("p (q k) -> p q k", q=PH)
        ba = take(2 * PH * TOPK).rearrange("p (w q k) -> p w q k", w=2, q=PH)
        bf = take(2 * PH * TOPK).rearrange("p (w q k) -> p w q k", w=2, q=PH)
        gsum = take(PH)
        top[0] = A0
        xh = split(KD * T).rearrange("p (k t) -> p k t", k=KD)
        xl = split(KD * T).rearrange("p (k t) -> p k t", k=KD)
        uraw = [take(KD * P).rearrange("p (k n) -> p k n", k=KD) for _ in range(2)]
        uh = [split(KD * P).rearrange("p (k n) -> p k n", k=KD) for _ in range(2)]
        ul = [split(KD * P).rearrange("p (k n) -> p k n", k=KD) for _ in range(2)]
        ge = [take(T) for _ in range(2)]
        assert top[0] <= e_top
        top[0] = e_top
        gs = [take(T) for _ in range(EC)]
        vraw = [take(D) for _ in range(2)]
        vh = [split(D) for _ in range(EC)]
        vl = [split(D) for _ in range(EC)]
        wf = [take(T) for _ in range(2)]
        wth = [split(T) for _ in range(EC)]
        wtl = [split(T) for _ in range(EC)]
        top[0] = A0
        pT = take(2 * T).rearrange("p (k t) -> p k t", k=2)
        sg = [take(T) for _ in range(2)]
        pg = [take(T) for _ in range(2)]
        sq3 = take(KD * T).rearrange("p (k t) -> p k t", k=KD)
        SQ = [sq, sq2, sq3]

        gate_d = nc.dram_tensor("gate_matrix", [P, NK, T], F32, kind="Internal").ap()

        const_in = sem("const_in")
        x_in = sem("x_in")
        small_in = sem("small_in")
        mixw_in = sem("mixw_in")
        wkv_in = sem("wkv_in")
        keys_in = sem("keys_in")
        p_in = sem("p_in")
        w_in_s = [sem(f"w_slot{i}") for i in range(2)]
        layer_free = sem("layer_free")
        tile_done = sem("tile_done")
        h_ready = sem("h_ready")
        sq_ready = sem("sq_ready")
        sumsq = sem("sumsq")
        rms_ready = sem("rms_ready")
        xn_ready = sem("xn_ready")
        in_free = sem("in_free")
        lam_abs, lam_exp, lam_u, lam_ln = (sem(n) for n in ("lam_abs", "lam_exp", "lam_u", "lam_ln"))
        nsp_ready = sem("nsp_ready")
        xc_ready = sem("xc_ready")
        r_done, r_out, i_done, i_out = (sem(n) for n in ("r_done", "r_out", "i_done", "i_out"))
        a_ready, m2_ready, mult_ready = sem("a_ready"), sem("m2_ready"), sem("mult_ready")
        gg_ready, lru_done = sem("gg_ready"), sem("lru_done")
        zs_ready, lora_ready = sem("zs_ready"), sem("lora_ready")
        dec_done, dec_out, icl_done, icl_out, g_done, g_out = (
            sem(n) for n in ("dec_done", "dec_out", "icl_done", "icl_out", "g_done", "g_out"))
        kk_sq, kk_sum, kk_rt = sem("kk_sq"), sem("kk_sum"), sem("kk_rt")
        bonus_in, bonus_done = sem("bonus_in"), sem("bonus_done")
        cum_ready, exp_ready = sem("cum_ready"), sem("exp_ready")
        tilde_ready = sem("tilde_ready")
        v_ready = sem("v_ready")
        pair_done = sem("pair_done")
        turn_done = sem("turn_done")
        turn_out = sem("turn_out")
        gm_ready = sem("gm_ready")
        f_done, f_out = sem("f_done"), sem("f_out")
        m_ready = sem("m_ready")
        y_done = sem("y_done")
        y_out = sem("y_out")
        x_done = sem("x_done")
        sa_done, sa_out = sem("sa_done"), sem("sa_out")
        step_done = sem("step_done")
        o_out = sem("o_out")
        mean_done, oc_ready, var_done, std_out = (
            sem(n) for n in ("mean_done", "oc_ready", "var_done", "std_out"))
        y_ready = sem("y_ready")
        out_free = sem("out_free")
        q_free = sem("q_free")
        qb_ready = sem("qb_ready")
        sc_done, sc_read = sem("sc_done"), sem("sc_read")
        best_ready, gexp = sem("best_ready"), sem("gexp")
        sel_ready, selT_done, selT_out = sem("sel_ready"), sem("selT_done"), sem("selT_out")
        ab_ready, gmat_done, gmat_out = sem("ab_ready"), sem("gmat_done"), sem("gmat_out")
        gate_saved = sem("gate_saved")
        u_in = [sem(f"u_in{i}") for i in range(2)]
        v_in = [sem(f"v_in{i}") for i in range(2)]
        xh_ready, xl_ready = sem("xh_ready"), sem("xl_ready")
        uh_ready, ul_ready = sem("uh_ready"), sem("ul_ready")
        vh_ready, vl_ready = sem("vh_ready"), sem("vl_ready")
        wh_ready, wl_ready = sem("wh_ready"), sem("wl_ready")
        g_in = [sem(f"g_in{i}") for i in range(EC)]
        hid_done = sem("hid_done")
        ge_out = sem("ge_out")
        w_ready = sem("w_ready")
        eo_done = sem("eo_done")
        eo_out = sem("eo_out")
        stage_free = sem("stage_free")
        ple_sig = sem("ple_sig")
        ple_free = sem("ple_free")
        outs_ready = sem("outs_ready")
        stored = sem("stored")
        y_stored = sem("y_stored")
        y_out_ready = sem("y_out_ready")

        waits_passed = {e.engine: sem(f"waits_passed{i}") for i, e in enumerate([nc.sync, nc.tensor, nc.vector, nc.scalar])}

        NCHUNK = NCH + 1
        NBLK = NB + 1

        def passed(eng):
            eng.sem_inc(waits_passed[eng.engine], 1)

        def halves(bank, w):
            return ps[:, bank:bank + 2, 0:w]

        def cut(ap, w):
            return ap.rearrange("p (a w) -> p a w", a=2)

        block = ctx.enter_context(nc.Block())

        @block.sync
        def _(sp_):
            sp_.dma_start(cn, const[:, :]).then_inc(const_in, 16)
            sp_.dma_start(h, x[:, :, :]).then_inc(x_in, 16)

            def weight(L, base, n, j, src, k=KD):
                sp_.wait_ge(tile_done, L * TILES + base + n + 1)
                sp_.dma_start(wslot[:, j, 0:k, :], src).then_inc(w_in_s[j], 16)

            with sp_.Fori(0, DEPTH) as L:
                sp_.wait_ge(layer_free, L + 1)
                sp_.dma_start(sm, small[L]).then_inc(small_in, 16)
                sp_.dma_start(mw, mixw[L]).then_inc(mixw_in, 16)
                with sp_.Fori(0, IN_T // 2) as g:
                    for j in range(2):
                        weight(L, 0, g * 2 + j, j, w_in[L].rearrange("(k p) n -> p k n", p=P)[:, :, bass.ds((g * 2 + j) * P, P)])
                sp_.wait_ge(lru_done, L + 1)
                sp_.wait_ge(zs_ready, L + 1)
                sp_.dma_start(sts, wkv0[L]).then_inc(wkv_in, 16)
                with sp_.Fori(0, OUT_T // 2) as g:
                    for j in range(2):
                        weight(L, OUT_0, g * 2 + j, j, w_out[L].rearrange("(k p) n -> p k n", p=P)[:, :, bass.ds((g * 2 + j) * P, P)])
                with sp_.Fori(0, Q_T // 2) as g:
                    for j in range(2):
                        weight(L, Q_0, g * 2 + j, j, wq[L].rearrange("(k p) n -> p k n", p=P)[:, :, bass.ds((g * 2 + j) * P, P)])
                if do_peer:
                    sp_.wait_ge(xn_ready, L * 3 + 2)
                    sp_.dma_start(kT, keys[L]).then_inc(keys_in, 16)
                    sp_.wait_ge(sel_ready, (L + 1) * NBLK)
                    sp_.wait_ge(sc_done, (L + 1) * NBLK)
                    sp_.wait_ge(selT_done, (L + 1) * NBLK)
                    passed(sp_)
                    with sp_.Fori(0, ESTEPS) as e:
                        def load_u(j):
                            sp_.wait_ge(ul_ready, L * NK + e * EC + j + 1)
                            sp_.dma_start(uraw[j % 2], ut[L, bass.ds(e * EC + j, 1)].rearrange("a p k n -> (a p) k n")).then_inc(u_in[j % 2], 16)

                        def load_v(j):
                            sp_.wait_ge(vl_ready, L * NK + e * EC + j + 1)
                            sp_.dma_start(vraw[j % 2], v[L].rearrange("(p n) d -> p n d", n=NK)[:, bass.ds(e * EC + j, 1), :].rearrange("p a d -> p (a d)")).then_inc(v_in[j % 2], 16)

                        load_u(0)
                        load_u(1)
                        sp_.wait_ge(gate_saved, (L + 1) * (16 * NBLK))
                        load_v(0)
                        load_v(1)
                        for j in range(EC):
                            sp_.wait_ge(w_ready, L * NK + e * EC + j + 1)
                            sp_.dma_start(gs[j], gate_d[:, bass.ds(e * EC + j, 1), :].rearrange("p a t -> p (a t)")).then_inc(g_in[j], 16)
                        for j in range(2, EC):
                            load_u(j)
                            load_v(j)
                sp_.wait_ge(h_ready, L * 3 + 3)
                sp_.dma_start(pT, p[L]).then_inc(p_in, 16)
                with sp_.Fori(0, PLE_T // 2) as g:
                    for j in range(2):
                        weight(L, PLE_0, g * 2 + j, j, wple[L].rearrange("(k p) n -> p k n", p=P)[:, :, bass.ds((g * 2 + j) * P, P)], WK)
            sp_.wait_ge(y_out_ready, 1)
            sp_.dma_start(y[:, :, :], xn).then_inc(y_stored, 16)
            sp_.wait_ge(y_stored, 16)
            sp_.wait_ge(stored, 16 * 3 * DEPTH)

        @block.gpsimd
        def _(pool):
            sub = nc.gpsimd.tensor_tensor
            pool.sem_inc(ul_ready, 2)
            pool.sem_inc(vl_ready, 2)
            with pool.Fori(0, DEPTH) as L:
                pool.wait_ge(outs_ready, L + 1)
                pool.dma_start(small_out[L], sout).then_inc(stored, 16)
                pool.dma_start(wkv_out[L, 0], stp).then_inc(stored, 16)
                pool.dma_start(wkv_out[L, 1], sts).then_inc(stored, 16)
                if do_peer:
                    with pool.Fori(0, NB) as b:
                        pool.wait_ge(gate_saved, (L * NBLK + b) * 16 + 16)
                        pool.sem_inc(stage_free, 1)
                    pool.wait_ge(xh_ready, L + 1)
                    sub(xl, xn, xh.bitcast(F32), ALU.subtract).then_inc(xl_ready, 1)
                    pool.wait_ge(gate_saved, (L + 1) * (NBLK * 16))
                    pool.sem_inc(stage_free, 1)
                    with pool.Fori(0, ESTEPS) as e:
                        def low_u(j):
                            pool.wait_ge(uh_ready, L * NK + e * EC + j + 1)
                            sub(ul[j % 2], uraw[j % 2], uh[j % 2].bitcast(F32), ALU.subtract).then_inc(ul_ready, 1)

                        def low_v(j):
                            pool.wait_ge(vh_ready, L * NK + e * EC + j + 1)
                            sub(vl[j], vraw[j % 2], vh[j].bitcast(F32), ALU.subtract).then_inc(vl_ready, 1)

                        low_u(0)
                        low_u(1)
                        low_v(0)
                        low_u(2)
                        low_v(1)
                        low_u(3)
                        low_v(2)
                        low_v(3)

        @block.tensor
        def _(pe):
            mm = nc.tensor.matmul
            pe.sem_inc(tile_done, 2)
            pe.sem_inc(hid_done, 2)
            pe.sem_inc(gmat_done, 2)
            pe.sem_inc(eo_done, KD)
            pe.wait_ge(const_in, 16)

            def norm(L, i):
                pe.wait_ge(sq_ready, L * 3 + i + 1)
                for a in range(2):
                    for k in range(KD):
                        last = mm(ps[:, a, 0:HALF], ones, SQ[i][:, k, a * HALF:(a + 1) * HALF],
                                  start=(k == 0), stop=(k == KD - 1))
                last.then_inc(sumsq, 1)

            def tile(j, slot, rhs, ks, bank, inc):
                for a in range(2):
                    for n, k in enumerate(ks):
                        last = mm(ps[:, bank + a, 0:HALF], wslot[:, slot, k, :], rhs[:, n, a * HALF:(a + 1) * HALF],
                                  start=(n == 0), stop=(n == len(ks) - 1))
                if inc:
                    last.then_inc(tile_done, 1)

            def linear(L, base, count, rhs, free):
                passed(pe)
                with pe.Fori(0, count // 2) as g:
                    for j in range(2):
                        pe.wait_ge(w_in_s[j], L * (16 * TILES // 2) + g * 16 + 16 * (base // 2) + 16)
                        pe.wait_ge(free, L * (count + 2) + g * 2 + j + 1)
                        tile(j, j, rhs, range(KD), 2 * j, True)

            def wide(lhs, rhs, n0=0):
                for n in range(NT):
                    for a in range(2):
                        last = mm(ps[:, 2 * n + a, 0:MH], lhs(n), rhs(n)[:, a * MH:(a + 1) * MH],
                                  start=True, stop=True)
                return last

            with pe.Fori(0, DEPTH) as L:
                norm(L, 0)
                pe.wait_ge(xn_ready, L * 3 + 1)
                linear(L, 0, IN_T, xn, in_free)
                pe.wait_ge(in_free, L * (IN_T + 2) + IN_T + 2)
                pe.wait_ge(mixw_in, L * 16 + 16)
                pe.wait_ge(xc_ready, L + 1)
                wide(lambda n: mw[:, 0, n * P:(n + 1) * P], lambda n: TB[0][:, n, :]).then_inc(r_done, 1)
                pe.wait_ge(r_out, L + 1)
                wide(lambda n: mw[:, 1, n * P:(n + 1) * P], lambda n: TB[0][:, n, :]).then_inc(i_done, 1)
                pe.wait_ge(i_out, L + 1)
                pe.wait_ge(lora_ready, L + 1)
                wide(lambda n: mw[0:64, 2, n * P:(n + 1) * P], lambda n: zs[0:64, 12, :]).then_inc(dec_done, 1)
                pe.wait_ge(dec_out, L + 1)
                wide(lambda n: mw[64:128, 2, n * P:(n + 1) * P], lambda n: zs[64:128, 12, :]).then_inc(icl_done, 1)
                pe.wait_ge(icl_out, L + 1)
                wide(lambda n: mw[:, 3, n * P:(n + 1) * P], lambda n: zs[:, 13, :]).then_inc(g_done, 1)
                pe.wait_ge(g_out, L + 1)
                pe.wait_ge(kk_sq, L + 1)
                wide(lambda n: hones, lambda n: TB[3][:, n, :]).then_inc(kk_sum, 1)
                pe.wait_ge(kk_rt, L + 1)
                pe.wait_ge(bonus_in, L + 1)
                wide(lambda n: hones, lambda n: TB[6][:, n, :]).then_inc(bonus_done, 1)
                pe.wait_ge(cum_ready, L + 1)

                def chunk(c):
                    n = L * NCHUNK + c
                    pe.wait_ge(tilde_ready, n + 1)
                    for hd in range(HEADS):
                        m, q = hd // 2, hd % 2 * HD
                        last = mm(ps[:, hd % 2, m * P:(m + 1) * P], bk[q:q + HD, m, :], ar[q:q + HD, m, :],
                                  start=True, stop=True)
                    last.then_inc(pair_done, 1)
                    pe.wait_ge(v_ready, n + 1)
                    for m in range(NT):
                        nc.tensor.transpose(ps[:, 2, m * P:(m + 1) * P], bk[:, m, :], ident)
                    for m in range(NT):
                        last = nc.tensor.transpose(ps[:, 3, m * P:(m + 1) * P], vc[:, m, :], ident)
                    last.then_inc(turn_done, 1)
                    pe.wait_ge(turn_out, n + 1)
                    pe.wait_ge(gm_ready, n + 1)
                    for m in range(NT):
                        mm(ps[0:C, 7, m * P:(m + 1) * P], ar[:, m, 0:C], st[:, m, :], start=True, stop=False)
                        for hd in (2 * m, 2 * m + 1):
                            last = mm(ps[0:C, 7, hd * HD:(hd + 1) * HD], gm[:, hd, 0:C], vz[:, hd * HD:(hd + 1) * HD],
                                      start=False, stop=(hd % 2 == 1))
                    last.then_inc(f_done, 1)
                    for lv in range(LEVELS):
                        pe.wait_ge(m_ready, n * (LEVELS + 1) + lv + 1)
                        passed(pe)
                        for hd in range(HEADS):
                            last = mm(ps[0:C, 4, hd * C:(hd + 1) * C], ml[lv % 2][0:C, hd, :],
                                      eye if lv == 0 else xi[0:C, hd, :], start=True, stop=True)
                        last.then_inc(y_done, 1)
                        if lv == 0:
                            continue
                        pe.wait_ge(y_out, n * (LEVELS - 1) + lv)
                        passed(pe)
                        for hd in range(HEADS):
                            last = mm(ps[0:C, 6, hd * C:(hd + 1) * C], ys[0:C, hd, :], xt[0:C, hd, :],
                                      start=True, stop=True)
                        if lv < LEVELS - 1:
                            for hd in range(HEADS):
                                last = mm(ps[0:C, 5, hd * C:(hd + 1) * C], xt[0:C, hd, :], ys[0:C, hd, :],
                                          start=True, stop=True)
                        last.then_inc(x_done, 1)
                    pe.wait_ge(m_ready, (n + 1) * (LEVELS + 1))
                    pe.wait_ge(f_out, n + 1)
                    passed(pe)
                    for hd in range(HEADS):
                        last = mm(ps[0:C, 4, hd * HD:(hd + 1) * HD], xt[0:C, hd, :], fs[0:C, hd * HD:(hd + 1) * HD],
                                  start=True, stop=True)
                    last.then_inc(sa_done, 1)
                    pe.wait_ge(sa_out, n + 1)
                    for hd in range(HEADS):
                        m, q = hd // 2, hd % 2 * HD
                        mm(ps[q:q + HD, 5, m * HD:(m + 1) * HD], bkT[:, hd * HD:(hd + 1) * HD],
                           sav[:, hd * HD:(hd + 1) * HD], start=True, stop=True)
                    for m in range(NT):
                        mm(ps[:, 6, m * C:(m + 1) * C], st[:, m, :], ar[:, m, C:P], start=True, stop=False)
                        for hd in (2 * m, 2 * m + 1):
                            q = hd % 2 * HD
                            last = mm(ps[q:q + HD, 6, m * C:(m + 1) * C], sav[:, hd * HD:(hd + 1) * HD], gm[:, hd, C:P],
                                      start=False, stop=True)
                    last.then_inc(step_done, 1)

                passed(pe)
                with pe.Fori(0, NCH) as c:
                    chunk(c)
                chunk(NCH)
                pe.wait_ge(o_out, (L + 1) * NCHUNK)
                pe.wait_ge(outs_ready, L + 1)
                wide(lambda n: hones, lambda n: o[:, n, :]).then_inc(mean_done, 1)
                pe.wait_ge(oc_ready, L + 1)
                wide(lambda n: hones, lambda n: TB[6][:, n, :]).then_inc(var_done, 1)
                pe.wait_ge(y_ready, L + 1)
                linear(L, OUT_0, OUT_T, ymix, out_free)
                norm(L, 1)
                pe.wait_ge(xn_ready, L * 3 + 2)
                linear(L, Q_0, Q_T, xn, q_free)
                if do_peer:
                    pe.wait_ge(q_free, L * (Q_T + 2) + Q_T + 2)
                    pe.wait_ge(keys_in, L * 16 + 16)

                    def route(b, nt):
                        n = L * NBLK + b
                        pe.wait_ge(qb_ready, n + 1)
                        for q in range(QH):
                            last = mm(ps[0:nt, q // 4, q % 4 * P:(q % 4 + 1) * P], qb[:, q, 0:nt], kT[:, q, :],
                                      start=True, stop=True)
                        last.then_inc(sc_done, 1)
                        pe.wait_ge(sel_ready, n + 1)
                        passed(pe)
                        for w in range(3):
                            last = nc.tensor.transpose(ps[:, 4, w * nt:(w + 1) * nt], sel_t[0:nt, w, :], ident[0:nt, 0:nt])
                        last.then_inc(selT_done, 1)
                        with pe.Fori(0, nt // (2 * GT)) as g:
                            for s in range(2):
                                i = L * GROUPS + b * (BLK // GT) + g * 2 + s
                                pe.wait_ge(ab_ready, i + 1)
                                pe.wait_ge(gmat_out, i + 1)
                                for j in range(GT):
                                    last = mm(ps[:, 5 + s, j * P:(j + 1) * P], oneA[:, s, j, :], oneB[:, s, j, :],
                                              start=True, stop=True)
                                last.then_inc(gmat_done, 1)

                    passed(pe)
                    with pe.Fori(0, NB) as b:
                        route(b, BLK)
                    route(NB, DEC)
                    pe.wait_ge(gmat_out, (L + 1) * GROUPS + 2)
                    pe.wait_ge(xl_ready, L + 1)
                    passed(pe)
                    with pe.Fori(0, ESTEPS) as e:
                        for j in range(EC):
                            i = L * NK + e * EC + j
                            pe.wait_ge(ul_ready, i + 1 + 2)
                            pe.wait_ge(ge_out, i + 1)
                            for a in range(2):
                                for k in range(KD):
                                    for w, (lhs, rhs) in enumerate([(uh, xh), (uh, xl), (ul, xh)]):
                                        last = mm(ps[:, j % 2 * 2 + a, 0:HALF], lhs[j % 2][:, k, :], rhs[:, k, a * HALF:(a + 1) * HALF],
                                                  start=(k + w == 0), stop=(k == KD - 1 and w == 2))
                            last.then_inc(hid_done, 1)
                        for m in range(KD):
                            pe.wait_ge(eo_out, (L * ESTEPS + e) * KD + m + 1)
                            for j in range(EC):
                                if m == 0:
                                    pe.wait_ge(vl_ready, L * NK + e * EC + j + 1 + 2)
                                    pe.wait_ge(wl_ready, L * NK + e * EC + j + 1)
                                for a in range(2):
                                    for w, (lhs, rhs) in enumerate([(vh, wth), (vh, wtl), (vl, wth)]):
                                        last = mm(ps[:, 4 + m % 2 * 2 + a, 0:HALF], lhs[j][:, m * P:(m + 1) * P],
                                                  rhs[j][:, a * HALF:(a + 1) * HALF], start=(j + w == 0), stop=(j == EC - 1 and w == 2))
                            last.then_inc(eo_done, 1)
                norm(L, 2)
                pe.wait_ge(xn_ready, L * 3 + 3)
                pe.wait_ge(p_in, L * 16 + 16)
                passed(pe)
                with pe.Fori(0, PLE_T // 2) as g:
                    for j in range(2):
                        pe.wait_ge(w_in_s[j], L * (16 * TILES // 2) + g * 16 + 16 * (PLE_0 // 2) + 16)
                        pe.wait_ge(ple_free, L * (PLE_T + 2) + g * 2 + j + 1)
                        tile(j, j, xn, range(KD), 2 * j, False)
                        tile(j, j, pT, [KD, KD + 1], 4 + 2 * j, True)
            pe.wait_ge(sq_ready, 3 * DEPTH + 1)
            for a in range(2):
                for k in range(KD):
                    last = mm(ps[:, a, 0:HALF], ones, SQ[2][:, k, a * HALF:(a + 1) * HALF],
                              start=(k == 0), stop=(k == KD - 1))
            last.then_inc(sumsq, 1)

        @block.scalar
        def _(act):
            av = nc.scalar.activation
            act.sem_inc(gmat_out, 2)
            act.sem_inc(ge_out, 2)
            act.sem_inc(stage_free, 1)
            act.wait_ge(const_in, 16)
            act.wait_ge(x_in, 16)

            def norm(n, i):
                act.wait_ge(h_ready, n)
                for k in range(KD):
                    last = av(SQ[i][:, k, :], h[:, k, :], ACT.Square)
                last.then_inc(sq_ready, 1)
                act.wait_ge(sumsq, n)
                av(cut(rms, HALF), halves(0, HALF), ACT.Sqrt, bias=epst[:, 0:1], scale=1.0 / D).then_inc(rms_ready, 1)

            def wide(dst, func, bias=None, part=slice(0, P)):
                for n in range(NT):
                    last = av(cut(dst[:, n, :], MH), halves(2 * n, MH), func,
                              **({"bias": bias(n)} if bias else {}))
                return last

            def done(L, base, n):
                act.wait_ge(tile_done, L * TILES + base + n + 3)

            with act.Fori(0, DEPTH) as L:
                norm(L * 3 + 1, 0)
                act.drain()
                act.sem_inc(in_free, 2)
                with act.Fori(0, IN_T // 2) as g:
                    for j in range(2):
                        done(L, 0, g * 2 + j)
                        at = zin[:, bass.ds(g * 2 + j, 1), :].rearrange("p a t -> p (a t)")
                        av(at[:, LEAD:LEAD + HALF], ps[:, 2 * j, 0:HALF], ACT.Copy)
                        av(at[:, LEAD + HALF:LEAD + SEQ], ps[:, 2 * j + 1, 0:SEQ - HALF], ACT.Copy)
                        av(at[:, ZW - DEC:ZW], ps[:, 2 * j + 1, SEQ - HALF:HALF], ACT.Copy).then_inc(in_free, 1)
                act.wait_ge(lam_abs, L + 1)
                av(sp[:, 4:8], sp[:, 0:4], ACT.Exp, scale=-1.0).then_inc(lam_exp, 1)
                act.wait_ge(lam_u, L + 1)
                av(sp[:, 16:20], sp[:, 8:12], ACT.Ln).then_inc(lam_ln, 1)
                act.wait_ge(r_done, L + 1)
                wide(TB[1], ACT.Sigmoid, lambda n: small_of("ba", n)).then_inc(r_out, 1)
                act.wait_ge(i_done, L + 1)
                wide(TB[2], ACT.Sigmoid, lambda n: small_of("bx", n)).then_inc(i_out, 1)
                act.wait_ge(nsp_ready, L + 1)
                passed(act)
                act.drain()
                for n in range(NT):
                    av(TB[3][:, n, :], TB[1][:, n, :], ACT.Tanh, scale=sp[:, 32 + n:33 + n])
                for n in range(NT):
                    last = av(TB[4][:, n, :], TB[1][:, n, :], ACT.Exp, scale=sp[:, 32 + n:33 + n])
                last.then_inc(a_ready, 1)
                for n in range(NT):
                    last = av(zin[:, NT + n, LEAD:ZW], zin[:, NT + n, LEAD:ZW], ACT.Gelu_apprx_tanh)
                last.then_inc(gg_ready, 1)
                act.wait_ge(m2_ready, L + 1)
                av(TB[5][:, :, :], TB[5][:, :, :], ACT.Sqrt, scale=-1.0).then_inc(mult_ready, 1)
                act.wait_ge(zs_ready, L + 1)
                av(zs[0:64, 12, :], zs[0:64, 12, :], ACT.Tanh)
                av(zs[:, 13, :], zs[:, 13, :], ACT.Sigmoid).then_inc(lora_ready, 1)
                act.wait_ge(lru_done, L + 1)
                act.wait_ge(dec_done, L + 1)
                wide(TB[0], ACT.Sigmoid, lambda n: small_of("w0", n)).then_inc(dec_out, 1)
                act.wait_ge(icl_done, L + 1)
                wide(TB[4], ACT.Sigmoid, lambda n: small_of("a0", n)).then_inc(icl_out, 1)
                act.wait_ge(g_done, L + 1)
                wide(TB[5], ACT.Copy).then_inc(g_out, 1)
                act.wait_ge(kk_sum, L + 1)
                wide(TB[6], ACT.Sqrt).then_inc(kk_rt, 1)
                act.wait_ge(cum_ready, L + 1)
                av(TB[0][:, :, :], TB[0][:, :, :], ACT.Exp)
                av(TB[6][:, :, :], TB[1][:, :, :], ACT.Exp, scale=-1.0)
                act.drain()
                av(TB[1][:, :, :], TB[1][:, :, :], ACT.Exp).then_inc(exp_ready, 1)

                def chunk(c, col):
                    n = L * NCHUNK + c
                    av(vc[:, :, C:P], zs[:, 8:12, col], ACT.Copy).then_inc(v_ready, 1)
                    act.wait_ge(turn_done, n + 1)
                    av(bkT, ps[:, 2, :], ACT.Copy)
                    av(vz, ps[:, 3, :], ACT.Copy)
                    av(sav[64:128, :], ps[64:128, 3, :], ACT.Copy).then_inc(turn_out, 1)
                    act.wait_ge(f_done, n + 1)
                    av(fs[0:C, :], ps[0:C, 7, :], ACT.Copy).then_inc(f_out, 1)
                    for lv in range(1, LEVELS):
                        act.wait_ge(y_done, n * LEVELS + lv + 1)
                        av(ys[0:C], ps[0:C, 4, :].rearrange("p (h t) -> p h t", h=HEADS), ACT.Copy).then_inc(y_out, 1)
                    act.wait_ge(sa_done, n + 1)
                    av(sav[0:C, :], ps[0:C, 4, :], ACT.Copy).then_inc(sa_out, 1)
                    act.wait_ge(step_done, n + 1)
                    av(o[:, :, col], ps[:, 6, 0:NT * C].rearrange("p (m t) -> p m t", m=NT), ACT.Copy).then_inc(o_out, 1)

                with act.Fori(0, NCH) as c:
                    chunk(c, bass.ds(c * C, C))
                chunk(NCH, slice(DEC0, DEC0 + C))
                act.wait_ge(var_done, L + 1)
                wide(TB[6], ACT.Sqrt, lambda n: epst[:, 1:2]).then_inc(std_out, 1)
                norm(L * 3 + 2, 1)
                act.drain()
                act.sem_inc(q_free, 2)
                with act.Fori(0, Q_T // 2) as g:
                    for j in range(2):
                        done(L, Q_0, g * 2 + j)
                        at = qT[:, bass.ds(g * 2 + j, 1), :].rearrange("p a t -> p (a t)")
                        av(cut(at, HALF), halves(2 * j, HALF), ACT.Copy).then_inc(q_free, 1)
                if do_peer:
                    def route(b, nt, col):
                        n = L * NBLK + b
                        av(qb[:, :, 0:nt], qT[:, :, col], ACT.Copy).then_inc(qb_ready, 1)
                        if nt < BLK:
                            act.drain()
                            av(xh, xn, ACT.Copy).then_inc(xh_ready, 1)
                        act.wait_ge(best_ready, n + 1)
                        av(bv[0:nt], bv[0:nt], ACT.Exp).then_inc(gexp, 1)
                        act.wait_ge(selT_done, n + 1)
                        av(sel[:, :, 0:nt], ps[:, 4, 0:3 * nt].rearrange("p (w t) -> p w t", w=3), ACT.Copy).then_inc(selT_out, 1)
                        act.wait_ge(stage_free, n + 1)
                        with act.Fori(0, nt // (2 * GT)) as g:
                            for s in range(2):
                                i = L * GROUPS + b * (BLK // GT) + g * 2 + s
                                act.wait_ge(gmat_done, i + 3)
                                av(stage[:, :, bass.ds(g * 2 * GT + s * GT, GT)],
                                   ps[:, 5 + s, :].rearrange("p (j n) -> p n j", j=GT), ACT.Copy).then_inc(gmat_out, 1)
                        act.wait_ge(gmat_out, L * GROUPS + b * (BLK // GT) + nt // GT + 2)
                        act.dma_start(gate_d[:, :, col], stage[:, :, 0:nt]).then_inc(gate_saved, 16)

                    act.drain()
                    with act.Fori(0, NB) as b:
                        route(b, BLK, bass.ds(b * BLK, BLK))
                    route(NB, DEC, slice(SEQ, T))
                    with act.Fori(0, ESTEPS) as e:
                        def high_u(j):
                            i = L * NK + e * EC + j
                            act.wait_ge(u_in[j % 2], L * (8 * NK) + e * (8 * EC) + 16 * (j // 2) + 16)
                            act.wait_ge(hid_done, i + 1)
                            av(uh[j % 2], uraw[j % 2], ACT.Copy).then_inc(uh_ready, 1)

                        def gelu(j):
                            i = L * NK + e * EC + j
                            act.wait_ge(hid_done, i + 1 + 2)
                            act.wait_ge(w_ready, i + 1 + EC - 2)
                            av(cut(ge[j % 2], HALF), halves(j % 2 * 2, HALF), ACT.Gelu_apprx_tanh).then_inc(ge_out, 1)

                        def high_w(j):
                            i = L * NK + e * EC + j
                            act.wait_ge(eo_done, (L * ESTEPS + e + 1) * KD)
                            act.wait_ge(w_ready, i + 1 + EC)
                            av(wth[j], wf[j % 2], ACT.Copy).then_inc(wh_ready, 1)

                        high_u(0)
                        high_u(1)
                        gelu(0)
                        high_u(2)
                        gelu(1)
                        high_w(0)
                        high_u(3)
                        gelu(2)
                        high_w(1)
                        gelu(3)
                        high_w(2)
                        high_w(3)
                norm(L * 3 + 3, 2)
                with act.Fori(0, PLE_T // 2) as g:
                    for j in range(2):
                        done(L, PLE_0, g * 2 + j)
                        act.wait_ge(ple_free, L * (PLE_T + 2) + g * 2 + j + 1)
                        av(cut(sg[j], HALF), halves(2 * j, HALF), ACT.Sigmoid).then_inc(ple_sig, 1)
            norm(3 * DEPTH + 1, 2)

        @block.vector
        def _(dve):
            ts, tt, stt = nc.vector.tensor_scalar, nc.vector.tensor_tensor, nc.vector.scalar_tensor_tensor
            copy = nc.vector.tensor_copy
            dve.memset(epst[:, 0:1], EPS)
            dve.memset(epst[:, 1:2], GN_EPS)
            dve.drain()
            dve.sem_inc(layer_free, 1)
            dve.sem_inc(w_ready, EC)
            dve.sem_inc(eo_out, 2)
            dve.wait_ge(const_in, 16)
            dve.wait_ge(x_in, 16)

            def norm(n, gain, last_sem):
                dve.wait_ge(rms_ready, n)
                dve.reciprocal(rms, rms)
                dve.drain()
                for k in range(KD):
                    last = stt(xn[:, k, :], h[:, k, :], small_of(gain, k), rms, ALU.mult, ALU.mult)
                last.then_inc(last_sem, 1)

            def add_tile(k, bank):
                at = h[:, k, :].rearrange("p a t -> p (a t)") if not isinstance(k, int) else h[:, k, :]
                return tt(cut(at, HALF), halves(bank, HALF), cut(at, HALF), ALU.add)

            with dve.Fori(0, DEPTH) as L:
                dve.drain()
                dve.sem_inc(h_ready, 1)
                dve.wait_ge(small_in, L * 16 + 16)
                dve.memset(zin[:, :, 0:LEAD], 0.0)
                dve.memset(zin[:, :, SEQ + LEAD:SEQ + 2 * LEAD], 0.0)
                stt(sp[:, 0:4], small_of("lam", 0, 4), -1.0, small_of("lam", 0, 4), ALU.mult, ALU.max).then_inc(lam_abs, 1)
                ts(sp[:, 36:40], small_of("lam", 0, 4), -1.0, 0.0, ALU.mult, ALU.max)
                dve.drain()
                copy(zin[:, 0:NT, SEQ + LEAD:SEQ + 2 * LEAD], small_of("cst", 0, 12).rearrange("p (n t) -> p n t", n=NT))
                copy(zin[:, 2 * NT:ZT, DEC0 + 2:DEC0 + 3], small_of("sst", 0, 14).rearrange("p (n t) -> p n t", n=ZR))
                norm(L * 3 + 1, "n1", xn_ready)
                dve.wait_ge(lam_exp, L + 1)
                ts(sp[:, 8:12], sp[:, 4:8], 1.0, None, ALU.add)
                dve.drain()
                ts(sp[:, 12:16], sp[:, 8:12], -1.0, None, ALU.add).then_inc(lam_u, 1)
                dve.wait_ge(lam_ln, L + 1)
                passed(dve)
                dve.drain()
                ts(sp[:, 20:24], sp[:, 12:16], 0.0, None, ALU.is_equal)
                dve.drain()
                tt(sp[:, 24:28], sp[:, 16:20], sp[:, 20:24], ALU.add)
                tt(sp[:, 28:32], sp[:, 12:16], sp[:, 20:24], ALU.add)
                dve.drain()
                dve.reciprocal(sp[:, 28:32], sp[:, 28:32])
                tt(sp[:, 24:28], sp[:, 24:28], sp[:, 4:8], ALU.mult)
                dve.drain()
                tt(sp[:, 24:28], sp[:, 24:28], sp[:, 28:32], ALU.mult)
                dve.drain()
                tt(sp[:, 24:28], sp[:, 24:28], sp[:, 36:40], ALU.add)
                dve.drain()
                ts(sp[:, 32:36], sp[:, 24:28], -8.0, None, ALU.mult).then_inc(nsp_ready, 1)
                xc = TB[0]
                dve.wait_ge(in_free, L * (IN_T + 2) + 2 + NT)
                dve.memset(xc[:, :, EW:MW], 0.0)
                for tap in range(4):
                    for n in range(NT):
                        src = zin[:, n, tap:tap + EW]
                        w = small_of("cw", tap * NT + n)
                        if tap == 0:
                            last = ts(xc[:, n, 0:EW], src, w, small_of("cb", n), ALU.mult, ALU.add)
                        else:
                            last = stt(xc[:, n, 0:EW], src, w, xc[:, n, 0:EW], ALU.mult, ALU.add)
                    if tap < 3:
                        dve.drain()
                last.then_inc(xc_ready, 1)
                dve.wait_ge(in_free, L * (IN_T + 2) + 2 + IN_T)
                zt = zin[:, 2 * NT:ZT, :]
                dve.memset(zs[:, :, EW:MW], 0.0)
                tt(zs[:, :, 0:EW], zt[:, :, LEAD - 1:LEAD - 1 + EW], zt[:, :, LEAD:LEAD + EW], ALU.subtract)
                dve.drain()
                for m in range(ZR):
                    stt(zs[:, m, 0:EW], zs[:, m, 0:EW], small_of("mu", m), zt[:, m, LEAD:LEAD + EW], ALU.mult, ALU.add)
                for w, (c0, c1) in enumerate([(SEQ, SEQ + LEAD), (ZW - LEAD, ZW)]):
                    copy(sout[:, SO["conv"][0] + 12 * w:SO["conv"][0] + 12 * w + 12].rearrange("p (n t) -> p n t", n=NT),
                         zin[:, 0:NT, c0:c1])
                    last = copy(sout[:, SO["shift"][0] + 14 * w:SO["shift"][0] + 14 * w + 14].rearrange("p (n t) -> p n t", n=ZR),
                                zt[:, :, c1 - 1:c1])
                last.then_inc(zs_ready, 1)
                dve.wait_ge(i_out, L + 1)
                tt(TB[2][:, :, :], TB[2][:, :, :], xc[:, :, :], ALU.mult)
                dve.wait_ge(a_ready, L + 1)
                tt(TB[5][:, :, :], TB[4][:, :, :], TB[4][:, :, :], ALU.mult)
                dve.drain()
                stt(TB[5][:, :, :], TB[5][:, :, :], 1.0, TB[3][:, :, :], ALU.add, ALU.mult).then_inc(m2_ready, 1)
                dve.wait_ge(mult_ready, L + 1)
                dve.memset(TB[5][:, :, 0:1], 1.0)
                dve.drain()
                tt(TB[2][:, :, :], TB[2][:, :, :], TB[5][:, :, :], ALU.mult)
                dve.drain()
                for n in range(NT):
                    nc.vector.tensor_tensor_scan(TB[6][:, n, 0:SEQ], TB[4][:, n, 0:SEQ], TB[2][:, n, 0:SEQ], 0.0, ALU.mult, ALU.add)
                    nc.vector.tensor_tensor_scan(TB[6][:, n, DEC0:EW], TB[4][:, n, DEC0:EW], TB[2][:, n, DEC0:EW],
                                                 small_of("lst", n), ALU.mult, ALU.add)
                dve.drain()
                for w, c in enumerate([SEQ - 1, EW - 1]):
                    copy(sout[:, SO["lru"][0] + 4 * w:SO["lru"][0] + 4 * w + 4].rearrange("p (n t) -> p n t", n=NT), TB[6][:, :, c:c + 1])
                dve.wait_ge(gg_ready, L + 1)
                tt(ymix[:, 0:NT, 0:SEQ], TB[6][:, :, 0:SEQ], zin[:, NT:2 * NT, LEAD:LEAD + SEQ], ALU.mult)
                tt(ymix[:, 0:NT, SEQ:T], TB[6][:, :, DEC0:EW], zin[:, NT:2 * NT, ZW - DEC:ZW], ALU.mult).then_inc(lru_done, 1)
                dve.drain()
                r_, k_, v_ = zs[:, 0:4, :], zs[:, 4:8, :], zs[:, 8:12, :]
                for n in range(NT):
                    ts(TB[2][:, n, :], k_[:, n, :], small_of("kk", n), None, ALU.mult)
                dve.drain()
                tt(TB[3][:, :, :], TB[2][:, :, :], TB[2][:, :, :], ALU.mult).then_inc(kk_sq, 1)
                ts(sp[:, 0:4], small_of("ka", 0, 4), -1.0, 1.0, ALU.mult, ALU.add)
                dve.wait_ge(dec_out, L + 1)
                ts(TB[0][:, :, :], TB[0][:, :, :], -float(np.exp(-0.5)), None, ALU.mult)
                dve.drain()
                dve.memset(TB[0][:, :, EW:MW], 0.0)
                dve.drain()
                for n in range(NT):
                    nc.vector.tensor_tensor_scan(TB[1][:, n, :], reset, TB[0][:, n, :], 0.0, ALU.mult, ALU.add)
                dve.drain()
                tt(TB[0][:, :, :], TB[1][:, :, :], TB[0][:, :, :], ALU.subtract)
                dve.wait_ge(kk_rt, L + 1)
                dve.wait_ge(icl_out, L + 1)
                ts(TB[6][:, :, :], TB[6][:, :, :], 1e-12, None, ALU.max)
                dve.drain()
                dve.reciprocal(TB[6][:, :, :], TB[6][:, :, :])
                dve.drain()
                tt(TB[2][:, :, :], TB[2][:, :, :], TB[6][:, :, :], ALU.mult)
                dve.drain()
                for n in range(NT):
                    ts(TB[6][:, n, :], TB[4][:, n, :], small_of("ka", n), sp[:, n:n + 1], ALU.mult, ALU.add)
                tt(TB[3][:, :, :], TB[2][:, :, :], TB[4][:, :, :], ALU.mult)
                dve.drain()
                tt(k_, k_, TB[6][:, :, :], ALU.mult)
                dve.drain()
                for n in range(NT):
                    last = stt(TB[6][:, n, :], r_[:, n, :], small_of("rk", n), k_[:, n, :], ALU.mult, ALU.mult)
                last.then_inc(bonus_in, 1)
                dve.memset(vc[:, :, 0:C], 0.0)
                dve.memset(st[:, :, :], 0.0)
                dve.memset(o[:, :, SEQ:DEC0], 0.0)
                dve.memset(o[:, :, MW - 1:MW], 0.0)
                dve.wait_ge(bonus_done, L + 1)
                for n in range(NT):
                    last = tt(cut(TB[4][:, n, :], MH), halves(2 * n, MH), cut(v_[:, n, :], MH), ALU.mult)
                last.then_inc(cum_ready, 1)
                dve.wait_ge(exp_ready, L + 1)
                passed(dve)

                def chunk(c, col, end):
                    n = L * NCHUNK + c
                    tt(bk[:, :, 0:C], TB[3][:, :, col], TB[6][:, :, col], ALU.mult)
                    tt(bk[:, :, C:P], k_[:, :, col], TB[6][:, :, col], ALU.mult)
                    tt(ar[:, :, C:P], r_[:, :, col], TB[1][:, :, col], ALU.mult)
                    tt(ar[:, :, 0:C], TB[2][:, :, col], TB[0][:, :, col], ALU.mult)
                    dve.drain()
                    ts(ar[:, :, 0:C], ar[:, :, 0:C], -1.0, None, ALU.mult).then_inc(tilde_ready, 1)
                    dve.wait_ge(pair_done, n + 1)
                    for b in range(2):
                        last = tt(gm[:, b:HEADS:2, :], ps[:, b, :].rearrange("p (h t) -> p h t", h=4),
                                  causal.unsqueeze(1).to_broadcast([P, 4, P]), ALU.mult)
                    last.then_inc(gm_ready, 1)
                    dve.drain()
                    amT = gm[0:C, :, 0:C]

                    def level(lv):
                        mask = cn[0:C, CN["level"] + lv * C:CN["level"] + (lv + 1) * C]
                        return tt(ml[lv % 2][0:C], amT, mask.unsqueeze(1).to_broadcast([C, HEADS, C]), ALU.mult)

                    eyes = eye.unsqueeze(1).to_broadcast([C, HEADS, C])
                    level(0).then_inc(m_ready, 1)
                    dve.drain()
                    tt(xt[0:C], ml[0][0:C], eyes, ALU.add)
                    level(1)
                    dve.wait_ge(y_done, n * LEVELS + 1)
                    tt(xi[0:C], ps[0:C, 4, :].rearrange("p (h t) -> p h t", h=HEADS), eyes, ALU.add).then_inc(m_ready, 1)
                    dve.drain()
                    for lv in range(1, LEVELS):
                        if lv + 1 < LEVELS:
                            level(lv + 1)
                        dve.wait_ge(x_done, n * (LEVELS - 1) + lv)
                        if lv + 1 < LEVELS:
                            tt(xi[0:C], ps[0:C, 5, :].rearrange("p (h t) -> p h t", h=HEADS), xi[0:C], ALU.add)
                        last = tt(xt[0:C], ps[0:C, 6, :].rearrange("p (h t) -> p h t", h=HEADS), xt[0:C], ALU.add)
                        last.then_inc(m_ready, 1)
                    dve.wait_ge(step_done, n + 1)
                    for q in (0, HD):
                        at = st[q:q + HD, :, q:q + HD]
                        tt(at, ps[q:q + HD, 5, 0:NT * HD].rearrange("p (m v) -> p m v", m=NT), at, ALU.add)
                    dve.drain()
                    for q in (0, HD):
                        at = st[q:q + HD, :, q:q + HD]
                        tt(at, at, TB[1][q:q + HD, :, end].to_broadcast([HD, NT, HD]), ALU.mult)
                    dve.drain()

                with dve.Fori(0, NCH) as c:
                    chunk(c, bass.ds(c * C, C), bass.ds(c * C + C - 1, 1))
                dve.wait_ge(wkv_in, L * 16 + 16)
                for q in (0, HD):
                    copy(stp[q:q + HD, :, :], st[q:q + HD, :, q:q + HD])
                dve.drain()
                for q in (0, HD):
                    copy(st[q:q + HD, :, q:q + HD], sts[q:q + HD, :, :])
                chunk(NCH, slice(DEC0, DEC0 + C), slice(DEC0 + C - 1, DEC0 + C))
                for q in (0, HD):
                    copy(sts[q:q + HD, :, :], st[q:q + HD, :, q:q + HD])
                dve.drain()
                dve.sem_inc(outs_ready, 1)
                dve.wait_ge(mean_done, L + 1)
                for n in range(NT):
                    stt(cut(TB[0][:, n, :], MH), halves(2 * n, MH), -1.0 / HD, cut(o[:, n, :], MH), ALU.mult, ALU.add)
                dve.drain()
                tt(TB[6][:, :, :], TB[0][:, :, :], TB[0][:, :, :], ALU.mult)
                dve.drain()
                ts(TB[6][:, :, :], TB[6][:, :, :], 1.0 / HD, None, ALU.mult).then_inc(oc_ready, 1)
                dve.wait_ge(std_out, L + 1)
                dve.reciprocal(TB[6][:, :, :], TB[6][:, :, :])
                dve.drain()
                tt(TB[0][:, :, :], TB[0][:, :, :], TB[6][:, :, :], ALU.mult)
                dve.drain()
                for n in range(NT):
                    ts(TB[0][:, n, :], TB[0][:, n, :], small_of("lnw", n), small_of("lnb", n), ALU.mult, ALU.add)
                dve.drain()
                tt(TB[0][:, :, :], TB[0][:, :, :], TB[4][:, :, :], ALU.add)
                dve.drain()
                tt(ymix[:, NT:KD, 0:SEQ], TB[0][:, :, 0:SEQ], TB[5][:, :, 0:SEQ], ALU.mult)
                tt(ymix[:, NT:KD, SEQ:T], TB[0][:, :, DEC0:EW], TB[5][:, :, DEC0:EW], ALU.mult).then_inc(y_ready, 1)
                dve.drain()
                dve.sem_inc(out_free, 2)
                with dve.Fori(0, OUT_T // 2) as g:
                    for j in range(2):
                        dve.wait_ge(tile_done, L * TILES + OUT_0 + g * 2 + j + 3)
                        add_tile(bass.ds(g * 2 + j, 1), 2 * j).then_inc(out_free, 1)
                dve.wait_ge(stored, (L + 1) * 48)
                passed(dve)
                dve.drain()
                dve.sem_inc(h_ready, 1)
                norm(L * 3 + 2, "n2", xn_ready)

                if do_peer:
                    def top16(nt, src, spare, n, width, vals, idx):
                        mx, mi, mr = nc.vector.max, nc.vector.max_index, nc.vector.match_replace
                        for q in range(n):
                            mx(vals[0:nt, q, 0:8], src(q))
                        dve.drain()
                        for q in range(n):
                            mi(idx[0:nt, q, 0:8], vals[0:nt, q, 0:8], src(q))
                            last = mr(spare[0:nt, q * width:(q + 1) * width], vals[0:nt, q, 0:8], src(q), NEG)
                        dve.drain()
                        for q in range(n):
                            mx(vals[0:nt, q, 8:16], spare[0:nt, q * width:(q + 1) * width])
                        dve.drain()
                        for q in range(n):
                            mi(idx[0:nt, q, 8:16], vals[0:nt, q, 8:16], spare[0:nt, q * width:(q + 1) * width])
                        dve.drain()

                    def route(b, nt):
                        n = L * NBLK + b
                        dve.wait_ge(sc_done, n + 1)
                        passed(dve)
                        top16(nt, lambda q: ps[0:nt, q // 4, q % 4 * NK:(q % 4 + 1) * NK], s1, QH, NK, tv, ti.bitcast(U32))
                        copy(tf[0:nt], ti[0:nt].bitcast(U32))
                        tvs = tv[0:nt].rearrange("p (q w) k -> p q w k", w=2)
                        cand = s2[0:nt].rearrange("p (q a b) -> p q a b", q=PH, a=TOPK)
                        shape = [nt, PH, TOPK, TOPK]
                        tt(cand, tvs[:, :, 0, :].unsqueeze(3).to_broadcast(shape),
                           tvs[:, :, 1, :].unsqueeze(2).to_broadcast(shape), ALU.add)
                        dve.drain()
                        top16(nt, lambda q: s2[0:nt, q * 256:(q + 1) * 256], s1, PH, 256, bv, bi.bitcast(U32))
                        mxs = bv[0:nt, :, 0:1]
                        copy(gsum[0:nt], mxs)
                        dve.drain()
                        tt(bv[0:nt], bv[0:nt], gsum[0:nt].unsqueeze(2).to_broadcast([nt, PH, TOPK]), ALU.subtract).then_inc(best_ready, 1)
                        ts(ba[0:nt, 0].bitcast(U32), bi[0:nt].bitcast(U32), 4, None, ALU.logical_shift_right)
                        ts(ba[0:nt, 1].bitcast(U32), bi[0:nt].bitcast(U32), 15, None, ALU.bitwise_and)
                        dve.drain()
                        copy(bf[0:nt], ba[0:nt].bitcast(U32))
                        dve.drain()
                        eq = s2[0:nt].rearrange("p (q k j) -> p q k j", q=PH, k=TOPK)
                        eq3 = s2[0:nt].rearrange("p (q j) -> p q j", q=PH * TOPK)
                        tfs = tf[0:nt].rearrange("p (q w) k -> p q w k", w=2)
                        for w in range(2):
                            b3 = bf[0:nt, w].rearrange("p q k -> p (q k)").unsqueeze(2).to_broadcast([nt, PH * TOPK, TOPK])
                            i3 = iota[0:nt, 0:TOPK].unsqueeze(1).to_broadcast([nt, PH * TOPK, TOPK])
                            tt(eq3, b3, i3, ALU.is_equal)
                            dve.drain()
                            tt(eq, eq, tfs[:, :, w, :].unsqueeze(2).to_broadcast(shape), ALU.mult)
                            dve.drain()
                            nc.vector.tensor_reduce(sel_t[0:nt, 1 + w, :], eq3, AX.X, ALU.add)
                            dve.drain()
                        dve.wait_ge(gexp, n + 1)
                        nc.vector.tensor_reduce(gsum[0:nt], bv[0:nt], AX.X, ALU.add)
                        dve.drain()
                        dve.reciprocal(gsum[0:nt], gsum[0:nt])
                        dve.drain()
                        tt(sel_t[0:nt, 0, :].rearrange("p (q k) -> p q k", q=PH), bv[0:nt],
                           gsum[0:nt].unsqueeze(2).to_broadcast([nt, PH, TOPK]), ALU.mult).then_inc(sel_ready, 1)
                        dve.wait_ge(selT_out, n + 1)
                        passed(dve)
                        with dve.Fori(0, nt // (2 * GT)) as g:
                            for s in range(2):
                                i = L * GROUPS + b * (BLK // GT) + g * 2 + s
                                dve.wait_ge(gmat_done, i - 1 + 1) if False else None
                                dve.wait_ge(gmat_done, i + 1)
                                for j in range(GT):
                                    t = bass.ds(g * (2 * GT) + s * GT + j, 1)
                                    ts(oneA[:, s, j, :], iota, sel[:, 1, t], None, ALU.is_equal)
                                    last = ts(oneB[:, s, j, :], iota, sel[:, 2, t], sel[:, 0, t], ALU.is_equal, ALU.mult)
                                last.then_inc(ab_ready, 1)

                    with dve.Fori(0, NB) as b:
                        route(b, BLK)
                    route(NB, DEC)
                    with dve.Fori(0, ESTEPS) as e:
                        def high_v(j):
                            dve.wait_ge(v_in[j % 2], L * (8 * NK) + e * (8 * EC) + 16 * (j // 2) + 16)
                            dve.wait_ge(eo_done, (L * ESTEPS + e + 1) * KD)
                            passed(dve)
                            copy(vh[j], vraw[j % 2]).then_inc(vh_ready, 1)

                        def weigh(j):
                            i = L * NK + e * EC + j
                            dve.drain()
                            dve.wait_ge(ge_out, i + 1 + 2)
                            dve.wait_ge(g_in[j], (L * ESTEPS + e + 1) * 16)
                            tt(wf[j % 2], ge[j % 2], gs[j], ALU.mult).then_inc(w_ready, 1)

                        def low_w(j):
                            dve.wait_ge(wh_ready, L * NK + e * EC + j + 1)
                            tt(wtl[j], wf[j % 2], wth[j].bitcast(F32), ALU.subtract).then_inc(wl_ready, 1)

                        high_v(0)
                        high_v(1)
                        weigh(0)
                        high_v(2)
                        weigh(1)
                        low_w(0)
                        high_v(3)
                        weigh(2)
                        low_w(1)
                        weigh(3)
                        low_w(2)
                        low_w(3)
                        for m in range(KD):
                            dve.wait_ge(eo_done, (L * ESTEPS + e + 1) * KD + m + 1)
                            add_tile(m, 4 + m % 2 * 2).then_inc(eo_out, 1)
                dve.drain()
                dve.sem_inc(h_ready, 1)
                norm(L * 3 + 3, "n3", xn_ready)
                dve.drain()
                dve.sem_inc(ple_free, 2)
                with dve.Fori(0, PLE_T // 2) as g:
                    for j in range(2):
                        dve.wait_ge(ple_sig, L * PLE_T + g * 2 + j + 1)
                        tt(cut(pg[j], HALF), halves(4 + 2 * j, HALF), cut(sg[j], HALF), ALU.mult)
                        dve.drain()
                        at = h[:, bass.ds(g * 2 + j, 1), :].rearrange("p a t -> p (a t)")
                        tt(at, at, pg[j], ALU.add).then_inc(ple_free, 1)
                if True:
                    dve.drain()
                    dve.sem_inc(layer_free, 1)
            dve.sem_inc(h_ready, 1)
            norm(3 * DEPTH + 1, "fin", y_out_ready)


def kernel(**inputs):
    import concourse.bacc as bacc
    from concourse.bass_utils import run_bass_kernel_spmd

    nc = bacc.Bacc("TRN2", target_bir_lowering=False, num_devices=1)
    arrays = lay_out(inputs)
    args = []
    for name, a in arrays.items():
        args.append(nc.dram_tensor(f"in_{name}", a.shape, mybir.dt.from_np(a.dtype), kind="ExternalInput").ap())
    for name, shape in OUTS.items():
        args.append(nc.dram_tensor(f"out_{name}", shape, F32, kind="ExternalOutput").ap())
    trunk(nc, *args)
    r = run_bass_kernel_spmd(nc, [{f"in_{n}": a for n, a in arrays.items()}], core_ids=[0]).results[0]
    return give_back({n: r[f"out_{n}"] for n in OUTS})


OUTS = {"y": (P, KD, T), "small": (DEPTH, P, NSO), "wkv": (DEPTH, 2, P, NT, HD)}


def lay_out(i):
    i = {k: np.asarray(a) for k, a in i.items()}

    def cols(a, axis=1):
        return np.swapaxes(a.reshape(DEPTH, -1, P), 1, 2)

    x = np.concatenate([i["x_prompt"][0], i["x_sample"][0]], 0).T.reshape(KD, P, T).transpose(1, 0, 2)
    p = np.concatenate([i["p_prompt"][:, 0], i["p_sample"][:, 0]], 1).transpose(0, 2, 1).reshape(DEPTH, 2, P, T).transpose(0, 2, 1, 3)
    small = np.zeros((DEPTH, P, NSM), np.float32)

    def put(name, a):
        small[:, :, SM[name]:SM[name] + a.shape[2]] = a

    put("n1", cols(i["norm1_g"]))
    put("n2", cols(i["norm2_g"]))
    put("n3", cols(i["norm3_g"]))
    put("fin", cols(np.stack([i["final_g"]] * DEPTH)))
    put("cw", cols(i["conv_w"].reshape(DEPTH, -1)))
    for name, key in [("cb", "conv_b"), ("ba", "lru_ba"), ("bx", "lru_bx"), ("lam", "lru_lambda"), ("mu", "rwkv_mu"),
                      ("w0", "rwkv_w0"), ("a0", "rwkv_a0"), ("kk", "rwkv_kk"), ("ka", "rwkv_ka"),
                      ("rk", "rwkv_rk"), ("lnw", "rwkv_ln_w"), ("lnb", "rwkv_ln_b")]:
        put(name, cols(i[key].reshape(DEPTH, -1)))
    put("cst", i["state_conv"][:, 0].reshape(DEPTH, 3, NT, P).transpose(0, 3, 2, 1).reshape(DEPTH, P, 12))
    put("lst", cols(i["state_lru"][:, 0]))
    put("sst", cols(i["state_shift"][:, 0]))
    mixw = np.stack([i["lru_wa"].transpose(0, 2, 1, 3).reshape(DEPTH, P, LW),
                     i["lru_wx"].transpose(0, 2, 1, 3).reshape(DEPTH, P, LW),
                     np.concatenate([i["rwkv_w2"], i["rwkv_a2"]], 1), i["rwkv_g2"]], 2)
    wkv0 = i["state_wkv"][:, 0].reshape(DEPTH, NT, 2, HD, HD).transpose(0, 2, 4, 1, 3).reshape(DEPTH, P, NT, HD)
    keys = i["peer_keys"].reshape(DEPTH, QH, NK, P).transpose(0, 3, 1, 2)
    ut = i["peer_u"].reshape(DEPTH, NK, NK, KD, P).transpose(0, 2, 4, 3, 1)
    wple = np.concatenate([i["ple_gate"], i["ple_w"]], 1)
    out = dict(x=x, p=p, small=small, const=constants(), mixw=mixw, wkv0=wkv0, w_in=i["w_in"], w_out=i["w_out"],
               wq=i["peer_wq"], keys=keys, ut=ut, v=i["peer_v"], wple=wple)
    return {k: np.ascontiguousarray(a) for k, a in out.items()}


def give_back(r):
    y = r["y"].transpose(2, 1, 0).reshape(T, D)
    so, wk = r["small"], r["wkv"]

    def cols(name, w):
        at, n = SO[name]
        return so[:, :, at + n * w:at + n * w + n]

    res = []
    for w in range(2):
        conv = cols("conv", w).reshape(DEPTH, P, NT, 3).transpose(0, 3, 2, 1).reshape(DEPTH, 1, 3, LW)
        lru = cols("lru", w).transpose(0, 2, 1).reshape(DEPTH, 1, LW)
        shift = cols("shift", w).transpose(0, 2, 1).reshape(DEPTH, 1, RCOLS)
        wkv = wk[:, w].reshape(DEPTH, 2, HD, NT, HD).transpose(0, 3, 1, 4, 2).reshape(DEPTH, 1, HEADS, HD, HD)
        res += [conv, lru, shift, wkv]
    return tuple(np.ascontiguousarray(a) for a in [y[None, :SEQ], y[None, SEQ:]] + res)
```

```python
from contextlib import ExitStack

import numpy as np

import concourse.bass as bass
from concourse import mybir

F32 = mybir.dt.float32
F32R = mybir.dt.float32r
U32 = mybir.dt.uint32
ALU = mybir.AluOpType
ACT = mybir.ActivationFunctionType
AX = mybir.AxisListType

P = 128
DEPTH, D, SEQ, DEC = 2, 1024, 512, 32
KD = D // P
T = SEQ + DEC
HALF = T // 2
LW = 512
NT = LW // P
RCOLS = 1792
ZT = 2 * NT + RCOLS // P
ZR = RCOLS // P
LEAD = 3
ZW = SEQ + DEC + 2 * LEAD
DEC0 = SEQ + LEAD
EW = DEC0 + DEC
MW = 580
MH = MW // 2
C = 64
NCH = SEQ // C
HEADS = 8
HD = 64
LEVELS = 6
QH = 16
NK = 128
PH = 8
TOPK = 16
EPS, GN_EPS = 1e-6, 64e-5
NEG = -3.0e38

IN_T, OUT_T, Q_T, PLE_T = ZT, KD, QH, KD
OUT_0, Q_0, PLE_0 = IN_T, IN_T + OUT_T, IN_T + OUT_T + Q_T
TILES = IN_T + OUT_T + Q_T + PLE_T
WK = KD + 2

SM = {}
_at = 0
for _name, _n in [("n1", 8), ("n2", 8), ("n3", 8), ("fin", 8), ("cw", 16), ("cb", 4), ("ba", 4), ("bx", 4),
                  ("lam", 4), ("mu", 14), ("w0", 4), ("a0", 4), ("kk", 4), ("ka", 4), ("rk", 4),
                  ("lnw", 4), ("lnb", 4), ("cst", 12), ("lst", 4), ("sst", 14)]:
    SM[_name] = _at
    _at += _n
NSM = _at
CN = {}
_at = 0
for _name, _n in [("ident", P), ("ones", P), ("heads", P), ("iota", P), ("causal", P), ("eye", C),
                  ("level", LEVELS * C), ("reset", MW)]:
    CN[_name] = _at
    _at += _n
NCN = _at
SO = {"conv": (0, 12), "lru": (24, 4), "shift": (32, 14)}
NSO = 60

BLK = 128
NB = SEQ // BLK
GT = 4
GROUPS = T // GT
EC = 4
ESTEPS = NK // EC
PAIRS_A, PAIRS_B = 8, 6
PAIRS_N = PAIRS_A + PAIRS_B
PAIRS_END = NK // 2 - NB * PAIRS_N
assert PAIRS_B * 4 <= BLK // GT and PAIRS_END >= 2


def constants():
    c = np.zeros((P, NCN), np.float32)
    i = np.arange(P)
    c[:, CN["ident"]:CN["ident"] + P] = np.eye(P)
    c[:, CN["ones"]:CN["ones"] + P] = 1.0
    c[:, CN["heads"]:CN["heads"] + P] = (i[:, None] // HD == i[None] // HD)
    c[:, CN["iota"]:CN["iota"] + P] = i[None]
    s, t = i[:, None] % C, np.arange(C)[None]
    c[:, CN["eye"]:CN["eye"] + C] = s == t
    c[:, CN["causal"]:CN["causal"] + C] = s < t
    c[:, CN["causal"] + C:CN["causal"] + P] = s <= t
    for k in range(LEVELS):
        b = 1 << k
        off = (s // (2 * b) == t // (2 * b)) & (s // b % 2 == 0) & (t // b % 2 == 1)
        c[:, CN["level"] + k * C:CN["level"] + (k + 1) * C] = off
    r = np.ones(MW)
    r[[k * C for k in range(NCH)] + [DEC0]] = 0.0
    c[:, CN["reset"]:CN["reset"] + MW] = r[None]
    return c


def trunk(nc, x, p, small, const, mixw, wkv0, w_in, w_out, wq, keys, ut, v, wple, y, small_out, wkv_out,
          do_peer=True):
    ctx = ExitStack()
    with ctx:
        def sem(name):
            return ctx.enter_context(nc.semaphore(name))

        words = 53214
        names = []
        RESERVED = 16512
        ps = ctx.enter_context(nc.psum_tensor("ps", [P, 8, 512], F32))
        top = [0]

        def aligned(at):
            return -(-at // 8) * 8

        def take(n, at=None, kind=F32):
            if at is None:
                at = aligned(top[0])
                top[0] = at + n
            assert at + n <= words, (at, n)
            names.append(f"m{len(names)}")
            return nc.alloc_sbuf_tensor_at(names[-1], [P, n], kind, offset=RESERVED + 4 * at)[:, :]

        def split(n):
            return take(n, kind=F32R)

        h = take(KD * T).rearrange("p (k t) -> p k t", k=KD)
        xn_at = top[0]
        xn = take(KD * T).rearrange("p (k t) -> p k t", k=KD)
        w_at = top[0]
        ymix = xn
        wslot = take(2 * WK * P).rearrange("p (s k n) -> p s k n", s=2, k=WK)
        sm = take(NSM)
        cn = take(NCN)
        rms = take(T)
        sout = take(NSO)
        sp = take(40)
        epst = take(2)
        A0 = aligned(top[0])

        def const_of(name, n):
            return cn[:, CN[name]:CN[name] + n]

        def small_of(name, i, n=1):
            return sm[:, SM[name] + i:SM[name] + i + n]

        ident, ones, hones, iota = (const_of(n, P) for n in ("ident", "ones", "heads", "iota"))
        causal, reset = const_of("causal", P), const_of("reset", MW)
        eye = const_of("eye", C)

        z_at = A0
        zin = take(ZT * ZW, z_at).rearrange("p (k t) -> p k t", k=ZT)
        zs_at = aligned(z_at + ZT * ZW)
        zs = take(ZR * MW, zs_at).rearrange("p (k t) -> p k t", k=ZR)
        sq = take(KD * T, zs_at).rearrange("p (k t) -> p k t", k=KD)
        mw_at = zs_at + ZR * MW
        mw = take(4 * LW, mw_at).rearrange("p (w n) -> p w n", w=4)
        t_at = mw_at + 4 * LW
        TB = [take(NT * MW, t_at + i * NT * MW).rearrange("p (k t) -> p k t", k=NT) for i in range(7)]
        assert t_at + 7 * NT * MW <= words
        top[0] = z_at
        bk = take(NT * P).rearrange("p (m t) -> p m t", m=NT)
        ar = take(NT * P).rearrange("p (m t) -> p m t", m=NT)
        vc = take(NT * P).rearrange("p (m t) -> p m t", m=NT)
        gm = take(HEADS * P).rearrange("p (h t) -> p h t", h=HEADS)
        bkT = take(LW)
        sav = take(LW)
        amT, ys, fs, ml0, ml1 = (take(NT * C).rearrange("p (m t) -> p m t", m=NT) for _ in range(5))
        ml = [ml0, ml1]
        xx = take(2 * NT * C).rearrange("p (w m t) -> p w m t", w=2, m=NT)
        xi, xt = xx[:, 0], xx[:, 1]
        st = take(NT * P).rearrange("p (m v) -> p m v", m=NT)
        stp = take(NT * HD).rearrange("p (m v) -> p m v", m=NT)
        sts = take(NT * HD).rearrange("p (m v) -> p m v", m=NT)
        o = zs[:, 8:12, :]
        assert top[0] <= zs_at

        top[0] = A0
        xh = split(KD * T).rearrange("p (k t) -> p k t", k=KD)
        xl = split(KD * T).rearrange("p (k t) -> p k t", k=KD)
        uraw = [take(KD * P).rearrange("p (k n) -> p k n", k=KD) for _ in range(2)]
        uh = [split(KD * P).rearrange("p (k n) -> p k n", k=KD) for _ in range(2)]
        ul = [split(KD * P).rearrange("p (k n) -> p k n", k=KD) for _ in range(2)]
        ge = [take(T) for _ in range(2)]
        s1 = take(2048)
        s2 = take(2048)
        e_top = aligned(top[0])
        stage = take(NK * BLK).rearrange("p (n t) -> p n t", n=NK)
        qT = take(QH * T, e_top).rearrange("p (q t) -> p q t", q=QH)
        sq2 = take(KD * T, e_top).rearrange("p (k t) -> p k t", k=KD)
        sel = take(3 * P).rearrange("p (w t) -> p w t", w=3)
        sel_t = take(3 * P).rearrange("p (w k) -> p w k", w=3)
        tv = take(QH * TOPK).rearrange("p (q k) -> p q k", q=QH)
        ti = take(QH * TOPK).rearrange("p (q k) -> p q k", q=QH)
        tf = take(QH * TOPK).rearrange("p (q k) -> p q k", q=QH)
        bv = take(PH * TOPK).rearrange("p (q k) -> p q k", q=PH)
        bi = take(PH * TOPK).rearrange("p (q k) -> p q k", q=PH)
        ba = take(2 * PH * TOPK).rearrange("p (w q k) -> p w q k", w=2, q=PH)
        bf = take(2 * PH * TOPK).rearrange("p (w q k) -> p w q k", w=2, q=PH)
        gsum = take(PH)
        qb = take(QH * BLK, xn_at).rearrange("p (q t) -> p q t", q=QH)
        kT = take(QH * NK, xn_at + QH * BLK).rearrange("p (q n) -> p q n", q=QH)
        oneA = take(2 * GT * P, w_at).rearrange("p (s j n) -> p s j n", s=2, j=GT)
        oneB = take(2 * GT * P, w_at + 2 * GT * P).rearrange("p (s j n) -> p s j n", s=2, j=GT)
        top[0] = A0
        vraw = [take(D) for _ in range(2)]
        vh = [split(D) for _ in range(2 * EC)]
        vl = [split(D) for _ in range(2 * EC)]
        assert top[0] <= e_top
        top[0] = e_top
        gs = [take(T) for _ in range(EC)]
        gf = [take(T) for _ in range(EC)]
        wf = [take(T) for _ in range(2)]
        wth = [split(T) for _ in range(2 * EC)]
        wtl = [split(T) for _ in range(2 * EC)]
        top[0] = A0
        pT = take(2 * T).rearrange("p (k t) -> p k t", k=2)
        sg = [take(T) for _ in range(2)]
        pg = [take(T) for _ in range(2)]
        sq3 = take(KD * T).rearrange("p (k t) -> p k t", k=KD)
        SQ = [sq, sq2, sq3]

        query_d = nc.dram_tensor("queries", [P, QH, T], F32, kind="Internal").ap()
        act_d = nc.dram_tensor("expert_inputs", [P, NK, T], F32, kind="Internal").ap()
        spare_d = nc.dram_tensor("spare", [3, P, 8], F32, kind="Internal").ap()
        gate_d = nc.dram_tensor("gate_matrix", [P, NK, T], F32, kind="Internal").ap()

        const_in = sem("const_in")
        x_in = sem("x_in")
        small_in = sem("small_in")
        mixw_in = sem("mixw_in")
        wkv_in = sem("wkv_in")
        keys_in = sem("keys_in")
        p_in = sem("p_in")
        w_in_s = [sem(f"w_slot{i}") for i in range(2)]
        layer_free = sem("layer_free")
        tile_done = sem("tile_done")
        h_ready = sem("h_ready")
        sq_ready = sem("sq_ready")
        sumsq = sem("sumsq")
        rms_ready = sem("rms_ready")
        xn_ready = sem("xn_ready")
        in_free = sem("in_free")
        lam_abs, lam_exp, lam_u, lam_ln = (sem(n) for n in ("lam_abs", "lam_exp", "lam_u", "lam_ln"))
        nsp_ready = sem("nsp_ready")
        xc_ready = sem("xc_ready")
        r_done, r_out, i_done, i_out = (sem(n) for n in ("r_done", "r_out", "i_done", "i_out"))
        a_ready, m2_ready, mult_ready = sem("a_ready"), sem("m2_ready"), sem("mult_ready")
        gg_ready, lru_done = sem("gg_ready"), sem("lru_done")
        zs_ready, lora_ready = sem("zs_ready"), sem("lora_ready")
        dec_done, dec_out, icl_done, icl_out, g_done, g_out = (
            sem(n) for n in ("dec_done", "dec_out", "icl_done", "icl_out", "g_done", "g_out"))
        kk_sq, kk_sum, kk_rt = sem("kk_sq"), sem("kk_sum"), sem("kk_rt")
        bonus_in, bonus_done = sem("bonus_in"), sem("bonus_done")
        cum_ready, exp_ready = sem("cum_ready"), sem("exp_ready")
        tilde_ready = sem("tilde_ready")
        v_ready = sem("v_ready")
        pair_done = sem("pair_done")
        turn_done = sem("turn_done")
        turn_out = sem("turn_out")
        gm_ready = sem("gm_ready")
        f_done, f_out = sem("f_done"), sem("f_out")
        m_ready = sem("m_ready")
        y_done = sem("y_done")
        y_out = sem("y_out")
        x_done = sem("x_done")
        sa_done, sa_out = sem("sa_done"), sem("sa_out")
        step_done = sem("step_done")
        o_out = sem("o_out")
        mean_done, oc_ready, var_done, std_out = (
            sem(n) for n in ("mean_done", "oc_ready", "var_done", "std_out"))
        y_ready = sem("y_ready")
        out_free = sem("out_free")
        q_free = sem("q_free")
        sc_done, sc_read = sem("sc_done"), sem("sc_read")
        best_ready, gexp = sem("best_ready"), sem("gexp")
        sel_ready, selT_done, selT_out = sem("sel_ready"), sem("selT_done"), sem("selT_out")
        hot_ready = sem("hot_ready")
        ab_ready, gmat_done, gmat_out = sem("ab_ready"), sem("gmat_done"), sem("gmat_out")
        gate_saved = sem("gate_saved")
        u_in = [sem(f"u_in{i}") for i in range(2)]
        v_in = [sem(f"v_in{i}") for i in range(2)]
        xh_ready, xl_ready = sem("xh_ready"), sem("xl_ready")
        uh_ready, ul_ready = sem("uh_ready"), sem("ul_ready")
        vh_ready, vl_ready = sem("vh_ready"), sem("vl_ready")
        wh_ready, wl_ready = sem("wh_ready"), sem("wl_ready")
        g_in = [sem(f"g_in{i}") for i in range(EC)]
        hid_done = sem("hid_done")
        ge_out = sem("ge_out")
        w_ready = sem("w_ready")
        eo_done = sem("eo_done")
        eo_out = sem("eo_out")
        q_saved = sem("q_saved")
        qb_in = sem("qb_in")
        act_saved = [sem(f"act_saved{i}") for i in range(2)]
        ple_sig = sem("ple_sig")
        ple_free = sem("ple_free")
        outs_ready = sem("outs_ready")
        stored = sem("stored")
        y_stored = sem("y_stored")
        y_out_ready = sem("y_out_ready")

        waits_passed = {e.engine: sem(f"waits_passed{i}") for i, e in enumerate([nc.sync, nc.tensor, nc.vector, nc.scalar])}

        NCHUNK = NCH + 1
        PAIRS = [(m, q) for m in range(NT) for q in (0, HD)]
        NBLK = NB + 1

        def passed(eng):
            eng.sem_inc(waits_passed[eng.engine], 1)

        def halves(bank, w):
            return ps[:, bank:bank + 2, 0:w]

        def cut(ap, w):
            return ap.rearrange("p (a w) -> p a w", a=2)

        block = ctx.enter_context(nc.Block())

        @block.sync
        def _(sp_):
            sp_.dma_start(cn, const[:, :]).then_inc(const_in, 16)
            sp_.dma_start(h, x[:, :, :]).then_inc(x_in, 16)

            def weight(L, base, n, j, src, k=KD):
                sp_.wait_ge(tile_done, L * TILES + base + n + 1)
                sp_.dma_start(wslot[:, j, 0:k, :], src).then_inc(w_in_s[j], 16)

            with sp_.Fori(0, DEPTH) as L:
                sp_.wait_ge(layer_free, L + 1)
                sp_.dma_start(sm, small[L]).then_inc(small_in, 16)
                sp_.dma_start(mw, mixw[L]).then_inc(mixw_in, 16)
                with sp_.Fori(0, IN_T // 2) as g:
                    for j in range(2):
                        weight(L, 0, g * 2 + j, j, w_in[L].rearrange("(k p) n -> p k n", p=P)[:, :, bass.ds((g * 2 + j) * P, P)])
                sp_.wait_ge(lru_done, L + 1)
                sp_.wait_ge(zs_ready, L + 1)
                sp_.dma_start(sts, wkv0[L]).then_inc(wkv_in, 16)
                with sp_.Fori(0, OUT_T // 2) as g:
                    for j in range(2):
                        weight(L, OUT_0, g * 2 + j, j, w_out[L].rearrange("(k p) n -> p k n", p=P)[:, :, bass.ds((g * 2 + j) * P, P)])
                with sp_.Fori(0, Q_T // 2) as g:
                    for j in range(2):
                        weight(L, Q_0, g * 2 + j, j, wq[L].rearrange("(k p) n -> p k n", p=P)[:, :, bass.ds((g * 2 + j) * P, P)])
                if do_peer:
                    sp_.wait_ge(xn_ready, L * 3 + 2)

                    def load_u(m, j):
                        sp_.wait_ge(ul_ready, L * NK + m * 2 + j + 1)
                        sp_.dma_start(uraw[j], ut[L, bass.ds(m * 2 + j, 1)].rearrange("a p k n -> (a p) k n")).then_inc(u_in[j], 16)

                    def load_qb(b, nt, col):
                        sp_.wait_ge(sc_done, L * NBLK + b + 1)
                        sp_.dma_start(qb[:, :, 0:nt], query_d[:, :, col]).then_inc(qb_in, 16)

                    load_u(0, 0)
                    load_u(0, 1)
                    sp_.wait_ge(xl_ready, L + 1)
                    sp_.wait_ge(tile_done, L * TILES + (Q_0 + Q_T + 2))
                    sp_.dma_start(kT, keys[L]).then_inc(keys_in, 16)
                    sp_.wait_ge(q_saved, L * 16 + 16)
                    passed(sp_)
                    with sp_.Fori(0, NB) as b:
                        load_qb(b, BLK, bass.ds(b * BLK, BLK))
                        with sp_.Fori(0, PAIRS_N) as g:
                            for j in range(2):
                                load_u(b * PAIRS_N + g + 1, j)
                    load_qb(NB, DEC, slice(SEQ, T))
                    with sp_.Fori(0, PAIRS_END - 1) as g:
                        for j in range(2):
                            load_u(g + (NB * PAIRS_N + 1), j)
                    sp_.wait_ge(sel_ready, (L + 1) * NBLK)
                    sp_.wait_ge(hid_done, (L + 1) * NK + 2)
                    for j in range(2):
                        sp_.wait_ge(act_saved[j], L * (8 * NK) + (8 * NK + 16))
                    passed(sp_)

                    def load_v(e, j):
                        sp_.wait_ge(vl_ready, L * NK + e * EC + j + 1)
                        sp_.dma_start(vraw[j % 2], v[L].rearrange("(p n) d -> p n d", n=NK)[:, bass.ds(e * EC + j, 1), :].rearrange("p a d -> p (a d)")).then_inc(v_in[j % 2], 16)

                    with sp_.Fori(0, ESTEPS) as e:
                        load_v(e, 0)
                        load_v(e, 1)
                        sp_.wait_ge(gate_saved, L * (16 * NBLK) + (16 * NBLK + 16))
                        for j in range(EC):
                            if j > 1:
                                load_v(e, j)
                            sp_.wait_ge(w_ready, L * NK + e * EC + j + 1)
                            for dst, src in ((gs[j], gate_d), (gf[j], act_d)):
                                sp_.dma_start(dst, src[:, bass.ds(e * EC + j, 1), :].rearrange("p a t -> p (a t)")).then_inc(g_in[j], 16)
                sp_.wait_ge(h_ready, L * 3 + 3)
                sp_.dma_start(pT, p[L]).then_inc(p_in, 16)
                with sp_.Fori(0, PLE_T // 2) as g:
                    for j in range(2):
                        weight(L, PLE_0, g * 2 + j, j, wple[L].rearrange("(k p) n -> p k n", p=P)[:, :, bass.ds((g * 2 + j) * P, P)], WK)
            sp_.wait_ge(y_out_ready, 1)
            sp_.dma_start(y[:, :, :], xn).then_inc(y_stored, 16)
            sp_.wait_ge(y_stored, 16)
            sp_.wait_ge(stored, 16 * 3 * DEPTH)

        @block.gpsimd
        def _(pool):
            tt = nc.gpsimd.tensor_tensor
            pool.sem_inc(ul_ready, 2)
            pool.sem_inc(vl_ready, 2)
            with pool.Fori(0, DEPTH) as L:
                pool.wait_ge(outs_ready, L + 1)
                pool.dma_start(small_out[L], sout).then_inc(stored, 16)
                pool.dma_start(wkv_out[L, 0], stp).then_inc(stored, 16)
                pool.dma_start(wkv_out[L, 1], sts).then_inc(stored, 16)
                if do_peer:
                    pool.wait_ge(xh_ready, L + 1)
                    tt(xl, xn, xh.bitcast(F32), ALU.subtract).then_inc(xl_ready, 1)

                    def low_u(m, j):
                        pool.wait_ge(uh_ready, L * NK + m * 2 + j + 1)
                        tt(ul[j], uraw[j], uh[j].bitcast(F32), ALU.subtract).then_inc(ul_ready, 1)

                    def weigh(b, g, k):
                        pool.wait_ge(hot_ready, (L * GROUPS + b * (BLK // GT) + g * 4 + k) * 2 + 1)
                        gate = sel[:, 0, bass.ds(g * (4 * GT) + k * GT, GT)]
                        tt(oneB[:, k % 2], oneB[:, k % 2], gate.unsqueeze(2).to_broadcast([P, GT, P]), ALU.mult).then_inc(ab_ready, 1)

                    low_u(0, 0)
                    low_u(0, 1)
                    with pool.Fori(0, NB) as b:
                        with pool.Fori(0, PAIRS_A) as g:
                            for j in range(2):
                                low_u(b * PAIRS_N + g + 1, j)
                        with pool.Fori(0, PAIRS_B) as g:
                            for j in range(2):
                                weigh(b, g, 2 * j)
                                weigh(b, g, 2 * j + 1)
                                low_u(b * PAIRS_N + g + (PAIRS_A + 1), j)
                        with pool.Fori(0, BLK // (4 * GT) - PAIRS_B) as g:
                            for k in range(4):
                                weigh(b, g + PAIRS_B, k)
                    with pool.Fori(0, PAIRS_END - 1) as g:
                        for j in range(2):
                            low_u(g + (NB * PAIRS_N + 1), j)
                    with pool.Fori(0, DEC // (4 * GT)) as g:
                        for k in range(4):
                            weigh(NB, g, k)
                    with pool.Fori(0, ESTEPS // 2) as e2:
                        for half in range(2):
                            for j in range(EC):
                                pool.wait_ge(vh_ready, L * NK + e2 * (2 * EC) + (half * EC + j + 1))
                                tt(vl[half * EC + j], vraw[j % 2], vh[half * EC + j].bitcast(F32), ALU.subtract).then_inc(vl_ready, 1)

        @block.tensor
        def _(pe):
            mm = nc.tensor.matmul
            pe.sem_inc(tile_done, 2)
            pe.sem_inc(hid_done, 2)
            pe.sem_inc(gmat_done, 2)
            pe.sem_inc(eo_done, 2 * KD)
            pe.sem_inc(sc_done, 1)
            pe.wait_ge(const_in, 16)

            def norm(L, i):
                pe.wait_ge(sq_ready, L * 3 + i + 1)
                for a in range(2):
                    for k in range(KD):
                        last = mm(ps[:, a, 0:HALF], ones, SQ[i][:, k, a * HALF:(a + 1) * HALF],
                                  start=(k == 0), stop=(k == KD - 1))
                last.then_inc(sumsq, 1)

            def tile(j, slot, rhs, ks, bank, inc):
                for a in range(2):
                    for n, k in enumerate(ks):
                        last = mm(ps[:, bank + a, 0:HALF], wslot[:, slot, k, :], rhs[:, n, a * HALF:(a + 1) * HALF],
                                  start=(n == 0), stop=(n == len(ks) - 1))
                if inc:
                    last.then_inc(tile_done, 1)

            def linear(L, base, count, rhs, free):
                passed(pe)
                with pe.Fori(0, count // 2) as g:
                    for j in range(2):
                        pe.wait_ge(w_in_s[j], L * (16 * TILES // 2) + g * 16 + 16 * (base // 2) + 16)
                        pe.wait_ge(free, L * (count + 2) + g * 2 + j + 1)
                        tile(j, j, rhs, range(KD), 2 * j, True)

            def wide(lhs, rhs, n0=0):
                for n in range(NT):
                    for a in range(2):
                        last = mm(ps[:, 2 * n + a, 0:MH], lhs(n), rhs(n)[:, a * MH:(a + 1) * MH],
                                  start=True, stop=True)
                return last

            with pe.Fori(0, DEPTH) as L:
                norm(L, 0)
                pe.wait_ge(xn_ready, L * 3 + 1)
                linear(L, 0, IN_T, xn, in_free)
                pe.wait_ge(in_free, L * (IN_T + 2) + IN_T + 2)
                pe.wait_ge(mixw_in, L * 16 + 16)
                pe.wait_ge(xc_ready, L + 1)
                wide(lambda n: mw[:, 0, n * P:(n + 1) * P], lambda n: TB[0][:, n, :]).then_inc(r_done, 1)
                pe.wait_ge(r_out, L + 1)
                wide(lambda n: mw[:, 1, n * P:(n + 1) * P], lambda n: TB[0][:, n, :]).then_inc(i_done, 1)
                pe.wait_ge(i_out, L + 1)
                pe.wait_ge(lora_ready, L + 1)
                wide(lambda n: mw[0:64, 2, n * P:(n + 1) * P], lambda n: zs[0:64, 12, :]).then_inc(dec_done, 1)
                pe.wait_ge(dec_out, L + 1)
                wide(lambda n: mw[64:128, 2, n * P:(n + 1) * P], lambda n: zs[64:128, 12, :]).then_inc(icl_done, 1)
                pe.wait_ge(icl_out, L + 1)
                wide(lambda n: mw[:, 3, n * P:(n + 1) * P], lambda n: zs[:, 13, :]).then_inc(g_done, 1)
                pe.wait_ge(g_out, L + 1)
                pe.wait_ge(kk_sq, L + 1)
                wide(lambda n: hones, lambda n: TB[3][:, n, :]).then_inc(kk_sum, 1)
                pe.wait_ge(kk_rt, L + 1)
                pe.wait_ge(bonus_in, L + 1)
                wide(lambda n: hones, lambda n: TB[6][:, n, :]).then_inc(bonus_done, 1)
                pe.wait_ge(cum_ready, L + 1)

                def chunk(c):
                    n = L * NCHUNK + c
                    pe.wait_ge(tilde_ready, n + 1)
                    for hd in range(HEADS):
                        m, q = hd // 2, hd % 2 * HD
                        last = mm(ps[:, hd % 2, m * P:(m + 1) * P], bk[q:q + HD, m, :], ar[q:q + HD, m, :],
                                  start=True, stop=True)
                    last.then_inc(pair_done, 1)
                    pe.wait_ge(v_ready, n + 1)
                    for m in range(NT):
                        nc.tensor.transpose(ps[:, 2, m * P:(m + 1) * P], bk[:, m, :], ident)
                    for m in range(NT):
                        last = nc.tensor.transpose(ps[:, 3, m * P:(m + 1) * P], vc[:, m, :], ident)
                    last.then_inc(turn_done, 1)
                    for lv in range(LEVELS):
                        pe.wait_ge(m_ready, n * (LEVELS + 1) + lv + 1)
                        passed(pe)
                        for m, q in PAIRS:
                            last = mm(ps[q:q + C, 4, m * C:(m + 1) * C], ml[lv % 2][q:q + C, m, :],
                                      eye[q:q + C] if lv == 0 else xi[q:q + C, m, :], start=True, stop=True)
                        last.then_inc(y_done, 1)
                        if lv == 0:
                            continue
                        pe.wait_ge(y_out, n * (LEVELS - 1) + lv)
                        passed(pe)
                        for m, q in PAIRS:
                            last = mm(ps[q:q + C, 6, m * C:(m + 1) * C], ys[q:q + C, m, :], xt[q:q + C, m, :],
                                      start=True, stop=True)
                        if lv < LEVELS - 1:
                            for m, q in PAIRS:
                                last = mm(ps[q:q + C, 5, m * C:(m + 1) * C], xt[q:q + C, m, :], ys[q:q + C, m, :],
                                          start=True, stop=True)
                        last.then_inc(x_done, 1)
                        if lv == 1:
                            pe.wait_ge(turn_out, n + 1)
                            pe.wait_ge(gm_ready, n + 1)
                            for m, q in PAIRS:
                                hd = 2 * m + q // HD
                                mm(ps[q:q + C, 7, m * C:(m + 1) * C], ar[:, m, 0:C], st[:, m, q:q + HD], start=True, stop=False)
                                last = mm(ps[q:q + C, 7, m * C:(m + 1) * C], gm[:, hd, 0:C], sav[:, hd * HD:(hd + 1) * HD],
                                          start=False, stop=True)
                            last.then_inc(f_done, 1)
                    pe.wait_ge(m_ready, (n + 1) * (LEVELS + 1))
                    pe.wait_ge(f_out, n + 1)
                    passed(pe)
                    for m, q in PAIRS:
                        last = mm(ps[q:q + C, 4, m * C:(m + 1) * C], xt[q:q + C, m, :], fs[q:q + C, m, :],
                                  start=True, stop=True)
                    last.then_inc(sa_done, 1)
                    pe.wait_ge(sa_out, n + 1)
                    for hd in range(HEADS):
                        m, q = hd // 2, hd % 2 * HD
                        mm(ps[q:q + HD, 5, m * HD:(m + 1) * HD], bkT[:, hd * HD:(hd + 1) * HD],
                           sav[:, hd * HD:(hd + 1) * HD], start=True, stop=True)
                    for m in range(NT):
                        mm(ps[:, 6, m * C:(m + 1) * C], st[:, m, :], ar[:, m, C:P], start=True, stop=False)
                        for hd in (2 * m, 2 * m + 1):
                            q = hd % 2 * HD
                            last = mm(ps[q:q + HD, 6, m * C:(m + 1) * C], sav[:, hd * HD:(hd + 1) * HD], gm[:, hd, C:P],
                                      start=False, stop=True)
                    last.then_inc(step_done, 1)

                passed(pe)
                with pe.Fori(0, NCH) as c:
                    chunk(c)
                chunk(NCH)
                pe.wait_ge(o_out, (L + 1) * NCHUNK)
                pe.wait_ge(outs_ready, L + 1)
                wide(lambda n: hones, lambda n: o[:, n, :]).then_inc(mean_done, 1)
                pe.wait_ge(oc_ready, L + 1)
                wide(lambda n: hones, lambda n: TB[6][:, n, :]).then_inc(var_done, 1)
                pe.wait_ge(y_ready, L + 1)
                linear(L, OUT_0, OUT_T, ymix, out_free)
                norm(L, 1)
                pe.wait_ge(xn_ready, L * 3 + 2)
                linear(L, Q_0, Q_T, xn, q_free)
                if do_peer:
                    pe.wait_ge(q_free, L * (Q_T + 2) + Q_T + 2)
                    pe.wait_ge(keys_in, L * 16 + 16)

                    pe.wait_ge(xl_ready, L + 1)

                    def hidden(m, j):
                        i = L * NK + m * 2 + j
                        pe.wait_ge(ul_ready, i + 1 + 2)
                        pe.wait_ge(ge_out, i + 1)
                        for a in range(2):
                            for k in range(KD):
                                for w, (lhs, rhs) in enumerate([(uh, xh), (uh, xl), (ul, xh)]):
                                    last = mm(ps[:, j * 2 + a, 0:HALF], lhs[j][:, k, :], rhs[:, k, a * HALF:(a + 1) * HALF],
                                              start=(k + w == 0), stop=(k == KD - 1 and w == 2))
                        last.then_inc(hid_done, 1)

                    def scores(b, nt):
                        n = L * NBLK + b
                        pe.wait_ge(qb_in, n * 16 + 16)
                        pe.wait_ge(ge_out, L * NK + b * (2 * PAIRS_N) + 2)
                        passed(pe)
                        for q in range(QH):
                            last = mm(ps[0:nt, q // 4, q % 4 * P:(q % 4 + 1) * P], qb[:, q, 0:nt], kT[:, q, :],
                                      start=True, stop=True)
                        last.then_inc(sc_done, 1)
                        pe.wait_ge(sc_read, n + 1)
                        passed(pe)

                    def turn(b, nt):
                        n = L * NBLK + b
                        pe.wait_ge(sel_ready, n + 1)
                        passed(pe)
                        for w in range(3):
                            last = nc.tensor.transpose(ps[:, 4, w * nt:(w + 1) * nt], sel_t[0:nt, w, :], ident[0:nt, 0:nt])
                        last.then_inc(selT_done, 1)

                    def gates(b, g, k):
                        i = L * GROUPS + b * (BLK // GT) + g * 4 + k
                        pe.wait_ge(hot_ready, i * 2 + 2)
                        pe.wait_ge(ab_ready, i + 1)
                        pe.wait_ge(gmat_out, i + 1)
                        for j in range(GT):
                            last = mm(ps[:, 5 + k % 2, j * P:(j + 1) * P], oneA[:, k % 2, j, :], oneB[:, k % 2, j, :],
                                      start=True, stop=True)
                        last.then_inc(gmat_done, 1)

                    passed(pe)
                    with pe.Fori(0, NB) as b:
                        scores(b, BLK)
                        with pe.Fori(0, PAIRS_A) as g:
                            for j in range(2):
                                hidden(b * PAIRS_N + g, j)
                        turn(b, BLK)
                        with pe.Fori(0, PAIRS_B) as g:
                            for j in range(2):
                                hidden(b * PAIRS_N + g + PAIRS_A, j)
                                gates(b, g, 2 * j)
                                gates(b, g, 2 * j + 1)
                        with pe.Fori(0, BLK // (4 * GT) - PAIRS_B) as g:
                            for k in range(4):
                                gates(b, g + PAIRS_B, k)
                    scores(NB, DEC)
                    with pe.Fori(0, PAIRS_END) as g:
                        for j in range(2):
                            hidden(g + NB * PAIRS_N, j)
                    turn(NB, DEC)
                    with pe.Fori(0, DEC // (4 * GT)) as g:
                        for k in range(4):
                            gates(NB, g, k)
                    pe.wait_ge(gmat_out, (L + 1) * GROUPS + 2)
                    passed(pe)
                    with pe.Fori(0, ESTEPS // 2) as e2:
                        for half in range(2):
                            for m in range(KD):
                                pe.wait_ge(eo_out, (L * ESTEPS + e2 * 2 + half) * KD + m + 1)
                                for j in range(EC):
                                    at = half * EC + j
                                    if m == 0:
                                        pe.wait_ge(vl_ready, L * NK + e2 * (2 * EC) + (at + 1 + 2))
                                        pe.wait_ge(wl_ready, L * NK + e2 * (2 * EC) + (at + 1))
                                    for a in range(2):
                                        for w, (lhs, rhs) in enumerate([(vh, wth), (vh, wtl), (vl, wth)]):
                                            last = mm(ps[:, 4 + m % 2 * 2 + a, 0:HALF], lhs[at][:, m * P:(m + 1) * P],
                                                      rhs[at][:, a * HALF:(a + 1) * HALF], start=(j + w == 0), stop=(j == EC - 1 and w == 2))
                                last.then_inc(eo_done, 1)
                norm(L, 2)
                pe.wait_ge(xn_ready, L * 3 + 3)
                pe.wait_ge(p_in, L * 16 + 16)
                passed(pe)
                with pe.Fori(0, PLE_T // 2) as g:
                    for j in range(2):
                        pe.wait_ge(w_in_s[j], L * (16 * TILES // 2) + g * 16 + 16 * (PLE_0 // 2) + 16)
                        pe.wait_ge(ple_free, L * (PLE_T + 2) + g * 2 + j + 1)
                        tile(j, j, xn, range(KD), 2 * j, False)
                        tile(j, j, pT, [KD, KD + 1], 4 + 2 * j, True)
            pe.wait_ge(sq_ready, 3 * DEPTH + 1)
            for a in range(2):
                for k in range(KD):
                    last = mm(ps[:, a, 0:HALF], ones, SQ[2][:, k, a * HALF:(a + 1) * HALF],
                              start=(k == 0), stop=(k == KD - 1))
            last.then_inc(sumsq, 1)

        @block.scalar
        def _(act):
            av = nc.scalar.activation
            act.sem_inc(gmat_out, 2)
            act.sem_inc(ge_out, 2)
            act.wait_ge(const_in, 16)
            act.wait_ge(x_in, 16)
            for i, s in enumerate([*act_saved, gate_saved]):
                act.dma_start(spare_d[i], cn[:, 0:8]).then_inc(s, 16)

            def norm(n, i):
                act.wait_ge(h_ready, n)
                for k in range(KD):
                    last = av(SQ[i][:, k, :], h[:, k, :], ACT.Square)
                last.then_inc(sq_ready, 1)
                act.wait_ge(sumsq, n)
                av(cut(rms, HALF), halves(0, HALF), ACT.Sqrt, bias=epst[:, 0:1], scale=1.0 / D).then_inc(rms_ready, 1)

            def wide(dst, func, bias=None, part=slice(0, P)):
                for n in range(NT):
                    last = av(cut(dst[:, n, :], MH), halves(2 * n, MH), func,
                              **({"bias": bias(n)} if bias else {}))
                return last

            def done(L, base, n):
                act.wait_ge(tile_done, L * TILES + base + n + 3)

            with act.Fori(0, DEPTH) as L:
                norm(L * 3 + 1, 0)
                act.drain()
                act.sem_inc(in_free, 2)
                with act.Fori(0, IN_T // 2) as g:
                    for j in range(2):
                        done(L, 0, g * 2 + j)
                        at = zin[:, bass.ds(g * 2 + j, 1), :].rearrange("p a t -> p (a t)")
                        av(at[:, LEAD:LEAD + HALF], ps[:, 2 * j, 0:HALF], ACT.Copy)
                        av(at[:, LEAD + HALF:LEAD + SEQ], ps[:, 2 * j + 1, 0:SEQ - HALF], ACT.Copy)
                        av(at[:, ZW - DEC:ZW], ps[:, 2 * j + 1, SEQ - HALF:HALF], ACT.Copy).then_inc(in_free, 1)
                act.wait_ge(lam_abs, L + 1)
                av(sp[:, 4:8], sp[:, 0:4], ACT.Exp, scale=-1.0).then_inc(lam_exp, 1)
                act.wait_ge(lam_u, L + 1)
                av(sp[:, 16:20], sp[:, 8:12], ACT.Ln).then_inc(lam_ln, 1)
                act.wait_ge(r_done, L + 1)
                wide(TB[1], ACT.Sigmoid, lambda n: small_of("ba", n)).then_inc(r_out, 1)
                act.wait_ge(i_done, L + 1)
                wide(TB[2], ACT.Sigmoid, lambda n: small_of("bx", n)).then_inc(i_out, 1)
                act.wait_ge(nsp_ready, L + 1)
                passed(act)
                act.drain()
                for n in range(NT):
                    av(TB[3][:, n, :], TB[1][:, n, :], ACT.Tanh, scale=sp[:, 32 + n:33 + n])
                for n in range(NT):
                    last = av(TB[4][:, n, :], TB[1][:, n, :], ACT.Exp, scale=sp[:, 32 + n:33 + n])
                last.then_inc(a_ready, 1)
                for n in range(NT):
                    last = av(zin[:, NT + n, LEAD:ZW], zin[:, NT + n, LEAD:ZW], ACT.Gelu_apprx_tanh)
                last.then_inc(gg_ready, 1)
                act.wait_ge(m2_ready, L + 1)
                av(TB[5][:, :, :], TB[5][:, :, :], ACT.Sqrt, scale=-1.0).then_inc(mult_ready, 1)
                act.wait_ge(zs_ready, L + 1)
                av(zs[0:64, 12, :], zs[0:64, 12, :], ACT.Tanh)
                av(zs[:, 13, :], zs[:, 13, :], ACT.Sigmoid).then_inc(lora_ready, 1)
                act.wait_ge(lru_done, L + 1)
                act.wait_ge(dec_done, L + 1)
                wide(TB[0], ACT.Sigmoid, lambda n: small_of("w0", n)).then_inc(dec_out, 1)
                act.wait_ge(icl_done, L + 1)
                wide(TB[4], ACT.Sigmoid, lambda n: small_of("a0", n)).then_inc(icl_out, 1)
                act.wait_ge(g_done, L + 1)
                wide(TB[5], ACT.Copy).then_inc(g_out, 1)
                act.wait_ge(kk_sum, L + 1)
                wide(TB[6], ACT.Sqrt).then_inc(kk_rt, 1)
                act.wait_ge(cum_ready, L + 1)
                av(TB[0][:, :, :], TB[0][:, :, :], ACT.Exp)
                av(TB[6][:, :, :], TB[1][:, :, :], ACT.Exp, scale=-1.0)
                act.drain()
                av(TB[1][:, :, :], TB[1][:, :, :], ACT.Exp).then_inc(exp_ready, 1)

                def chunk(c, col):
                    n = L * NCHUNK + c
                    av(vc[0:HD, :, C:P], zs[0:HD, 8:12, col], ACT.Copy)
                    av(vc[HD:P, :, 0:C], zs[HD:P, 8:12, col], ACT.Copy).then_inc(v_ready, 1)
                    act.wait_ge(turn_done, n + 1)
                    av(bkT, ps[:, 2, :], ACT.Copy)
                    av(sav, ps[:, 3, :], ACT.Copy).then_inc(turn_out, 1)
                    for lv in range(1, LEVELS):
                        act.wait_ge(y_done, n * LEVELS + lv + 1)
                        av(ys, ps[:, 4, 0:NT * C].rearrange("p (m t) -> p m t", m=NT), ACT.Copy).then_inc(y_out, 1)
                        if lv == 1:
                            act.wait_ge(f_done, n + 1)
                            av(fs, ps[:, 7, 0:NT * C].rearrange("p (m t) -> p m t", m=NT), ACT.Copy).then_inc(f_out, 1)
                    act.wait_ge(sa_done, n + 1)
                    for q in (0, HD):
                        last = av(sav[q:q + C, :].rearrange("p (m w v) -> p m w v", m=NT, w=2)[:, :, q // HD, :],
                                  ps[q:q + C, 4, 0:NT * C].rearrange("p (m t) -> p m t", m=NT), ACT.Copy)
                    last.then_inc(sa_out, 1)
                    act.wait_ge(step_done, n + 1)
                    passed(act)
                    av(o[:, :, col], ps[:, 6, 0:NT * C].rearrange("p (m t) -> p m t", m=NT), ACT.Copy).then_inc(o_out, 1)

                with act.Fori(0, NCH) as c:
                    chunk(c, bass.ds(c * C, C))
                chunk(NCH, slice(DEC0, DEC0 + C))
                act.wait_ge(var_done, L + 1)
                wide(TB[6], ACT.Sqrt, lambda n: epst[:, 1:2]).then_inc(std_out, 1)
                norm(L * 3 + 2, 1)
                if do_peer:
                    act.wait_ge(xn_ready, L * 3 + 2)
                    passed(act)
                    av(xh, xn, ACT.Copy).then_inc(xh_ready, 1)
                act.drain()
                act.sem_inc(q_free, 2)
                with act.Fori(0, Q_T // 2) as g:
                    for j in range(2):
                        done(L, Q_0, g * 2 + j)
                        at = qT[:, bass.ds(g * 2 + j, 1), :].rearrange("p a t -> p (a t)")
                        av(cut(at, HALF), halves(2 * j, HALF), ACT.Copy).then_inc(q_free, 1)
                if do_peer:
                    act.wait_ge(q_free, L * (Q_T + 2) + (Q_T + 2))
                    act.dma_start(query_d[:, :, :], qT).then_inc(q_saved, 16)

                    def high_u(m, j):
                        act.wait_ge(u_in[j], L * (8 * NK) + m * 16 + 16)
                        act.wait_ge(hid_done, L * NK + m * 2 + j + 1)
                        av(uh[j], uraw[j], ACT.Copy).then_inc(uh_ready, 1)

                    def gelu(m, j, ahead=True):
                        i = L * NK + m * 2 + j
                        act.wait_ge(hid_done, i + 1 + 2)
                        act.wait_ge(act_saved[j], L * (8 * NK) + m * 16 + 16)
                        av(cut(ge[j], HALF), halves(j * 2, HALF), ACT.Gelu_apprx_tanh).then_inc(ge_out, 1)
                        if ahead:
                            high_u(m + 1, j)
                        act.wait_ge(ge_out, i + 1 + 2)
                        act.dma_start(act_d[:, bass.ds(m * 2 + j, 1), :].rearrange("p a t -> p (a t)"), ge[j]).then_inc(act_saved[j], 16)

                    def scores(b, nt):
                        act.wait_ge(sc_done, L * NBLK + b + 2)
                        av(s2[0:nt].rearrange("p (a n) -> p a n", a=4), ps[0:nt, 0:4, :], ACT.Copy).then_inc(sc_read, 1)

                    def soften(b, nt):
                        act.wait_ge(best_ready, L * NBLK + b + 1)
                        av(bv[0:nt], bv[0:nt], ACT.Exp).then_inc(gexp, 1)

                    def turned(b, nt):
                        n = L * NBLK + b
                        act.wait_ge(selT_done, n + 1)
                        av(sel[:, :, 0:nt], ps[:, 4, 0:3 * nt].rearrange("p (w t) -> p w t", w=3), ACT.Copy).then_inc(selT_out, 1)
                        act.wait_ge(q_saved, L * 16 + 16)
                        act.wait_ge(gate_saved, n * 16 + 16)

                    def gates(b, g, k):
                        act.wait_ge(gmat_done, L * GROUPS + b * (BLK // GT) + g * 4 + k + 3)
                        av(stage[:, :, bass.ds(g * (4 * GT) + k * GT, GT)],
                           ps[:, 5 + k % 2, :].rearrange("p (j n) -> p n j", j=GT), ACT.Copy).then_inc(gmat_out, 1)

                    def save(b, nt, col):
                        act.wait_ge(gmat_out, L * GROUPS + b * (BLK // GT) + nt // GT + 2)
                        act.dma_start(gate_d[:, :, col], stage[:, :, 0:nt]).then_inc(gate_saved, 16)

                    high_u(0, 0)
                    high_u(0, 1)
                    with act.Fori(0, NB) as b:
                        scores(b, BLK)
                        with act.Fori(0, PAIRS_A - 2) as g:
                            for j in range(2):
                                gelu(b * PAIRS_N + g, j)
                        soften(b, BLK)
                        with act.Fori(0, 2) as g:
                            for j in range(2):
                                gelu(b * PAIRS_N + g + (PAIRS_A - 2), j)
                        turned(b, BLK)
                        with act.Fori(0, PAIRS_B) as g:
                            for j in range(2):
                                gelu(b * PAIRS_N + g + PAIRS_A, j)
                                gates(b, g, 2 * j)
                                gates(b, g, 2 * j + 1)
                        with act.Fori(0, BLK // (4 * GT) - PAIRS_B) as g:
                            for k in range(4):
                                gates(b, g + PAIRS_B, k)
                        save(b, BLK, bass.ds(b * BLK, BLK))
                    scores(NB, DEC)
                    with act.Fori(0, PAIRS_END - 1) as g:
                        for j in range(2):
                            gelu(g + NB * PAIRS_N, j)
                    soften(NB, DEC)
                    for j in range(2):
                        gelu(NK // 2 - 1, j, ahead=False)
                    turned(NB, DEC)
                    with act.Fori(0, DEC // (4 * GT)) as g:
                        for k in range(4):
                            gates(NB, g, k)
                    save(NB, DEC, slice(SEQ, T))
                    with act.Fori(0, ESTEPS // 2) as e2:
                        for half in range(2):
                            for j in range(EC):
                                act.wait_ge(eo_done, (L * ESTEPS + e2 * 2 + half + 1) * KD)
                                act.wait_ge(w_ready, L * NK + e2 * (2 * EC) + (half * EC + j + 1 + EC))
                                av(wth[half * EC + j], wf[j % 2], ACT.Copy).then_inc(wh_ready, 1)
                norm(L * 3 + 3, 2)
                with act.Fori(0, PLE_T // 2) as g:
                    for j in range(2):
                        done(L, PLE_0, g * 2 + j)
                        act.wait_ge(ple_free, L * (PLE_T + 2) + g * 2 + j + 1)
                        av(cut(sg[j], HALF), halves(2 * j, HALF), ACT.Sigmoid).then_inc(ple_sig, 1)
            norm(3 * DEPTH + 1, 2)

        @block.vector
        def _(dve):
            ts, tt, stt = nc.vector.tensor_scalar, nc.vector.tensor_tensor, nc.vector.scalar_tensor_tensor
            copy = nc.vector.tensor_copy
            dve.memset(epst[:, 0:1], EPS)
            dve.memset(epst[:, 1:2], GN_EPS)
            dve.drain()
            dve.sem_inc(layer_free, 1)
            dve.sem_inc(w_ready, EC)
            dve.sem_inc(eo_out, 2)
            dve.wait_ge(const_in, 16)
            dve.wait_ge(x_in, 16)

            def norm(n, gain, last_sem):
                dve.wait_ge(rms_ready, n)
                dve.reciprocal(rms, rms)
                dve.drain()
                for k in range(KD):
                    last = stt(xn[:, k, :], h[:, k, :], small_of(gain, k), rms, ALU.mult, ALU.mult)
                last.then_inc(last_sem, 1)

            def add_tile(k, bank):
                at = h[:, k, :].rearrange("p a t -> p (a t)") if not isinstance(k, int) else h[:, k, :]
                return tt(cut(at, HALF), halves(bank, HALF), cut(at, HALF), ALU.add)

            with dve.Fori(0, DEPTH) as L:
                dve.drain()
                dve.sem_inc(h_ready, 1)
                dve.wait_ge(small_in, L * 16 + 16)
                dve.memset(zin[:, :, 0:LEAD], 0.0)
                dve.memset(zin[:, :, SEQ + LEAD:SEQ + 2 * LEAD], 0.0)
                stt(sp[:, 0:4], small_of("lam", 0, 4), -1.0, small_of("lam", 0, 4), ALU.mult, ALU.max).then_inc(lam_abs, 1)
                ts(sp[:, 36:40], small_of("lam", 0, 4), -1.0, 0.0, ALU.mult, ALU.max)
                dve.drain()
                copy(zin[:, 0:NT, SEQ + LEAD:SEQ + 2 * LEAD], small_of("cst", 0, 12).rearrange("p (n t) -> p n t", n=NT))
                copy(zin[:, 2 * NT:ZT, DEC0 + 2:DEC0 + 3], small_of("sst", 0, 14).rearrange("p (n t) -> p n t", n=ZR))
                norm(L * 3 + 1, "n1", xn_ready)
                dve.wait_ge(lam_exp, L + 1)
                ts(sp[:, 8:12], sp[:, 4:8], 1.0, None, ALU.add)
                dve.drain()
                ts(sp[:, 12:16], sp[:, 8:12], -1.0, None, ALU.add).then_inc(lam_u, 1)
                dve.wait_ge(lam_ln, L + 1)
                passed(dve)
                dve.drain()
                ts(sp[:, 20:24], sp[:, 12:16], 0.0, None, ALU.is_equal)
                dve.drain()
                tt(sp[:, 24:28], sp[:, 16:20], sp[:, 20:24], ALU.add)
                tt(sp[:, 28:32], sp[:, 12:16], sp[:, 20:24], ALU.add)
                dve.drain()
                dve.reciprocal(sp[:, 28:32], sp[:, 28:32])
                tt(sp[:, 24:28], sp[:, 24:28], sp[:, 4:8], ALU.mult)
                dve.drain()
                tt(sp[:, 24:28], sp[:, 24:28], sp[:, 28:32], ALU.mult)
                dve.drain()
                tt(sp[:, 24:28], sp[:, 24:28], sp[:, 36:40], ALU.add)
                dve.drain()
                ts(sp[:, 32:36], sp[:, 24:28], -8.0, None, ALU.mult).then_inc(nsp_ready, 1)
                xc = TB[0]
                dve.wait_ge(in_free, L * (IN_T + 2) + 2 + NT)
                dve.memset(xc[:, :, EW:MW], 0.0)
                for tap in range(4):
                    for n in range(NT):
                        src = zin[:, n, tap:tap + EW]
                        w = small_of("cw", tap * NT + n)
                        if tap == 0:
                            last = ts(xc[:, n, 0:EW], src, w, small_of("cb", n), ALU.mult, ALU.add)
                        else:
                            last = stt(xc[:, n, 0:EW], src, w, xc[:, n, 0:EW], ALU.mult, ALU.add)
                    if tap < 3:
                        dve.drain()
                last.then_inc(xc_ready, 1)
                dve.wait_ge(in_free, L * (IN_T + 2) + 2 + IN_T)
                zt = zin[:, 2 * NT:ZT, :]
                dve.memset(zs[:, :, EW:MW], 0.0)
                tt(zs[:, :, 0:EW], zt[:, :, LEAD - 1:LEAD - 1 + EW], zt[:, :, LEAD:LEAD + EW], ALU.subtract)
                dve.drain()
                for m in range(ZR):
                    stt(zs[:, m, 0:EW], zs[:, m, 0:EW], small_of("mu", m), zt[:, m, LEAD:LEAD + EW], ALU.mult, ALU.add)
                for w, (c0, c1) in enumerate([(SEQ, SEQ + LEAD), (ZW - LEAD, ZW)]):
                    copy(sout[:, SO["conv"][0] + 12 * w:SO["conv"][0] + 12 * w + 12].rearrange("p (n t) -> p n t", n=NT),
                         zin[:, 0:NT, c0:c1])
                    last = copy(sout[:, SO["shift"][0] + 14 * w:SO["shift"][0] + 14 * w + 14].rearrange("p (n t) -> p n t", n=ZR),
                                zt[:, :, c1 - 1:c1])
                last.then_inc(zs_ready, 1)
                dve.wait_ge(i_out, L + 1)
                tt(TB[2][:, :, :], TB[2][:, :, :], xc[:, :, :], ALU.mult)
                dve.wait_ge(a_ready, L + 1)
                tt(TB[5][:, :, :], TB[4][:, :, :], TB[4][:, :, :], ALU.mult)
                dve.drain()
                stt(TB[5][:, :, :], TB[5][:, :, :], 1.0, TB[3][:, :, :], ALU.add, ALU.mult).then_inc(m2_ready, 1)
                dve.wait_ge(mult_ready, L + 1)
                dve.memset(TB[5][:, :, 0:1], 1.0)
                dve.drain()
                tt(TB[2][:, :, :], TB[2][:, :, :], TB[5][:, :, :], ALU.mult)
                dve.drain()
                for n in range(NT):
                    nc.vector.tensor_tensor_scan(TB[6][:, n, 0:SEQ], TB[4][:, n, 0:SEQ], TB[2][:, n, 0:SEQ], 0.0, ALU.mult, ALU.add)
                    nc.vector.tensor_tensor_scan(TB[6][:, n, DEC0:EW], TB[4][:, n, DEC0:EW], TB[2][:, n, DEC0:EW],
                                                 small_of("lst", n), ALU.mult, ALU.add)
                dve.drain()
                for w, c in enumerate([SEQ - 1, EW - 1]):
                    copy(sout[:, SO["lru"][0] + 4 * w:SO["lru"][0] + 4 * w + 4].rearrange("p (n t) -> p n t", n=NT), TB[6][:, :, c:c + 1])
                dve.wait_ge(gg_ready, L + 1)
                tt(ymix[:, 0:NT, 0:SEQ], TB[6][:, :, 0:SEQ], zin[:, NT:2 * NT, LEAD:LEAD + SEQ], ALU.mult)
                tt(ymix[:, 0:NT, SEQ:T], TB[6][:, :, DEC0:EW], zin[:, NT:2 * NT, ZW - DEC:ZW], ALU.mult).then_inc(lru_done, 1)
                dve.drain()
                r_, k_, v_ = zs[:, 0:4, :], zs[:, 4:8, :], zs[:, 8:12, :]
                for n in range(NT):
                    ts(TB[2][:, n, :], k_[:, n, :], small_of("kk", n), None, ALU.mult)
                dve.drain()
                tt(TB[3][:, :, :], TB[2][:, :, :], TB[2][:, :, :], ALU.mult).then_inc(kk_sq, 1)
                ts(sp[:, 0:4], small_of("ka", 0, 4), -1.0, 1.0, ALU.mult, ALU.add)
                dve.wait_ge(dec_out, L + 1)
                ts(TB[0][:, :, :], TB[0][:, :, :], -float(np.exp(-0.5)), None, ALU.mult)
                dve.drain()
                dve.memset(TB[0][:, :, EW:MW], 0.0)
                dve.drain()
                for n in range(NT):
                    nc.vector.tensor_tensor_scan(TB[1][:, n, :], reset, TB[0][:, n, :], 0.0, ALU.mult, ALU.add)
                dve.drain()
                tt(TB[0][:, :, :], TB[1][:, :, :], TB[0][:, :, :], ALU.subtract)
                dve.wait_ge(kk_rt, L + 1)
                dve.wait_ge(icl_out, L + 1)
                ts(TB[6][:, :, :], TB[6][:, :, :], 1e-12, None, ALU.max)
                dve.drain()
                dve.reciprocal(TB[6][:, :, :], TB[6][:, :, :])
                dve.drain()
                tt(TB[2][:, :, :], TB[2][:, :, :], TB[6][:, :, :], ALU.mult)
                dve.drain()
                for n in range(NT):
                    ts(TB[6][:, n, :], TB[4][:, n, :], small_of("ka", n), sp[:, n:n + 1], ALU.mult, ALU.add)
                tt(TB[3][:, :, :], TB[2][:, :, :], TB[4][:, :, :], ALU.mult)
                dve.drain()
                tt(k_, k_, TB[6][:, :, :], ALU.mult)
                dve.drain()
                for n in range(NT):
                    last = stt(TB[6][:, n, :], r_[:, n, :], small_of("rk", n), k_[:, n, :], ALU.mult, ALU.mult)
                last.then_inc(bonus_in, 1)
                dve.memset(vc[0:HD, :, 0:C], 0.0)
                dve.memset(vc[HD:P, :, C:P], 0.0)
                dve.memset(st[:, :, :], 0.0)
                dve.wait_ge(bonus_done, L + 1)
                for n in range(NT):
                    last = tt(cut(TB[4][:, n, :], MH), halves(2 * n, MH), cut(v_[:, n, :], MH), ALU.mult)
                last.then_inc(cum_ready, 1)
                dve.wait_ge(exp_ready, L + 1)
                passed(dve)

                def chunk(c, col, end):
                    n = L * NCHUNK + c
                    for q, (b_at, k_at) in ((0, (0, C)), (HD, (C, 0))):
                        tt(bk[q:q + HD, :, b_at:b_at + C], TB[3][q:q + HD, :, col], TB[6][q:q + HD, :, col], ALU.mult)
                        tt(bk[q:q + HD, :, k_at:k_at + C], k_[q:q + HD, :, col], TB[6][q:q + HD, :, col], ALU.mult)
                    tt(ar[:, :, C:P], r_[:, :, col], TB[1][:, :, col], ALU.mult)
                    stt(ar[:, :, 0:C], TB[2][:, :, col], -1.0, TB[0][:, :, col], ALU.mult, ALU.mult).then_inc(tilde_ready, 1)
                    dve.wait_ge(pair_done, n + 1)
                    for q in (0, HD):
                        tt(amT[q:q + C], ps[q:q + C, q // HD, :].rearrange("p (m t) -> p m t", m=NT)[:, :, 0:C],
                           causal[q:q + C, 0:C].unsqueeze(1).to_broadcast([C, NT, C]), ALU.mult)
                    dve.drain()

                    def level(lv):
                        mask = cn[:, CN["level"] + lv * C:CN["level"] + (lv + 1) * C]
                        return tt(ml[lv % 2], amT, mask.unsqueeze(1).to_broadcast([P, NT, C]), ALU.mult)

                    eyes = eye.unsqueeze(1).to_broadcast([P, NT, C])
                    level(0).then_inc(m_ready, 1)
                    dve.drain()
                    tt(xt, ml[0], eyes, ALU.add)
                    level(1)
                    dve.wait_ge(y_done, n * LEVELS + 1)
                    tt(xi, ps[:, 4, 0:NT * C].rearrange("p (m t) -> p m t", m=NT), eyes, ALU.add).then_inc(m_ready, 1)
                    for b in range(2):
                        last = tt(gm[:, b:HEADS:2, :], ps[:, b, :].rearrange("p (h t) -> p h t", h=4),
                                  causal.unsqueeze(1).to_broadcast([P, 4, P]), ALU.mult)
                    last.then_inc(gm_ready, 1)
                    dve.drain()
                    for lv in range(1, LEVELS):
                        if lv + 1 < LEVELS:
                            level(lv + 1)
                        dve.wait_ge(x_done, n * (LEVELS - 1) + lv)
                        if lv + 1 < LEVELS:
                            tt(xi, ps[:, 5, 0:NT * C].rearrange("p (m t) -> p m t", m=NT), xi, ALU.add)
                        last = tt(xt, ps[:, 6, 0:NT * C].rearrange("p (m t) -> p m t", m=NT), xt, ALU.add)
                        last.then_inc(m_ready, 1)
                    dve.wait_ge(step_done, n + 1)
                    for q in (0, HD):
                        at = st[q:q + HD, :, q:q + HD]
                        tt(at, ps[q:q + HD, 5, 0:NT * HD].rearrange("p (m v) -> p m v", m=NT), at, ALU.add)
                    dve.drain()
                    for q in (0, HD):
                        at = st[q:q + HD, :, q:q + HD]
                        tt(at, at, TB[1][q:q + HD, :, end].to_broadcast([HD, NT, HD]), ALU.mult)
                    dve.drain()

                with dve.Fori(0, NCH) as c:
                    chunk(c, bass.ds(c * C, C), bass.ds(c * C + C - 1, 1))
                dve.wait_ge(wkv_in, L * 16 + 16)
                for q in (0, HD):
                    copy(stp[q:q + HD, :, :], st[q:q + HD, :, q:q + HD])
                dve.drain()
                for q in (0, HD):
                    copy(st[q:q + HD, :, q:q + HD], sts[q:q + HD, :, :])
                chunk(NCH, slice(DEC0, DEC0 + C), slice(DEC0 + C - 1, DEC0 + C))
                for q in (0, HD):
                    copy(sts[q:q + HD, :, :], st[q:q + HD, :, q:q + HD])
                dve.drain()
                dve.sem_inc(outs_ready, 1)
                dve.wait_ge(mean_done, L + 1)
                for n in range(NT):
                    stt(cut(TB[0][:, n, :], MH), halves(2 * n, MH), -1.0 / HD, cut(o[:, n, :], MH), ALU.mult, ALU.add)
                dve.drain()
                tt(TB[6][:, :, :], TB[0][:, :, :], TB[0][:, :, :], ALU.mult)
                dve.drain()
                ts(TB[6][:, :, :], TB[6][:, :, :], 1.0 / HD, None, ALU.mult).then_inc(oc_ready, 1)
                dve.wait_ge(std_out, L + 1)
                dve.reciprocal(TB[6][:, :, :], TB[6][:, :, :])
                dve.drain()
                tt(TB[0][:, :, :], TB[0][:, :, :], TB[6][:, :, :], ALU.mult)
                dve.drain()
                for n in range(NT):
                    ts(TB[0][:, n, :], TB[0][:, n, :], small_of("lnw", n), small_of("lnb", n), ALU.mult, ALU.add)
                dve.drain()
                tt(TB[0][:, :, :], TB[0][:, :, :], TB[4][:, :, :], ALU.add)
                dve.drain()
                tt(ymix[:, NT:KD, 0:SEQ], TB[0][:, :, 0:SEQ], TB[5][:, :, 0:SEQ], ALU.mult)
                tt(ymix[:, NT:KD, SEQ:T], TB[0][:, :, DEC0:EW], TB[5][:, :, DEC0:EW], ALU.mult).then_inc(y_ready, 1)
                dve.drain()
                dve.sem_inc(out_free, 2)
                with dve.Fori(0, OUT_T // 2) as g:
                    for j in range(2):
                        dve.wait_ge(tile_done, L * TILES + OUT_0 + g * 2 + j + 3)
                        add_tile(bass.ds(g * 2 + j, 1), 2 * j).then_inc(out_free, 1)
                dve.wait_ge(stored, (L + 1) * 48)
                passed(dve)
                dve.drain()
                dve.sem_inc(h_ready, 1)
                norm(L * 3 + 2, "n2", xn_ready)

                if do_peer:
                    def top16(nt, src, spare, n, width, vals, idx):
                        mx, mi, mr = nc.vector.max, nc.vector.max_index, nc.vector.match_replace
                        for q in range(n):
                            mx(vals[0:nt, q, 0:8], src(q))
                        dve.drain()
                        for q in range(n):
                            mi(idx[0:nt, q, 0:8], vals[0:nt, q, 0:8], src(q))
                            last = mr(spare[0:nt, q * width:(q + 1) * width], vals[0:nt, q, 0:8], src(q), NEG)
                        dve.drain()
                        for q in range(n):
                            mx(vals[0:nt, q, 8:16], spare[0:nt, q * width:(q + 1) * width])
                        dve.drain()
                        for q in range(n):
                            mi(idx[0:nt, q, 8:16], vals[0:nt, q, 8:16], spare[0:nt, q * width:(q + 1) * width])
                        dve.drain()

                    def route(b, nt):
                        n = L * NBLK + b
                        dve.wait_ge(sc_read, n + 1)
                        passed(dve)
                        top16(nt, lambda q: s2[0:nt, q * NK:(q + 1) * NK], s1, QH, NK, tv, ti.bitcast(U32))
                        copy(tf[0:nt], ti[0:nt].bitcast(U32))
                        tvs = tv[0:nt].rearrange("p (q w) k -> p q w k", w=2)
                        cand = s2[0:nt].rearrange("p (q a b) -> p q a b", q=PH, a=TOPK)
                        shape = [nt, PH, TOPK, TOPK]
                        tt(cand, tvs[:, :, 0, :].unsqueeze(3).to_broadcast(shape),
                           tvs[:, :, 1, :].unsqueeze(2).to_broadcast(shape), ALU.add)
                        dve.drain()
                        top16(nt, lambda q: s2[0:nt, q * 256:(q + 1) * 256], s1, PH, 256, bv, bi.bitcast(U32))
                        mxs = bv[0:nt, :, 0:1]
                        copy(gsum[0:nt], mxs)
                        dve.drain()
                        tt(bv[0:nt], bv[0:nt], gsum[0:nt].unsqueeze(2).to_broadcast([nt, PH, TOPK]), ALU.subtract).then_inc(best_ready, 1)
                        ts(ba[0:nt, 0].bitcast(U32), bi[0:nt].bitcast(U32), 4, None, ALU.logical_shift_right)
                        ts(ba[0:nt, 1].bitcast(U32), bi[0:nt].bitcast(U32), 15, None, ALU.bitwise_and)
                        dve.drain()
                        copy(bf[0:nt], ba[0:nt].bitcast(U32))
                        dve.drain()
                        eq = s2[0:nt].rearrange("p (q k j) -> p q k j", q=PH, k=TOPK)
                        eq3 = s2[0:nt].rearrange("p (q j) -> p q j", q=PH * TOPK)
                        tfs = tf[0:nt].rearrange("p (q w) k -> p q w k", w=2)
                        for w in range(2):
                            b3 = bf[0:nt, w].rearrange("p q k -> p (q k)").unsqueeze(2).to_broadcast([nt, PH * TOPK, TOPK])
                            i3 = iota[0:nt, 0:TOPK].unsqueeze(1).to_broadcast([nt, PH * TOPK, TOPK])
                            tt(eq3, b3, i3, ALU.is_equal)
                            dve.drain()
                            tt(eq, eq, tfs[:, :, w, :].unsqueeze(2).to_broadcast(shape), ALU.mult)
                            dve.drain()
                            nc.vector.tensor_reduce(sel_t[0:nt, 1 + w, :], eq3, AX.X, ALU.add)
                            dve.drain()
                        dve.wait_ge(gexp, n + 1)
                        nc.vector.tensor_reduce(gsum[0:nt], bv[0:nt], AX.X, ALU.add)
                        dve.drain()
                        dve.reciprocal(gsum[0:nt], gsum[0:nt])
                        dve.drain()
                        tt(sel_t[0:nt, 0, :].rearrange("p (q k) -> p q k", q=PH), bv[0:nt],
                           gsum[0:nt].unsqueeze(2).to_broadcast([nt, PH, TOPK]), ALU.mult).then_inc(sel_ready, 1)
                        dve.wait_ge(selT_out, n + 1)
                        passed(dve)
                        with dve.Fori(0, nt // (2 * GT)) as g:
                            for s in range(2):
                                i = L * GROUPS + b * (BLK // GT) + g * 2 + s
                                dve.wait_ge(gmat_done, i + 1)
                                for hot, w in ((oneB, 2), (oneA, 1)):
                                    number = sel[:, w, bass.ds(g * (2 * GT) + s * GT, GT)]
                                    tt(hot[:, s], iota.unsqueeze(1).to_broadcast([P, GT, P]),
                                       number.unsqueeze(2).to_broadcast([P, GT, P]), ALU.is_equal).then_inc(hot_ready, 1)

                    with dve.Fori(0, NB) as b:
                        route(b, BLK)
                    route(NB, DEC)

                    def high_v(e, half, j):
                        dve.wait_ge(v_in[j % 2], L * (8 * NK) + e * (8 * EC) + 16 * (j // 2) + 16)
                        dve.wait_ge(eo_done, (L * ESTEPS + e + 1) * KD)
                        passed(dve)
                        copy(vh[half * EC + j], vraw[j % 2]).then_inc(vh_ready, 1)

                    def weigh(e, half, j):
                        dve.drain()
                        dve.wait_ge(g_in[j], (L * ESTEPS + e + 1) * 32)
                        tt(wf[j % 2], gf[j], gs[j], ALU.mult).then_inc(w_ready, 1)

                    def low_w(e, half, j):
                        dve.wait_ge(wh_ready, L * NK + e * EC + j + 1)
                        tt(wtl[half * EC + j], wf[j % 2], wth[half * EC + j].bitcast(F32), ALU.subtract).then_inc(wl_ready, 1)

                    prepare = [[(high_v, 0), (high_v, 1)], [(weigh, 0), (weigh, 1)], [(high_v, 2), (low_w, 0)],
                               [(weigh, 2), (low_w, 1)], [(high_v, 3), (weigh, 3)], [(low_w, 2), (low_w, 3)], [], []]

                    def add(e, m):
                        dve.wait_ge(eo_done, (L * ESTEPS + e) * KD + m + 1 + 2 * KD)
                        add_tile(m, 4 + m % 2 * 2).then_inc(eo_out, 1)

                    def step(e, half):
                        for m in range(KD):
                            add(e, m)
                            for make, j in prepare[m]:
                                make(e + 1, 1 - half, j)

                    for part in prepare:
                        for make, j in part:
                            make(0, 0, j)
                    with dve.Fori(0, ESTEPS // 2 - 1) as e2:
                        step(e2 * 2, 0)
                        step(e2 * 2 + 1, 1)
                    step(ESTEPS - 2, 0)
                    for m in range(KD):
                        add(ESTEPS - 1, m)
                dve.drain()
                dve.sem_inc(h_ready, 1)
                norm(L * 3 + 3, "n3", xn_ready)
                dve.drain()
                dve.sem_inc(ple_free, 2)
                with dve.Fori(0, PLE_T // 2) as g:
                    for j in range(2):
                        dve.wait_ge(ple_sig, L * PLE_T + g * 2 + j + 1)
                        tt(cut(pg[j], HALF), halves(4 + 2 * j, HALF), cut(sg[j], HALF), ALU.mult)
                        dve.drain()
                        at = h[:, bass.ds(g * 2 + j, 1), :].rearrange("p a t -> p (a t)")
                        tt(at, at, pg[j], ALU.add).then_inc(ple_free, 1)
                if True:
                    dve.drain()
                    dve.sem_inc(layer_free, 1)
            dve.sem_inc(h_ready, 1)
            norm(3 * DEPTH + 1, "fin", y_out_ready)


def kernel(**inputs):
    import concourse.bacc as bacc
    from concourse.bass_utils import run_bass_kernel_spmd

    nc = bacc.Bacc("TRN2", target_bir_lowering=False, num_devices=1)
    arrays = lay_out(inputs)
    args = []
    for name, a in arrays.items():
        args.append(nc.dram_tensor(f"in_{name}", a.shape, mybir.dt.from_np(a.dtype), kind="ExternalInput").ap())
    for name, shape in OUTS.items():
        args.append(nc.dram_tensor(f"out_{name}", shape, F32, kind="ExternalOutput").ap())
    trunk(nc, *args)
    r = run_bass_kernel_spmd(nc, [{f"in_{n}": a for n, a in arrays.items()}], core_ids=[0]).results[0]
    return give_back({n: r[f"out_{n}"] for n in OUTS})


OUTS = {"y": (P, KD, T), "small": (DEPTH, P, NSO), "wkv": (DEPTH, 2, P, NT, HD)}


def lay_out(i):
    i = {k: np.asarray(a) for k, a in i.items()}

    def cols(a, axis=1):
        return np.swapaxes(a.reshape(DEPTH, -1, P), 1, 2)

    x = np.concatenate([i["x_prompt"][0], i["x_sample"][0]], 0).T.reshape(KD, P, T).transpose(1, 0, 2)
    p = np.concatenate([i["p_prompt"][:, 0], i["p_sample"][:, 0]], 1).transpose(0, 2, 1).reshape(DEPTH, 2, P, T).transpose(0, 2, 1, 3)
    small = np.zeros((DEPTH, P, NSM), np.float32)

    def put(name, a):
        small[:, :, SM[name]:SM[name] + a.shape[2]] = a

    put("n1", cols(i["norm1_g"]))
    put("n2", cols(i["norm2_g"]))
    put("n3", cols(i["norm3_g"]))
    put("fin", cols(np.stack([i["final_g"]] * DEPTH)))
    put("cw", cols(i["conv_w"].reshape(DEPTH, -1)))
    for name, key in [("cb", "conv_b"), ("ba", "lru_ba"), ("bx", "lru_bx"), ("lam", "lru_lambda"), ("mu", "rwkv_mu"),
                      ("w0", "rwkv_w0"), ("a0", "rwkv_a0"), ("kk", "rwkv_kk"), ("ka", "rwkv_ka"),
                      ("rk", "rwkv_rk"), ("lnw", "rwkv_ln_w"), ("lnb", "rwkv_ln_b")]:
        put(name, cols(i[key].reshape(DEPTH, -1)))
    put("cst", i["state_conv"][:, 0].reshape(DEPTH, 3, NT, P).transpose(0, 3, 2, 1).reshape(DEPTH, P, 12))
    put("lst", cols(i["state_lru"][:, 0]))
    put("sst", cols(i["state_shift"][:, 0]))
    mixw = np.stack([i["lru_wa"].transpose(0, 2, 1, 3).reshape(DEPTH, P, LW),
                     i["lru_wx"].transpose(0, 2, 1, 3).reshape(DEPTH, P, LW),
                     np.concatenate([i["rwkv_w2"], i["rwkv_a2"]], 1), i["rwkv_g2"]], 2)
    wkv0 = i["state_wkv"][:, 0].reshape(DEPTH, NT, 2, HD, HD).transpose(0, 2, 4, 1, 3).reshape(DEPTH, P, NT, HD)
    keys = i["peer_keys"].reshape(DEPTH, QH, NK, P).transpose(0, 3, 1, 2)
    ut = i["peer_u"].reshape(DEPTH, NK, NK, KD, P).transpose(0, 2, 4, 3, 1)
    wple = np.concatenate([i["ple_gate"], i["ple_w"]], 1)
    out = dict(x=x, p=p, small=small, const=constants(), mixw=mixw, wkv0=wkv0, w_in=i["w_in"], w_out=i["w_out"],
               wq=i["peer_wq"], keys=keys, ut=ut, v=i["peer_v"], wple=wple)
    return {k: np.ascontiguousarray(a) for k, a in out.items()}


def give_back(r):
    y = r["y"].transpose(2, 1, 0).reshape(T, D)
    so, wk = r["small"], r["wkv"]

    def cols(name, w):
        at, n = SO[name]
        return so[:, :, at + n * w:at + n * w + n]

    res = []
    for w in range(2):
        conv = cols("conv", w).reshape(DEPTH, P, NT, 3).transpose(0, 3, 2, 1).reshape(DEPTH, 1, 3, LW)
        lru = cols("lru", w).transpose(0, 2, 1).reshape(DEPTH, 1, LW)
        shift = cols("shift", w).transpose(0, 2, 1).reshape(DEPTH, 1, RCOLS)
        wkv = wk[:, w].reshape(DEPTH, 2, HD, NT, HD).transpose(0, 3, 1, 4, 2).reshape(DEPTH, 1, HEADS, HD, HD)
        res += [conv, lru, shift, wkv]
    return tuple(np.ascontiguousarray(a) for a in [y[None, :SEQ], y[None, SEQ:]] + res)
```

```python
from contextlib import ExitStack

import numpy as np

import concourse.bass as bass
from concourse import mybir

F32 = mybir.dt.float32
F32R = mybir.dt.float32r
U32 = mybir.dt.uint32
ALU = mybir.AluOpType
ACT = mybir.ActivationFunctionType
AX = mybir.AxisListType

P = 128
DEPTH, D, SEQ, DEC = 2, 1024, 512, 32
KD = D // P
T = SEQ + DEC
HALF = T // 2
LW = 512
NT = LW // P
RCOLS = 1792
ZT = 2 * NT + RCOLS // P
ZR = RCOLS // P
LEAD = 3
ZW = SEQ + DEC + 2 * LEAD
DEC0 = SEQ + LEAD
EW = DEC0 + DEC
MW = 580
MH = MW // 2
C = 64
NCH = SEQ // C
HEADS = 8
HD = 64
LEVELS = 6
QH = 16
NK = 128
PH = 8
TOPK = 16
EPS, GN_EPS = 1e-6, 64e-5
NEG = -3.0e38

IN_T, OUT_T, Q_T, PLE_T = ZT, KD, QH, KD
OUT_0, Q_0, PLE_0 = IN_T, IN_T + OUT_T, IN_T + OUT_T + Q_T
TILES = IN_T + OUT_T + Q_T + PLE_T
SPLIT_T = IN_T + Q_T
WK = KD + 2

SM = {}
_at = 0
for _name, _n in [("n1", 8), ("n2", 8), ("n3", 8), ("fin", 8), ("cw", 16), ("cb", 4), ("ba", 4), ("bx", 4),
                  ("lam", 4), ("mu", 14), ("w0", 4), ("a0", 4), ("kk", 4), ("ka", 4), ("rk", 4),
                  ("lnw", 4), ("lnb", 4), ("cst", 12), ("lst", 4), ("sst", 14)]:
    SM[_name] = _at
    _at += _n
NSM = _at
CN = {}
_at = 0
for _name, _n in [("ident", P), ("ones", P), ("heads", P), ("iota", P), ("causal", P), ("eye", C),
                  ("level", LEVELS * C), ("reset", MW)]:
    CN[_name] = _at
    _at += _n
NCN = _at
SO = {"conv": (0, 12), "lru": (24, 4), "shift": (32, 14)}
NSO = 60

BLK = 128
NB = SEQ // BLK
GT = 4
GROUPS = T // GT
EC = 4
ESTEPS = NK // EC
PAIRS_A, PAIRS_B = 8, 6
PAIRS_N = PAIRS_A + PAIRS_B
PAIRS_END = NK // 2 - NB * PAIRS_N
assert PAIRS_B * 4 <= BLK // GT and PAIRS_END >= 2


def constants():
    c = np.zeros((P, NCN), np.float32)
    i = np.arange(P)
    c[:, CN["ident"]:CN["ident"] + P] = np.eye(P)
    c[:, CN["ones"]:CN["ones"] + P] = 1.0
    c[:, CN["heads"]:CN["heads"] + P] = (i[:, None] // HD == i[None] // HD)
    c[:, CN["iota"]:CN["iota"] + P] = i[None]
    s, t = i[:, None] % C, np.arange(C)[None]
    c[:, CN["eye"]:CN["eye"] + C] = s == t
    c[:, CN["causal"]:CN["causal"] + C] = s < t
    c[:, CN["causal"] + C:CN["causal"] + P] = s <= t
    for k in range(LEVELS):
        b = 1 << k
        off = (s // (2 * b) == t // (2 * b)) & (s // b % 2 == 0) & (t // b % 2 == 1)
        c[:, CN["level"] + k * C:CN["level"] + (k + 1) * C] = off
    r = np.ones(MW)
    r[[k * C for k in range(NCH)] + [DEC0]] = 0.0
    c[:, CN["reset"]:CN["reset"] + MW] = r[None]
    return c


def trunk(nc, x, p, small, const, mixw, wkv0, w_in, w_out, wq, keys, ut, v, wple, y, small_out, wkv_out):
    ctx = ExitStack()
    with ctx:
        def sem(name):
            return ctx.enter_context(nc.semaphore(name))

        words = 53214
        names = []
        RESERVED = 16512
        ps = ctx.enter_context(nc.psum_tensor("ps", [P, 8, 512], F32))
        top = [0]

        def aligned(at):
            return -(-at // 8) * 8

        def take(n, at=None, kind=F32):
            if at is None:
                at = aligned(top[0])
                top[0] = at + n
            assert at + n <= words, (at, n)
            names.append(f"m{len(names)}")
            return nc.alloc_sbuf_tensor_at(names[-1], [P, n], kind, offset=RESERVED + 4 * at)[:, :]

        def split(n):
            return take(n, kind=F32R)

        h = take(KD * T).rearrange("p (k t) -> p k t", k=KD)
        xn_at = top[0]
        xn = take(KD * T).rearrange("p (k t) -> p k t", k=KD)
        w_at = top[0]
        ymix = xn
        wslot = take(2 * WK * P).rearrange("p (s k n) -> p s k n", s=2, k=WK)
        sm = take(NSM)
        cn = take(NCN)
        rms = take(T)
        sout = take(NSO)
        sp = take(40)
        epst = take(2)
        A0 = aligned(top[0])

        def const_of(name, n):
            return cn[:, CN[name]:CN[name] + n]

        def small_of(name, i, n=1):
            return sm[:, SM[name] + i:SM[name] + i + n]

        ident, ones, hones, iota = (const_of(n, P) for n in ("ident", "ones", "heads", "iota"))
        causal, reset = const_of("causal", P), const_of("reset", MW)
        eye = const_of("eye", C)

        z_at = A0
        zin = take(ZT * ZW, z_at).rearrange("p (k t) -> p k t", k=ZT)
        zs_at = aligned(z_at + ZT * ZW)
        zs = take(ZR * MW, zs_at).rearrange("p (k t) -> p k t", k=ZR)
        sq = take(KD * T, zs_at).rearrange("p (k t) -> p k t", k=KD)
        mw_at = zs_at + ZR * MW
        mw = take(4 * LW, mw_at).rearrange("p (w n) -> p w n", w=4)
        t_at = mw_at + 4 * LW
        TB = [take(NT * MW, t_at + i * NT * MW).rearrange("p (k t) -> p k t", k=NT) for i in range(7)]
        assert t_at + 7 * NT * MW <= words
        top[0] = aligned(t_at + NT * MW)
        xh1 = split(KD * T).rearrange("p (k t) -> p k t", k=KD)
        xl1 = split(KD * T).rearrange("p (k t) -> p k t", k=KD)
        wh1 = [split(KD * P).rearrange("p (k n) -> p k n", k=KD) for _ in range(2)]
        wl1 = [split(KD * P).rearrange("p (k n) -> p k n", k=KD) for _ in range(2)]
        top[0] = z_at
        class Slot:
            def __init__(self, i):
                self.i = i
                self.bank = 4 * i
                self.per = NCH // 2 + (i == 0)
                self.bk = take(NT * P).rearrange("p (m t) -> p m t", m=NT)
                self.ar = take(NT * P).rearrange("p (m t) -> p m t", m=NT)
                self.vc = take(NT * P).rearrange("p (m t) -> p m t", m=NT)
                self.gm = take(HEADS * P).rearrange("p (h t) -> p h t", h=HEADS)
                self.bkT = take(LW)
                self.sav = take(LW)
                self.amT, self.ys, self.fs, m0, m1 = (take(NT * C).rearrange("p (m t) -> p m t", m=NT) for _ in range(5))
                self.ml = [m0, m1]
                self.xx = take(2 * NT * C)
                self.xi, self.xt = (self.xx[:, w * NT * C:(w + 1) * NT * C].rearrange("p (m t) -> p m t", m=NT) for w in range(2))
                self.tilde_ready = sem(f"tilde_ready{i}")
                self.v_ready = sem(f"v_ready{i}")
                self.pair_done = sem(f"pair_done{i}")
                self.turn_done = sem(f"turn_done{i}")
                self.turn_out = sem(f"turn_out{i}")
                self.gm_ready = sem(f"gm_ready{i}")
                self.f_done, self.f_out = sem(f"f_done{i}"), sem(f"f_out{i}")
                self.m_ready = sem(f"m_ready{i}")
                self.y_done = sem(f"y_done{i}")
                self.y_out = sem(f"y_out{i}")
                self.x_done = sem(f"x_done{i}")
                self.sa_done, self.sa_out = sem(f"sa_done{i}"), sem(f"sa_out{i}")
                self.step_done = sem(f"step_done{i}")

            def psum(self, b, at=0):
                return ps[:, self.bank + b, at:at + NT * C].rearrange("p (m t) -> p m t", m=NT)

        st = take(NT * P).rearrange("p (m v) -> p m v", m=NT)
        stp = take(NT * HD).rearrange("p (m v) -> p m v", m=NT)
        sts = take(NT * HD).rearrange("p (m v) -> p m v", m=NT)
        slots = [Slot(i) for i in range(2)]
        o = zs[:, 8:12, :]
        assert top[0] <= zs_at

        top[0] = A0
        xh = split(KD * T).rearrange("p (k t) -> p k t", k=KD)
        xl = split(KD * T).rearrange("p (k t) -> p k t", k=KD)
        uraw = [take(KD * P).rearrange("p (k n) -> p k n", k=KD) for _ in range(2)]
        uh = [split(KD * P).rearrange("p (k n) -> p k n", k=KD) for _ in range(2)]
        ul = [split(KD * P).rearrange("p (k n) -> p k n", k=KD) for _ in range(2)]
        ge = [take(T) for _ in range(2)]
        s1 = take(2048)
        s2 = take(2048)
        e_top = aligned(top[0])
        stage = take(NK * BLK).rearrange("p (n t) -> p n t", n=NK)
        qT = take(QH * T, e_top).rearrange("p (q t) -> p q t", q=QH)
        sq2 = take(KD * T, e_top).rearrange("p (k t) -> p k t", k=KD)
        sel = take(3 * P).rearrange("p (w t) -> p w t", w=3)
        sel_t = take(3 * P).rearrange("p (w k) -> p w k", w=3)
        tv = take(QH * TOPK).rearrange("p (q k) -> p q k", q=QH)
        ti = take(QH * TOPK).rearrange("p (q k) -> p q k", q=QH)
        tf = take(QH * TOPK).rearrange("p (q k) -> p q k", q=QH)
        bv = take(PH * TOPK).rearrange("p (q k) -> p q k", q=PH)
        bi = take(PH * TOPK).rearrange("p (q k) -> p q k", q=PH)
        ba = take(2 * PH * TOPK).rearrange("p (w q k) -> p w q k", w=2, q=PH)
        bf = take(2 * PH * TOPK).rearrange("p (w q k) -> p w q k", w=2, q=PH)
        gsum = take(PH)
        qb = take(QH * BLK, xn_at).rearrange("p (q t) -> p q t", q=QH)
        kT = take(QH * NK, xn_at + QH * BLK).rearrange("p (q n) -> p q n", q=QH)
        oneA = take(2 * GT * P, w_at).rearrange("p (s j n) -> p s j n", s=2, j=GT)
        oneB = take(2 * GT * P, w_at + 2 * GT * P).rearrange("p (s j n) -> p s j n", s=2, j=GT)
        top[0] = A0
        vraw = [take(D) for _ in range(2)]
        vh = [split(D) for _ in range(2 * EC)]
        vl = [split(D) for _ in range(2 * EC)]
        assert top[0] <= e_top
        top[0] = e_top
        gs = [take(T) for _ in range(EC)]
        gf = [take(T) for _ in range(EC)]
        wf = [take(T) for _ in range(2)]
        wth = [split(T) for _ in range(2 * EC)]
        wtl = [split(T) for _ in range(2 * EC)]
        top[0] = A0
        pT = take(2 * T).rearrange("p (k t) -> p k t", k=2)
        sg = [take(T) for _ in range(2)]
        pg = [take(T) for _ in range(2)]
        sq3 = take(KD * T).rearrange("p (k t) -> p k t", k=KD)
        SQ = [sq, sq2, sq3]

        query_d = nc.dram_tensor("queries", [P, QH, T], F32, kind="Internal").ap()
        act_d = nc.dram_tensor("expert_inputs", [P, NK, T], F32, kind="Internal").ap()
        spare_d = nc.dram_tensor("spare", [3, P, 8], F32, kind="Internal").ap()
        gate_d = nc.dram_tensor("gate_matrix", [P, NK, T], F32, kind="Internal").ap()

        const_in = sem("const_in")
        x_in = sem("x_in")
        small_in = sem("small_in")
        mixw_in = sem("mixw_in")
        wkv_in = sem("wkv_in")
        keys_in = sem("keys_in")
        p_in = sem("p_in")
        w_in_s = [sem(f"w_slot{i}") for i in range(2)]
        layer_free = sem("layer_free")
        tile_done = sem("tile_done")
        h_ready = sem("h_ready")
        sq_ready = sem("sq_ready")
        sumsq = sem("sumsq")
        rms_ready = sem("rms_ready")
        xn_ready = sem("xn_ready")
        high_ready = sem("high_ready")
        low_ready = sem("low_ready")
        in_free = sem("in_free")
        lam_abs, lam_exp, lam_u, lam_ln = (sem(n) for n in ("lam_abs", "lam_exp", "lam_u", "lam_ln"))
        nsp_ready = sem("nsp_ready")
        xc_ready = sem("xc_ready")
        r_done, r_out, i_done, i_out = (sem(n) for n in ("r_done", "r_out", "i_done", "i_out"))
        a_ready, m2_ready, mult_ready = sem("a_ready"), sem("m2_ready"), sem("mult_ready")
        gg_ready, lru_done = sem("gg_ready"), sem("lru_done")
        zs_ready, lora_ready = sem("zs_ready"), sem("lora_ready")
        dec_done, dec_out, icl_done, icl_out, g_done, g_out = (
            sem(n) for n in ("dec_done", "dec_out", "icl_done", "icl_out", "g_done", "g_out"))
        kk_sq, kk_sum, kk_rt = sem("kk_sq"), sem("kk_sum"), sem("kk_rt")
        bonus_in, bonus_done = sem("bonus_in"), sem("bonus_done")
        cum_ready, exp_ready = sem("cum_ready"), sem("exp_ready")
        state_ready = sem("state_ready")
        o_out = sem("o_out")
        mean_done, oc_ready, var_done, std_out = (
            sem(n) for n in ("mean_done", "oc_ready", "var_done", "std_out"))
        y_ready = sem("y_ready")
        out_free = sem("out_free")
        q_free = sem("q_free")
        sc_done, sc_read = sem("sc_done"), sem("sc_read")
        best_ready, gexp = sem("best_ready"), sem("gexp")
        sel_ready, selT_done, selT_out = sem("sel_ready"), sem("selT_done"), sem("selT_out")
        hot_ready = sem("hot_ready")
        ab_ready, gmat_done, gmat_out = sem("ab_ready"), sem("gmat_done"), sem("gmat_out")
        gate_saved = sem("gate_saved")
        u_in = [sem(f"u_in{i}") for i in range(2)]
        v_in = [sem(f"v_in{i}") for i in range(2)]
        xh_ready, xl_ready = sem("xh_ready"), sem("xl_ready")
        uh_ready, ul_ready = sem("uh_ready"), sem("ul_ready")
        vh_ready, vl_ready = sem("vh_ready"), sem("vl_ready")
        wh_ready, wl_ready = sem("wh_ready"), sem("wl_ready")
        g_in = [sem(f"g_in{i}") for i in range(EC)]
        hid_done = sem("hid_done")
        ge_out = sem("ge_out")
        w_ready = sem("w_ready")
        eo_done = sem("eo_done")
        eo_out = sem("eo_out")
        q_saved = sem("q_saved")
        qb_in = sem("qb_in")
        act_saved = [sem(f"act_saved{i}") for i in range(2)]
        ple_sig = sem("ple_sig")
        ple_free = sem("ple_free")
        outs_ready = sem("outs_ready")
        stored = sem("stored")
        y_stored = sem("y_stored")
        y_out_ready = sem("y_out_ready")

        waits_passed = {e.engine: sem(f"waits_passed{i}") for i, e in enumerate([nc.sync, nc.tensor, nc.vector, nc.scalar])}

        NCHUNK = NCH + 1
        PAIRS = [(m, q) for m in range(NT) for q in (0, HD)]
        NBLK = NB + 1

        def passed(eng):
            eng.sem_inc(waits_passed[eng.engine], 1)

        def halves(bank, w):
            return ps[:, bank:bank + 2, 0:w]

        def cut(ap, w):
            return ap.rearrange("p (a w) -> p a w", a=2)

        block = ctx.enter_context(nc.Block())

        @block.sync
        def _(sp_):
            sp_.dma_start(cn, const[:, :]).then_inc(const_in, 16)
            sp_.dma_start(h, x[:, :, :]).then_inc(x_in, 16)

            def weight(L, base, n, j, src, k=KD):
                sp_.wait_ge(tile_done, L * TILES + base + n + 1)
                sp_.dma_start(wslot[:, j, 0:k, :], src).then_inc(w_in_s[j], 16)

            def split_weight(L, at, n, j, src):
                sp_.wait_ge(low_ready, L * SPLIT_T + at + n + 1)
                sp_.dma_start(wslot[:, j, 0:KD, :], src).then_inc(w_in_s[j], 16)

            with sp_.Fori(0, DEPTH) as L:
                sp_.wait_ge(layer_free, L + 1)
                sp_.dma_start(sm, small[L]).then_inc(small_in, 16)
                sp_.dma_start(mw, mixw[L]).then_inc(mixw_in, 16)
                sp_.wait_ge(tile_done, L * TILES + 2)
                passed(sp_)
                with sp_.Fori(0, IN_T // 2) as g:
                    for j in range(2):
                        split_weight(L, 0, g * 2 + j, j, w_in[L].rearrange("(k p) n -> p k n", p=P)[:, :, bass.ds((g * 2 + j) * P, P)])
                sp_.wait_ge(lru_done, L + 1)
                sp_.wait_ge(zs_ready, L + 1)
                sp_.dma_start(sts, wkv0[L]).then_inc(wkv_in, 16)
                with sp_.Fori(0, OUT_T // 2) as g:
                    for j in range(2):
                        weight(L, OUT_0, g * 2 + j, j, w_out[L].rearrange("(k p) n -> p k n", p=P)[:, :, bass.ds((g * 2 + j) * P, P)])
                sp_.wait_ge(tile_done, L * TILES + (Q_0 + 2))
                passed(sp_)
                with sp_.Fori(0, Q_T // 2) as g:
                    for j in range(2):
                        split_weight(L, IN_T, g * 2 + j, j, wq[L].rearrange("(k p) n -> p k n", p=P)[:, :, bass.ds((g * 2 + j) * P, P)])
                sp_.wait_ge(xn_ready, (L * 3 + 2) * KD)

                def load_u(m, j):
                    sp_.wait_ge(ul_ready, L * NK + m * 2 + j + 1)
                    sp_.dma_start(uraw[j], ut[L, bass.ds(m * 2 + j, 1)].rearrange("a p k n -> (a p) k n")).then_inc(u_in[j], 16)

                def load_qb(b, nt, col):
                    sp_.wait_ge(sc_done, L * NBLK + b + 1)
                    sp_.dma_start(qb[:, :, 0:nt], query_d[:, :, col]).then_inc(qb_in, 16)

                load_u(0, 0)
                load_u(0, 1)
                sp_.wait_ge(xl_ready, L * (2 * KD) + 2 * KD)
                passed(sp_)
                sp_.wait_ge(tile_done, L * TILES + (Q_0 + Q_T + 2))
                sp_.dma_start(kT, keys[L]).then_inc(keys_in, 16)
                sp_.wait_ge(q_saved, L * 16 + 16)
                passed(sp_)
                with sp_.Fori(0, NB) as b:
                    load_qb(b, BLK, bass.ds(b * BLK, BLK))
                    with sp_.Fori(0, PAIRS_N) as g:
                        for j in range(2):
                            load_u(b * PAIRS_N + g + 1, j)
                load_qb(NB, DEC, slice(SEQ, T))
                with sp_.Fori(0, PAIRS_END - 1) as g:
                    for j in range(2):
                        load_u(g + (NB * PAIRS_N + 1), j)
                sp_.wait_ge(sel_ready, (L + 1) * NBLK)
                sp_.wait_ge(hid_done, (L + 1) * NK + 2)
                for j in range(2):
                    sp_.wait_ge(act_saved[j], L * (8 * NK) + (8 * NK + 16))
                passed(sp_)

                def load_v(e, j):
                    sp_.wait_ge(vl_ready, L * NK + e * EC + j + 1)
                    sp_.dma_start(vraw[j % 2], v[L].rearrange("(p n) d -> p n d", n=NK)[:, bass.ds(e * EC + j, 1), :].rearrange("p a d -> p (a d)")).then_inc(v_in[j % 2], 16)

                with sp_.Fori(0, ESTEPS) as e:
                    load_v(e, 0)
                    load_v(e, 1)
                    sp_.wait_ge(gate_saved, L * (16 * NBLK) + (16 * NBLK + 16))
                    for j in range(EC):
                        if j > 1:
                            load_v(e, j)
                        sp_.wait_ge(w_ready, L * NK + e * EC + j + 1)
                        for dst, src in ((gs[j], gate_d), (gf[j], act_d)):
                            sp_.dma_start(dst, src[:, bass.ds(e * EC + j, 1), :].rearrange("p a t -> p (a t)")).then_inc(g_in[j], 16)
                sp_.wait_ge(h_ready, L * 3 + 3)
                sp_.dma_start(pT, p[L]).then_inc(p_in, 16)
                with sp_.Fori(0, PLE_T // 2) as g:
                    for j in range(2):
                        weight(L, PLE_0, g * 2 + j, j, wple[L].rearrange("(k p) n -> p k n", p=P)[:, :, bass.ds((g * 2 + j) * P, P)], WK)
            sp_.wait_ge(y_out_ready, KD)
            sp_.dma_start(y[:, :, :], xn).then_inc(y_stored, 16)
            sp_.wait_ge(y_stored, 16)
            sp_.wait_ge(stored, 16 * 3 * DEPTH)

        @block.gpsimd
        def _(pool):
            tt = nc.gpsimd.tensor_tensor
            pool.sem_inc(ul_ready, 2)
            pool.sem_inc(vl_ready, 2)
            pool.sem_inc(low_ready, 2)

            def low_norm(L, i, dst, high):
                for k in range(KD):
                    pool.wait_ge(xh_ready, L * (2 * KD) + (i * KD + k + 1))
                    tt(dst[:, k, :], xn[:, k, :], high[:, k, :].bitcast(F32), ALU.subtract).then_inc(xl_ready, 1)

            def low_weight(L, at, n, j, dst, high):
                pool.wait_ge(high_ready, L * SPLIT_T + at + n + 1)
                tt(dst[j], wslot[:, j, 0:KD, :], high[j].bitcast(F32), ALU.subtract).then_inc(low_ready, 1)

            def low_weights(L, at, count, dst, high):
                with pool.Fori(0, count // 2) as g:
                    for j in range(2):
                        low_weight(L, at, g * 2 + j, j, dst, high)

            with pool.Fori(0, DEPTH) as L:
                low_norm(L, 0, xl1, xh1)
                low_weights(L, 0, IN_T, wl1, wh1)
                pool.wait_ge(outs_ready, L + 1)
                pool.dma_start(small_out[L], sout).then_inc(stored, 16)
                pool.dma_start(wkv_out[L, 0], stp).then_inc(stored, 16)
                pool.dma_start(wkv_out[L, 1], sts).then_inc(stored, 16)
                low_norm(L, 1, xl, xh)
                low_weights(L, IN_T, Q_T, ul, uh)

                def low_u(m, j):
                    pool.wait_ge(uh_ready, L * NK + m * 2 + j + 1)
                    tt(ul[j], uraw[j], uh[j].bitcast(F32), ALU.subtract).then_inc(ul_ready, 1)

                def weigh(b, g, k):
                    pool.wait_ge(hot_ready, (L * GROUPS + b * (BLK // GT) + g * 4 + k) * 2 + 1)
                    gate = sel[:, 0, bass.ds(g * (4 * GT) + k * GT, GT)]
                    tt(oneB[:, k % 2], oneB[:, k % 2], gate.unsqueeze(2).to_broadcast([P, GT, P]), ALU.mult).then_inc(ab_ready, 1)

                low_u(0, 0)
                low_u(0, 1)
                with pool.Fori(0, NB) as b:
                    with pool.Fori(0, PAIRS_A) as g:
                        for j in range(2):
                            low_u(b * PAIRS_N + g + 1, j)
                    with pool.Fori(0, PAIRS_B) as g:
                        for j in range(2):
                            weigh(b, g, 2 * j)
                            weigh(b, g, 2 * j + 1)
                            low_u(b * PAIRS_N + g + (PAIRS_A + 1), j)
                    with pool.Fori(0, BLK // (4 * GT) - PAIRS_B) as g:
                        for k in range(4):
                            weigh(b, g + PAIRS_B, k)
                with pool.Fori(0, PAIRS_END - 1) as g:
                    for j in range(2):
                        low_u(g + (NB * PAIRS_N + 1), j)
                with pool.Fori(0, DEC // (4 * GT)) as g:
                    for k in range(4):
                        weigh(NB, g, k)
                with pool.Fori(0, ESTEPS // 2) as e2:
                    for half in range(2):
                        for j in range(EC):
                            pool.wait_ge(vh_ready, L * NK + e2 * (2 * EC) + (half * EC + j + 1))
                            tt(vl[half * EC + j], vraw[j % 2], vh[half * EC + j].bitcast(F32), ALU.subtract).then_inc(vl_ready, 1)

        @block.tensor
        def _(pe):
            mm = nc.tensor.matmul
            pe.sem_inc(tile_done, 2)
            pe.sem_inc(hid_done, 2)
            pe.sem_inc(gmat_done, 2)
            pe.sem_inc(eo_done, 2 * KD)
            pe.sem_inc(sc_done, 1)
            pe.wait_ge(const_in, 16)

            def norm(L, i):
                for k in range(KD):
                    pe.wait_ge(sq_ready, (L * 3 + i) * KD + k + 1)
                    for a in range(2):
                        last = mm(ps[:, a, 0:HALF], ones, SQ[i][:, k, a * HALF:(a + 1) * HALF],
                                  start=(k == 0), stop=(k == KD - 1))
                last.then_inc(sumsq, 1)

            def tile(j, slot, rhs, ks, bank, inc):
                for a in range(2):
                    for n, k in enumerate(ks):
                        last = mm(ps[:, bank + a, 0:HALF], wslot[:, slot, k, :], rhs[:, n, a * HALF:(a + 1) * HALF],
                                  start=(n == 0), stop=(n == len(ks) - 1))
                if inc:
                    last.then_inc(tile_done, 1)

            def linear(L, base, count, rhs, free):
                passed(pe)
                with pe.Fori(0, count // 2) as g:
                    for j in range(2):
                        pe.wait_ge(w_in_s[j], L * (16 * TILES // 2) + g * 16 + 16 * (base // 2) + 16)
                        pe.wait_ge(free, L * (count + 2) + g * 2 + j + 1)
                        tile(j, j, rhs, range(KD), 2 * j, True)

            def split_linear(L, base, at, i, count, high, low, xh, xl, free):
                with pe.Fori(0, count // 2) as g:
                    for j in range(2):
                        pe.wait_ge(low_ready, L * SPLIT_T + at + g * 2 + j + 1 + 2)
                        pe.wait_ge(free, L * (count + 2) + g * 2 + j + 1)
                        passed(pe)
                        for w, (lhs, rhs) in enumerate([(high, xh), (low, xh), (high, xl)]):
                            if w == 2:
                                pe.wait_ge(xl_ready, L * (2 * KD) + (i + 1) * KD)
                                passed(pe)
                            for a in range(2):
                                for k in range(KD):
                                    last = mm(ps[:, 2 * j + a, 0:HALF], lhs[j][:, k, :], rhs[:, k, a * HALF:(a + 1) * HALF],
                                              start=(k + w == 0), stop=(k == KD - 1 and w == 2))
                        last.then_inc(tile_done, 1)

            def wide(lhs, rhs, n0=0):
                for n in range(NT):
                    for a in range(2):
                        last = mm(ps[:, 2 * n + a, 0:MH], lhs(n), rhs(n)[:, a * MH:(a + 1) * MH],
                                  start=True, stop=True)
                return last

            with pe.Fori(0, DEPTH) as L:
                norm(L, 0)
                pe.wait_ge(xh_ready, L * (2 * KD) + KD)
                passed(pe)
                split_linear(L, 0, 0, 0, IN_T, wh1, wl1, xh1, xl1, in_free)
                pe.wait_ge(in_free, L * (IN_T + 2) + IN_T + 2)
                pe.wait_ge(mixw_in, L * 16 + 16)
                pe.wait_ge(xc_ready, L + 1)
                wide(lambda n: mw[:, 0, n * P:(n + 1) * P], lambda n: TB[0][:, n, :]).then_inc(r_done, 1)
                pe.wait_ge(r_out, L + 1)
                wide(lambda n: mw[:, 1, n * P:(n + 1) * P], lambda n: TB[0][:, n, :]).then_inc(i_done, 1)
                pe.wait_ge(i_out, L + 1)
                pe.wait_ge(lora_ready, L + 1)
                wide(lambda n: mw[0:64, 2, n * P:(n + 1) * P], lambda n: zs[0:64, 12, :]).then_inc(dec_done, 1)
                pe.wait_ge(dec_out, L + 1)
                wide(lambda n: mw[64:128, 2, n * P:(n + 1) * P], lambda n: zs[64:128, 12, :]).then_inc(icl_done, 1)
                pe.wait_ge(icl_out, L + 1)
                wide(lambda n: mw[:, 3, n * P:(n + 1) * P], lambda n: zs[:, 13, :]).then_inc(g_done, 1)
                pe.wait_ge(g_out, L + 1)
                pe.wait_ge(kk_sq, L + 1)
                wide(lambda n: hones, lambda n: TB[3][:, n, :]).then_inc(kk_sum, 1)
                pe.wait_ge(kk_rt, L + 1)
                pe.wait_ge(bonus_in, L + 1)
                wide(lambda n: hones, lambda n: TB[6][:, n, :]).then_inc(bonus_done, 1)
                pe.wait_ge(cum_ready, L + 1)

                def products(s, k):
                    n = L * s.per + k
                    pe.wait_ge(s.tilde_ready, n + 1)
                    pe.wait_ge(s.v_ready, n + 1)
                    passed(pe)
                    for m, q in PAIRS:
                        last = mm(ps[:, s.bank + q // HD, m * P:(m + 1) * P], s.bk[q:q + HD, m, :], s.ar[q:q + HD, m, :],
                                  start=True, stop=True)
                    last.then_inc(s.pair_done, 1)
                    for m in range(NT):
                        nc.tensor.transpose(ps[:, s.bank + 2, m * P:(m + 1) * P], s.bk[:, m, :], ident)
                    for m in range(NT):
                        last = nc.tensor.transpose(ps[:, s.bank + 3, m * P:(m + 1) * P], s.vc[:, m, :], ident)
                    last.then_inc(s.turn_done, 1)

                def level_y(s, k, lv):
                    n = L * s.per + k
                    if lv == 0:
                        pe.wait_ge(s.turn_out, n + 1)
                    pe.wait_ge(s.m_ready, n * (LEVELS + 1) + lv + 1)
                    passed(pe)
                    for m, q in PAIRS:
                        last = mm(s.psum(2)[q:q + C, m, :], s.ml[lv % 2][q:q + C, m, :],
                                  eye[q:q + C] if lv == 0 else s.xi[q:q + C, m, :], start=True, stop=True)
                    last.then_inc(s.y_done, 1)

                def level_x(s, k, lv):
                    pe.wait_ge(s.y_out, (L * s.per + k) * (LEVELS - 1) + lv)
                    passed(pe)
                    for m, q in PAIRS:
                        last = mm(s.psum(3, NT * C)[q:q + C, m, :], s.ys[q:q + C, m, :], s.xt[q:q + C, m, :],
                                  start=True, stop=True)
                    if lv < LEVELS - 1:
                        for m, q in PAIRS:
                            last = mm(s.psum(3)[q:q + C, m, :], s.xt[q:q + C, m, :], s.ys[q:q + C, m, :],
                                      start=True, stop=True)
                    last.then_inc(s.x_done, 1)

                def right_side(s, k):
                    pe.wait_ge(s.gm_ready, L * s.per + k + 1)
                    if s.i == 1:
                        pe.wait_ge(state_ready, L * s.per + k + 1)
                    passed(pe)
                    for m, q in PAIRS:
                        hd = 2 * m + q // HD
                        mm(s.psum(0)[q:q + C, m, :], s.ar[:, m, 0:C], st[:, m, q:q + HD], start=True, stop=False)
                        last = mm(s.psum(0)[q:q + C, m, :], s.gm[:, hd, 0:C], s.sav[:, hd * HD:(hd + 1) * HD],
                                  start=False, stop=True)
                    last.then_inc(s.f_done, 1)

                def finish(s, k):
                    n = L * s.per + k
                    pe.wait_ge(s.m_ready, (n + 1) * (LEVELS + 1))
                    pe.wait_ge(s.f_out, n + 1)
                    passed(pe)
                    for m, q in PAIRS:
                        last = mm(s.psum(2)[q:q + C, m, :], s.xt[q:q + C, m, :], s.fs[q:q + C, m, :], start=True, stop=True)
                    last.then_inc(s.sa_done, 1)
                    pe.wait_ge(s.sa_out, n + 1)
                    passed(pe)
                    for m, q in PAIRS:
                        hd = 2 * m + q // HD
                        mm(s.psum(1)[q:q + HD, m, :], s.bkT[:, hd * HD:(hd + 1) * HD], s.sav[:, hd * HD:(hd + 1) * HD],
                           start=True, stop=True)
                    for m in range(NT):
                        mm(s.psum(0)[:, m, :], st[:, m, :], s.ar[:, m, C:P], start=True, stop=False)
                        for hd in (2 * m, 2 * m + 1):
                            q = hd % 2 * HD
                            last = mm(s.psum(0)[q:q + HD, m, :], s.sav[:, hd * HD:(hd + 1) * HD], s.gm[:, hd, C:P],
                                      start=False, stop=True)
                    last.then_inc(s.step_done, 1)

                def chunks(k, work):
                    for s in work:
                        products(s, k)
                    for lv in range(LEVELS):
                        for s in work:
                            level_y(s, k, lv)
                        if lv > 0:
                            for s in work:
                                level_x(s, k, lv)
                        if lv == 1:
                            right_side(slots[0], k)
                    for s in work:
                        if s.i == 1:
                            right_side(s, k)
                        finish(s, k)

                passed(pe)
                with pe.Fori(0, NCH // 2) as k:
                    chunks(k, slots)
                chunks(NCH // 2, slots[:1])
                pe.wait_ge(o_out, (L + 1) * NCHUNK)
                pe.wait_ge(outs_ready, L + 1)
                wide(lambda n: hones, lambda n: o[:, n, :]).then_inc(mean_done, 1)
                pe.wait_ge(oc_ready, L + 1)
                wide(lambda n: hones, lambda n: TB[6][:, n, :]).then_inc(var_done, 1)
                pe.wait_ge(y_ready, L + 1)
                linear(L, OUT_0, OUT_T, ymix, out_free)
                norm(L, 1)
                pe.wait_ge(xh_ready, L * (2 * KD) + 2 * KD)
                passed(pe)
                split_linear(L, Q_0, IN_T, 1, Q_T, uh, ul, xh, xl, q_free)
                pe.wait_ge(q_free, L * (Q_T + 2) + Q_T + 2)
                pe.wait_ge(keys_in, L * 16 + 16)

                def hidden(m, j):
                    i = L * NK + m * 2 + j
                    pe.wait_ge(ul_ready, i + 1 + 2)
                    pe.wait_ge(ge_out, i + 1)
                    for a in range(2):
                        for k in range(KD):
                            for w, (lhs, rhs) in enumerate([(uh, xh), (uh, xl), (ul, xh)]):
                                last = mm(ps[:, j * 2 + a, 0:HALF], lhs[j][:, k, :], rhs[:, k, a * HALF:(a + 1) * HALF],
                                          start=(k + w == 0), stop=(k == KD - 1 and w == 2))
                    last.then_inc(hid_done, 1)

                def scores(b, nt):
                    n = L * NBLK + b
                    pe.wait_ge(qb_in, n * 16 + 16)
                    pe.wait_ge(ge_out, L * NK + b * (2 * PAIRS_N) + 2)
                    passed(pe)
                    for q in range(QH):
                        last = mm(ps[0:nt, q // 4, q % 4 * P:(q % 4 + 1) * P], qb[:, q, 0:nt], kT[:, q, :],
                                  start=True, stop=True)
                    last.then_inc(sc_done, 1)
                    pe.wait_ge(sc_read, n + 1)
                    passed(pe)

                def turn(b, nt):
                    n = L * NBLK + b
                    pe.wait_ge(sel_ready, n + 1)
                    passed(pe)
                    for w in range(3):
                        last = nc.tensor.transpose(ps[:, 4, w * nt:(w + 1) * nt], sel_t[0:nt, w, :], ident[0:nt, 0:nt])
                    last.then_inc(selT_done, 1)

                def gates(b, g, k):
                    i = L * GROUPS + b * (BLK // GT) + g * 4 + k
                    pe.wait_ge(hot_ready, i * 2 + 2)
                    pe.wait_ge(ab_ready, i + 1)
                    pe.wait_ge(gmat_out, i + 1)
                    for j in range(GT):
                        last = mm(ps[:, 5 + k % 2, j * P:(j + 1) * P], oneA[:, k % 2, j, :], oneB[:, k % 2, j, :],
                                  start=True, stop=True)
                    last.then_inc(gmat_done, 1)

                passed(pe)
                with pe.Fori(0, NB) as b:
                    scores(b, BLK)
                    with pe.Fori(0, PAIRS_A) as g:
                        for j in range(2):
                            hidden(b * PAIRS_N + g, j)
                    turn(b, BLK)
                    with pe.Fori(0, PAIRS_B) as g:
                        for j in range(2):
                            hidden(b * PAIRS_N + g + PAIRS_A, j)
                            gates(b, g, 2 * j)
                            gates(b, g, 2 * j + 1)
                    with pe.Fori(0, BLK // (4 * GT) - PAIRS_B) as g:
                        for k in range(4):
                            gates(b, g + PAIRS_B, k)
                scores(NB, DEC)
                with pe.Fori(0, PAIRS_END) as g:
                    for j in range(2):
                        hidden(g + NB * PAIRS_N, j)
                turn(NB, DEC)
                with pe.Fori(0, DEC // (4 * GT)) as g:
                    for k in range(4):
                        gates(NB, g, k)
                pe.wait_ge(gmat_out, (L + 1) * GROUPS + 2)
                passed(pe)
                with pe.Fori(0, ESTEPS // 2) as e2:
                    for half in range(2):
                        for m in range(KD):
                            pe.wait_ge(eo_out, (L * ESTEPS + e2 * 2 + half) * KD + m + 1)
                            for j in range(EC):
                                at = half * EC + j
                                if m == 0:
                                    pe.wait_ge(vl_ready, L * NK + e2 * (2 * EC) + (at + 1 + 2))
                                    pe.wait_ge(wl_ready, L * NK + e2 * (2 * EC) + (at + 1))
                                for a in range(2):
                                    for w, (lhs, rhs) in enumerate([(vh, wth), (vh, wtl), (vl, wth)]):
                                        last = mm(ps[:, 4 + m % 2 * 2 + a, 0:HALF], lhs[at][:, m * P:(m + 1) * P],
                                                  rhs[at][:, a * HALF:(a + 1) * HALF], start=(j + w == 0), stop=(j == EC - 1 and w == 2))
                            last.then_inc(eo_done, 1)
                norm(L, 2)
                pe.wait_ge(xn_ready, (L * 3 + 3) * KD)
                pe.wait_ge(p_in, L * 16 + 16)
                passed(pe)
                with pe.Fori(0, PLE_T // 2) as g:
                    for j in range(2):
                        pe.wait_ge(w_in_s[j], L * (16 * TILES // 2) + g * 16 + 16 * (PLE_0 // 2) + 16)
                        pe.wait_ge(ple_free, L * (PLE_T + 2) + g * 2 + j + 1)
                        tile(j, j, xn, range(KD), 2 * j, False)
                        tile(j, j, pT, [KD, KD + 1], 4 + 2 * j, True)
            for k in range(KD):
                pe.wait_ge(sq_ready, 3 * DEPTH * KD + k + 1)
                for a in range(2):
                    last = mm(ps[:, a, 0:HALF], ones, SQ[2][:, k, a * HALF:(a + 1) * HALF],
                              start=(k == 0), stop=(k == KD - 1))
            last.then_inc(sumsq, 1)

        @block.scalar
        def _(act):
            av = nc.scalar.activation
            act.sem_inc(gmat_out, 2)
            act.sem_inc(ge_out, 2)
            act.wait_ge(const_in, 16)
            act.wait_ge(x_in, 16)
            for i, s in enumerate([*act_saved, gate_saved]):
                act.dma_start(spare_d[i], cn[:, 0:8]).then_inc(s, 16)

            def norm(n, i):
                act.wait_ge(h_ready, n)
                for k in range(KD):
                    av(SQ[i][:, k, :], h[:, k, :], ACT.Square).then_inc(sq_ready, 1)
                act.wait_ge(sumsq, n)
                av(cut(rms, HALF), halves(0, HALF), ACT.Sqrt, bias=epst[:, 0:1], scale=1.0 / D).then_inc(rms_ready, 1)

            def wide(dst, func, bias=None, scale=1.0):
                for n in range(NT):
                    last = av(cut(dst[:, n, :], MH), halves(2 * n, MH), func,
                              scale=scale, **({"bias": bias(n)} if bias else {}))
                return last

            def high_norm(L, i, number, dst):
                for k in range(KD):
                    act.wait_ge(xn_ready, (L * 3 + number) * KD + k + 1)
                    av(dst[:, k, :], xn[:, k, :], ACT.Copy).then_inc(xh_ready, 1)

            def high_weight(L, base, n, j, dst):
                act.wait_ge(w_in_s[j], L * (16 * TILES // 2) + (16 * (base // 2) + 16) + n * 16)
                act.wait_ge(tile_done, L * TILES + base + n * 2 + j + 1)
                av(dst[j], wslot[:, j, 0:KD, :], ACT.Copy).then_inc(high_ready, 1)

            def done(L, base, n):
                act.wait_ge(tile_done, L * TILES + base + n + 3)

            with act.Fori(0, DEPTH) as L:
                norm(L * 3 + 1, 0)
                act.drain()
                act.sem_inc(in_free, 2)
                high_norm(L, 0, 0, xh1)
                for j in range(2):
                    high_weight(L, 0, 0, j, wh1)

                act.wait_ge(lam_abs, L + 1)
                av(sp[:, 4:8], sp[:, 0:4], ACT.Exp, scale=-1.0).then_inc(lam_exp, 1)
                act.wait_ge(lam_u, L + 1)
                av(sp[:, 16:20], sp[:, 8:12], ACT.Ln).then_inc(lam_ln, 1)

                def projected(g, j):
                    done(L, 0, g * 2 + j)
                    at = zin[:, bass.ds(g * 2 + j, 1), :].rearrange("p a t -> p (a t)")
                    av(at[:, LEAD:LEAD + HALF], ps[:, 2 * j, 0:HALF], ACT.Copy)
                    av(at[:, LEAD + HALF:LEAD + SEQ], ps[:, 2 * j + 1, 0:SEQ - HALF], ACT.Copy)
                    av(at[:, ZW - DEC:ZW], ps[:, 2 * j + 1, SEQ - HALF:HALF], ACT.Copy).then_inc(in_free, 1)

                with act.Fori(0, IN_T // 2 - 1) as g:
                    for j in range(2):
                        projected(g, j)
                        high_weight(L, 0, g + 1, j, wh1)
                for j in range(2):
                    projected(IN_T // 2 - 1, j)
                act.wait_ge(r_done, L + 1)
                wide(TB[1], ACT.Sigmoid, lambda n: small_of("ba", n)).then_inc(r_out, 1)
                act.wait_ge(i_done, L + 1)
                wide(TB[2], ACT.Sigmoid, lambda n: small_of("bx", n)).then_inc(i_out, 1)
                act.wait_ge(nsp_ready, L + 1)
                passed(act)
                act.drain()
                for n in range(NT):
                    av(TB[3][:, n, :], TB[1][:, n, :], ACT.Tanh, scale=sp[:, 32 + n:33 + n])
                for n in range(NT):
                    last = av(TB[4][:, n, :], TB[1][:, n, :], ACT.Exp, scale=sp[:, 32 + n:33 + n])
                last.then_inc(a_ready, 1)
                for n in range(NT):
                    last = av(zin[:, NT + n, LEAD:ZW], zin[:, NT + n, LEAD:ZW], ACT.Gelu_apprx_tanh)
                last.then_inc(gg_ready, 1)
                act.wait_ge(m2_ready, L + 1)
                av(TB[5][:, :, :], TB[5][:, :, :], ACT.Sqrt, scale=-1.0).then_inc(mult_ready, 1)
                act.wait_ge(zs_ready, L + 1)
                av(zs[0:64, 12, :], zs[0:64, 12, :], ACT.Tanh)
                av(zs[:, 13, :], zs[:, 13, :], ACT.Sigmoid).then_inc(lora_ready, 1)
                act.wait_ge(lru_done, L + 1)
                act.wait_ge(dec_done, L + 1)
                wide(TB[0], ACT.Sigmoid, lambda n: small_of("w0", n)).then_inc(dec_out, 1)
                act.wait_ge(icl_done, L + 1)
                wide(TB[4], ACT.Sigmoid, lambda n: small_of("a0", n)).then_inc(icl_out, 1)
                act.wait_ge(g_done, L + 1)
                wide(TB[5], ACT.Copy).then_inc(g_out, 1)
                act.wait_ge(kk_sum, L + 1)
                wide(TB[6], ACT.Sqrt).then_inc(kk_rt, 1)
                act.wait_ge(cum_ready, L + 1)
                av(TB[0][:, :, :], TB[0][:, :, :], ACT.Exp)
                av(TB[6][:, :, :], TB[1][:, :, :], ACT.Exp, scale=-1.0)
                act.drain()
                av(TB[1][:, :, :], TB[1][:, :, :], ACT.Exp).then_inc(exp_ready, 1)

                def values(s, col):
                    av(s.vc[0:HD, :, C:P], zs[0:HD, 8:12, col], ACT.Copy)
                    av(s.vc[HD:P, :, 0:C], zs[HD:P, 8:12, col], ACT.Copy).then_inc(s.v_ready, 1)

                def turned(s, k):
                    act.wait_ge(s.turn_done, L * s.per + k + 1)
                    av(s.bkT, ps[:, s.bank + 2, :], ACT.Copy)
                    av(s.sav, ps[:, s.bank + 3, :], ACT.Copy).then_inc(s.turn_out, 1)

                def level(s, k, lv):
                    act.wait_ge(s.y_done, (L * s.per + k) * LEVELS + lv + 1)
                    av(s.ys, s.psum(2), ACT.Copy).then_inc(s.y_out, 1)

                def right_side(s, k):
                    act.wait_ge(s.f_done, L * s.per + k + 1)
                    av(s.fs, s.psum(0), ACT.Copy).then_inc(s.f_out, 1)

                def finish(s, k, col):
                    n = L * s.per + k
                    act.wait_ge(s.sa_done, n + 1)
                    for q in (0, HD):
                        last = av(s.sav[q:q + C, :].rearrange("p (m w v) -> p m w v", m=NT, w=2)[:, :, q // HD, :],
                                  s.psum(2)[q:q + C], ACT.Copy)
                    last.then_inc(s.sa_out, 1)
                    act.wait_ge(s.step_done, n + 1)
                    passed(act)
                    av(o[:, :, col], s.psum(0), ACT.Copy).then_inc(o_out, 1)

                def chunks(k, work, col):
                    for s in work:
                        values(s, col(s))
                    for s in work:
                        turned(s, k)
                    for lv in range(1, LEVELS):
                        for s in work:
                            level(s, k, lv)
                        if lv == 1:
                            right_side(slots[0], k)
                    for s in work:
                        if s.i == 1:
                            right_side(s, k)
                        finish(s, k, col(s))

                with act.Fori(0, NCH // 2) as k:
                    chunks(k, slots, lambda s: bass.ds(k * (2 * C) + s.i * C, C))
                chunks(NCH // 2, slots[:1], lambda s: slice(DEC0, DEC0 + C))
                act.wait_ge(var_done, L + 1)
                wide(TB[6], ACT.Sqrt, lambda n: epst[:, 1:2], scale=1.0 / HD).then_inc(std_out, 1)
                norm(L * 3 + 2, 1)
                act.drain()
                act.sem_inc(q_free, 2)
                high_norm(L, 1, 1, xh)
                for j in range(2):
                    high_weight(L, Q_0, 0, j, uh)

                def query(g, j):
                    done(L, Q_0, g * 2 + j)
                    at = qT[:, bass.ds(g * 2 + j, 1), :].rearrange("p a t -> p (a t)")
                    av(cut(at, HALF), halves(2 * j, HALF), ACT.Copy).then_inc(q_free, 1)

                with act.Fori(0, Q_T // 2 - 1) as g:
                    for j in range(2):
                        query(g, j)
                        high_weight(L, Q_0, g + 1, j, uh)
                for j in range(2):
                    query(Q_T // 2 - 1, j)
                act.wait_ge(q_free, L * (Q_T + 2) + (Q_T + 2))
                act.dma_start(query_d[:, :, :], qT).then_inc(q_saved, 16)

                def high_u(m, j):
                    act.wait_ge(u_in[j], L * (8 * NK) + m * 16 + 16)
                    act.wait_ge(hid_done, L * NK + m * 2 + j + 1)
                    av(uh[j], uraw[j], ACT.Copy).then_inc(uh_ready, 1)

                def gelu(m, j, ahead=True):
                    i = L * NK + m * 2 + j
                    act.wait_ge(hid_done, i + 1 + 2)
                    act.wait_ge(act_saved[j], L * (8 * NK) + m * 16 + 16)
                    av(cut(ge[j], HALF), halves(j * 2, HALF), ACT.Gelu_apprx_tanh).then_inc(ge_out, 1)
                    if ahead:
                        high_u(m + 1, j)
                    act.wait_ge(ge_out, i + 1 + 2)
                    act.dma_start(act_d[:, bass.ds(m * 2 + j, 1), :].rearrange("p a t -> p (a t)"), ge[j]).then_inc(act_saved[j], 16)

                def scores(b, nt):
                    act.wait_ge(sc_done, L * NBLK + b + 2)
                    av(s2[0:nt].rearrange("p (a n) -> p a n", a=4), ps[0:nt, 0:4, :], ACT.Copy).then_inc(sc_read, 1)

                def soften(b, nt):
                    act.wait_ge(best_ready, L * NBLK + b + 1)
                    av(bv[0:nt], bv[0:nt], ACT.Exp).then_inc(gexp, 1)

                def turned(b, nt):
                    n = L * NBLK + b
                    act.wait_ge(selT_done, n + 1)
                    av(sel[:, :, 0:nt], ps[:, 4, 0:3 * nt].rearrange("p (w t) -> p w t", w=3), ACT.Copy).then_inc(selT_out, 1)
                    act.wait_ge(q_saved, L * 16 + 16)
                    act.wait_ge(gate_saved, n * 16 + 16)

                def gates(b, g, k):
                    act.wait_ge(gmat_done, L * GROUPS + b * (BLK // GT) + g * 4 + k + 3)
                    av(stage[:, :, bass.ds(g * (4 * GT) + k * GT, GT)],
                       ps[:, 5 + k % 2, :].rearrange("p (j n) -> p n j", j=GT), ACT.Copy).then_inc(gmat_out, 1)

                def save(b, nt, col):
                    act.wait_ge(gmat_out, L * GROUPS + b * (BLK // GT) + nt // GT + 2)
                    act.dma_start(gate_d[:, :, col], stage[:, :, 0:nt]).then_inc(gate_saved, 16)

                high_u(0, 0)
                high_u(0, 1)
                with act.Fori(0, NB) as b:
                    scores(b, BLK)
                    with act.Fori(0, PAIRS_A - 2) as g:
                        for j in range(2):
                            gelu(b * PAIRS_N + g, j)
                    soften(b, BLK)
                    with act.Fori(0, 2) as g:
                        for j in range(2):
                            gelu(b * PAIRS_N + g + (PAIRS_A - 2), j)
                    turned(b, BLK)
                    with act.Fori(0, PAIRS_B) as g:
                        for j in range(2):
                            gelu(b * PAIRS_N + g + PAIRS_A, j)
                            gates(b, g, 2 * j)
                            gates(b, g, 2 * j + 1)
                    with act.Fori(0, BLK // (4 * GT) - PAIRS_B) as g:
                        for k in range(4):
                            gates(b, g + PAIRS_B, k)
                    save(b, BLK, bass.ds(b * BLK, BLK))
                scores(NB, DEC)
                with act.Fori(0, PAIRS_END - 1) as g:
                    for j in range(2):
                        gelu(g + NB * PAIRS_N, j)
                soften(NB, DEC)
                for j in range(2):
                    gelu(NK // 2 - 1, j, ahead=False)
                turned(NB, DEC)
                with act.Fori(0, DEC // (4 * GT)) as g:
                    for k in range(4):
                        gates(NB, g, k)
                save(NB, DEC, slice(SEQ, T))
                with act.Fori(0, ESTEPS // 2) as e2:
                    for half in range(2):
                        for j in range(EC):
                            act.wait_ge(eo_done, (L * ESTEPS + e2 * 2 + half + 1) * KD)
                            act.wait_ge(w_ready, L * NK + e2 * (2 * EC) + (half * EC + j + 1 + EC))
                            av(wth[half * EC + j], wf[j % 2], ACT.Copy).then_inc(wh_ready, 1)
                norm(L * 3 + 3, 2)
                with act.Fori(0, PLE_T // 2) as g:
                    for j in range(2):
                        done(L, PLE_0, g * 2 + j)
                        act.wait_ge(ple_free, L * (PLE_T + 2) + g * 2 + j + 1)
                        av(cut(sg[j], HALF), halves(2 * j, HALF), ACT.Sigmoid).then_inc(ple_sig, 1)
            norm(3 * DEPTH + 1, 2)

        @block.vector
        def _(dve):
            ts, tt, stt = nc.vector.tensor_scalar, nc.vector.tensor_tensor, nc.vector.scalar_tensor_tensor
            copy = nc.vector.tensor_copy
            dve.memset(epst[:, 0:1], EPS)
            dve.memset(epst[:, 1:2], GN_EPS)
            dve.drain()
            dve.sem_inc(layer_free, 1)
            dve.sem_inc(w_ready, EC)
            dve.sem_inc(eo_out, 2)
            dve.wait_ge(const_in, 16)
            dve.wait_ge(x_in, 16)

            def norm(n, gain, last_sem):
                dve.wait_ge(rms_ready, n)
                dve.reciprocal(rms, rms)
                dve.drain()
                for k in range(KD):
                    stt(xn[:, k, :], h[:, k, :], small_of(gain, k), rms, ALU.mult, ALU.mult).then_inc(last_sem, 1)

            def add_tile(k, bank):
                at = h[:, k, :].rearrange("p a t -> p (a t)") if not isinstance(k, int) else h[:, k, :]
                return tt(cut(at, HALF), halves(bank, HALF), cut(at, HALF), ALU.add)

            with dve.Fori(0, DEPTH) as L:
                dve.drain()
                dve.sem_inc(h_ready, 1)
                dve.wait_ge(small_in, L * 16 + 16)
                dve.memset(zin[:, :, 0:LEAD], 0.0)
                dve.memset(zin[:, :, SEQ + LEAD:SEQ + 2 * LEAD], 0.0)
                stt(sp[:, 0:4], small_of("lam", 0, 4), -1.0, small_of("lam", 0, 4), ALU.mult, ALU.max).then_inc(lam_abs, 1)
                ts(sp[:, 36:40], small_of("lam", 0, 4), -1.0, 0.0, ALU.mult, ALU.max)
                dve.drain()
                copy(zin[:, 0:NT, SEQ + LEAD:SEQ + 2 * LEAD], small_of("cst", 0, 12).rearrange("p (n t) -> p n t", n=NT))
                copy(zin[:, 2 * NT:ZT, DEC0 + 2:DEC0 + 3], small_of("sst", 0, 14).rearrange("p (n t) -> p n t", n=ZR))
                norm(L * 3 + 1, "n1", xn_ready)
                dve.wait_ge(lam_exp, L + 1)
                ts(sp[:, 8:12], sp[:, 4:8], 1.0, None, ALU.add)
                dve.drain()
                ts(sp[:, 12:16], sp[:, 8:12], -1.0, None, ALU.add).then_inc(lam_u, 1)
                dve.wait_ge(lam_ln, L + 1)
                passed(dve)
                dve.drain()
                ts(sp[:, 20:24], sp[:, 12:16], 0.0, None, ALU.is_equal)
                dve.drain()
                tt(sp[:, 24:28], sp[:, 16:20], sp[:, 20:24], ALU.add)
                tt(sp[:, 28:32], sp[:, 12:16], sp[:, 20:24], ALU.add)
                dve.drain()
                dve.reciprocal(sp[:, 28:32], sp[:, 28:32])
                tt(sp[:, 24:28], sp[:, 24:28], sp[:, 4:8], ALU.mult)
                dve.drain()
                tt(sp[:, 24:28], sp[:, 24:28], sp[:, 28:32], ALU.mult)
                dve.drain()
                tt(sp[:, 24:28], sp[:, 24:28], sp[:, 36:40], ALU.add)
                dve.drain()
                ts(sp[:, 32:36], sp[:, 24:28], -8.0, None, ALU.mult).then_inc(nsp_ready, 1)
                xc = TB[0]
                dve.wait_ge(in_free, L * (IN_T + 2) + 2 + NT)
                dve.memset(xc[:, :, EW:MW], 0.0)
                for tap in range(4):
                    for n in range(NT):
                        src = zin[:, n, tap:tap + EW]
                        w = small_of("cw", tap * NT + n)
                        if tap == 0:
                            last = ts(xc[:, n, 0:EW], src, w, small_of("cb", n), ALU.mult, ALU.add)
                        else:
                            last = stt(xc[:, n, 0:EW], src, w, xc[:, n, 0:EW], ALU.mult, ALU.add)
                    if tap < 3:
                        dve.drain()
                last.then_inc(xc_ready, 1)
                zt = zin[:, 2 * NT:ZT, :]
                dve.memset(zs[:, :, EW:MW], 0.0)
                for m in range(ZR):
                    dve.wait_ge(in_free, L * (IN_T + 2) + (2 + 2 * NT + m + 1))
                    tt(zs[:, m, 0:EW], zt[:, m, LEAD - 1:LEAD - 1 + EW], zt[:, m, LEAD:LEAD + EW], ALU.subtract)
                    dve.drain()
                    stt(zs[:, m, 0:EW], zs[:, m, 0:EW], small_of("mu", m), zt[:, m, LEAD:LEAD + EW], ALU.mult, ALU.add)
                for w, (c0, c1) in enumerate([(SEQ, SEQ + LEAD), (ZW - LEAD, ZW)]):
                    copy(sout[:, SO["conv"][0] + 12 * w:SO["conv"][0] + 12 * w + 12].rearrange("p (n t) -> p n t", n=NT),
                         zin[:, 0:NT, c0:c1])
                    last = copy(sout[:, SO["shift"][0] + 14 * w:SO["shift"][0] + 14 * w + 14].rearrange("p (n t) -> p n t", n=ZR),
                                zt[:, :, c1 - 1:c1])
                last.then_inc(zs_ready, 1)
                dve.wait_ge(i_out, L + 1)
                tt(TB[2][:, :, :], TB[2][:, :, :], xc[:, :, :], ALU.mult)
                dve.wait_ge(a_ready, L + 1)
                tt(TB[5][:, :, :], TB[4][:, :, :], TB[4][:, :, :], ALU.mult)
                dve.drain()
                stt(TB[5][:, :, :], TB[5][:, :, :], 1.0, TB[3][:, :, :], ALU.add, ALU.mult).then_inc(m2_ready, 1)
                dve.wait_ge(mult_ready, L + 1)
                dve.memset(TB[5][:, :, 0:1], 1.0)
                dve.drain()
                tt(TB[2][:, :, :], TB[2][:, :, :], TB[5][:, :, :], ALU.mult)
                dve.drain()
                for n in range(NT):
                    nc.vector.tensor_tensor_scan(TB[6][:, n, 0:SEQ], TB[4][:, n, 0:SEQ], TB[2][:, n, 0:SEQ], 0.0, ALU.mult, ALU.add)
                    nc.vector.tensor_tensor_scan(TB[6][:, n, DEC0:EW], TB[4][:, n, DEC0:EW], TB[2][:, n, DEC0:EW],
                                                 small_of("lst", n), ALU.mult, ALU.add)
                dve.drain()
                for w, c in enumerate([SEQ - 1, EW - 1]):
                    copy(sout[:, SO["lru"][0] + 4 * w:SO["lru"][0] + 4 * w + 4].rearrange("p (n t) -> p n t", n=NT), TB[6][:, :, c:c + 1])
                dve.wait_ge(gg_ready, L + 1)
                tt(ymix[:, 0:NT, 0:SEQ], TB[6][:, :, 0:SEQ], zin[:, NT:2 * NT, LEAD:LEAD + SEQ], ALU.mult)
                tt(ymix[:, 0:NT, SEQ:T], TB[6][:, :, DEC0:EW], zin[:, NT:2 * NT, ZW - DEC:ZW], ALU.mult).then_inc(lru_done, 1)
                dve.drain()
                r_, k_, v_ = zs[:, 0:4, :], zs[:, 4:8, :], zs[:, 8:12, :]
                for n in range(NT):
                    ts(TB[2][:, n, :], k_[:, n, :], small_of("kk", n), None, ALU.mult)
                dve.drain()
                tt(TB[3][:, :, :], TB[2][:, :, :], TB[2][:, :, :], ALU.mult).then_inc(kk_sq, 1)
                ts(sp[:, 0:4], small_of("ka", 0, 4), -1.0, 1.0, ALU.mult, ALU.add)
                dve.wait_ge(dec_out, L + 1)
                ts(TB[0][:, :, :], TB[0][:, :, :], -float(np.exp(-0.5)), None, ALU.mult)
                dve.drain()
                dve.memset(TB[0][:, :, EW:MW], 0.0)
                dve.drain()
                for n in range(NT):
                    nc.vector.tensor_tensor_scan(TB[1][:, n, :], reset, TB[0][:, n, :], 0.0, ALU.mult, ALU.add)
                dve.drain()
                tt(TB[0][:, :, :], TB[1][:, :, :], TB[0][:, :, :], ALU.subtract)
                dve.wait_ge(kk_rt, L + 1)
                dve.wait_ge(icl_out, L + 1)
                ts(TB[6][:, :, :], TB[6][:, :, :], 1e-12, None, ALU.max)
                dve.drain()
                dve.reciprocal(TB[6][:, :, :], TB[6][:, :, :])
                dve.drain()
                tt(TB[2][:, :, :], TB[2][:, :, :], TB[6][:, :, :], ALU.mult)
                dve.drain()
                for n in range(NT):
                    ts(TB[6][:, n, :], TB[4][:, n, :], small_of("ka", n), sp[:, n:n + 1], ALU.mult, ALU.add)
                tt(TB[3][:, :, :], TB[2][:, :, :], TB[4][:, :, :], ALU.mult)
                dve.drain()
                tt(k_, k_, TB[6][:, :, :], ALU.mult)
                dve.drain()
                for n in range(NT):
                    last = stt(TB[6][:, n, :], r_[:, n, :], small_of("rk", n), k_[:, n, :], ALU.mult, ALU.mult)
                last.then_inc(bonus_in, 1)
                for s in slots:
                    dve.memset(s.vc[0:HD, :, 0:C], 0.0)
                    dve.memset(s.vc[HD:P, :, C:P], 0.0)
                dve.memset(st[:, :, :], 0.0)
                dve.wait_ge(bonus_done, L + 1)
                for n in range(NT):
                    last = tt(cut(TB[4][:, n, :], MH), halves(2 * n, MH), cut(v_[:, n, :], MH), ALU.mult)
                last.then_inc(cum_ready, 1)
                dve.wait_ge(exp_ready, L + 1)
                passed(dve)

                eyes = eye.unsqueeze(1).to_broadcast([P, NT, C])

                def tilde(s, col):
                    for q, (b_at, k_at) in ((0, (0, C)), (HD, (C, 0))):
                        tt(s.bk[q:q + HD, :, b_at:b_at + C], TB[3][q:q + HD, :, col], TB[6][q:q + HD, :, col], ALU.mult)
                        tt(s.bk[q:q + HD, :, k_at:k_at + C], k_[q:q + HD, :, col], TB[6][q:q + HD, :, col], ALU.mult)
                    tt(s.ar[:, :, C:P], r_[:, :, col], TB[1][:, :, col], ALU.mult)
                    stt(s.ar[:, :, 0:C], TB[2][:, :, col], -1.0, TB[0][:, :, col], ALU.mult, ALU.mult).then_inc(s.tilde_ready, 1)

                def mask(s, lv):
                    m = cn[:, CN["level"] + lv * C:CN["level"] + (lv + 1) * C]
                    return tt(s.ml[lv % 2], s.amT, m.unsqueeze(1).to_broadcast([P, NT, C]), ALU.mult)

                def first(s, k):
                    dve.wait_ge(s.pair_done, L * s.per + k + 1)
                    for q in (0, HD):
                        tt(s.amT[q:q + C], ps[q:q + C, s.bank + q // HD, :].rearrange("p (m t) -> p m t", m=NT)[:, :, 0:C],
                           causal[q:q + C, 0:C].unsqueeze(1).to_broadcast([C, NT, C]), ALU.mult)
                    dve.drain()
                    mask(s, 0).then_inc(s.m_ready, 1)
                    dve.drain()
                    tt(s.xt, s.ml[0], eyes, ALU.add)
                    mask(s, 1)

                def second(s, k):
                    dve.wait_ge(s.y_done, (L * s.per + k) * LEVELS + 1)
                    tt(s.xi, s.psum(2), eyes, ALU.add).then_inc(s.m_ready, 1)
                    for b in range(2):
                        last = tt(s.gm[:, b:HEADS:2, :], ps[:, s.bank + b, :].rearrange("p (h t) -> p h t", h=4),
                                  causal.unsqueeze(1).to_broadcast([P, 4, P]), ALU.mult)
                    last.then_inc(s.gm_ready, 1)

                def level(s, k, lv):
                    if lv + 1 < LEVELS:
                        mask(s, lv + 1)
                    dve.wait_ge(s.x_done, (L * s.per + k) * (LEVELS - 1) + lv)
                    if lv + 1 < LEVELS:
                        tt(s.xx, ps[:, s.bank + 3, :], s.xx, ALU.add).then_inc(s.m_ready, 1)
                    else:
                        tt(s.xt, s.psum(3, NT * C), s.xt, ALU.add).then_inc(s.m_ready, 1)

                def carry(s, k, end):
                    dve.wait_ge(s.step_done, L * s.per + k + 1)
                    for q in (0, HD):
                        at = st[q:q + HD, :, q:q + HD]
                        tt(at, s.psum(1)[q:q + HD], at, ALU.add)
                    dve.drain()
                    for q in (0, HD):
                        at = st[q:q + HD, :, q:q + HD]
                        tt(at, at, TB[1][q:q + HD, :, end].to_broadcast([HD, NT, HD]), ALU.mult)
                    dve.drain()

                def chunks(k, work, col, end):
                    for s in work:
                        tilde(s, col(s))
                    for s in work:
                        first(s, k)
                    for s in work:
                        second(s, k)
                    dve.drain()
                    for lv in range(1, LEVELS):
                        for s in work:
                            level(s, k, lv)
                    for s in work:
                        carry(s, k, end(s))
                        if s.i == 0 and len(work) == 2:
                            dve.sem_inc(state_ready, 1)

                with dve.Fori(0, NCH // 2) as k:
                    chunks(k, slots, lambda s: bass.ds(k * (2 * C) + s.i * C, C),
                           lambda s: bass.ds(k * (2 * C) + (s.i * C + C - 1), 1))
                dve.wait_ge(wkv_in, L * 16 + 16)
                for q in (0, HD):
                    copy(stp[q:q + HD, :, :], st[q:q + HD, :, q:q + HD])
                dve.drain()
                for q in (0, HD):
                    copy(st[q:q + HD, :, q:q + HD], sts[q:q + HD, :, :])
                chunks(NCH // 2, slots[:1], lambda s: slice(DEC0, DEC0 + C), lambda s: slice(DEC0 + C - 1, DEC0 + C))
                for q in (0, HD):
                    copy(sts[q:q + HD, :, :], st[q:q + HD, :, q:q + HD])
                dve.drain()
                dve.sem_inc(outs_ready, 1)
                dve.wait_ge(mean_done, L + 1)
                for n in range(NT):
                    stt(cut(TB[0][:, n, :], MH), halves(2 * n, MH), -1.0 / HD, cut(o[:, n, :], MH), ALU.mult, ALU.add)
                dve.drain()
                tt(TB[6][:, :, :], TB[0][:, :, :], TB[0][:, :, :], ALU.mult).then_inc(oc_ready, 1)
                dve.wait_ge(std_out, L + 1)
                dve.reciprocal(TB[6][:, :, :], TB[6][:, :, :])
                dve.drain()
                tt(TB[0][:, :, :], TB[0][:, :, :], TB[6][:, :, :], ALU.mult)
                dve.drain()
                for n in range(NT):
                    ts(TB[0][:, n, :], TB[0][:, n, :], small_of("lnw", n), small_of("lnb", n), ALU.mult, ALU.add)
                dve.drain()
                tt(TB[0][:, :, :], TB[0][:, :, :], TB[4][:, :, :], ALU.add)
                dve.drain()
                tt(ymix[:, NT:KD, 0:SEQ], TB[0][:, :, 0:SEQ], TB[5][:, :, 0:SEQ], ALU.mult)
                tt(ymix[:, NT:KD, SEQ:T], TB[0][:, :, DEC0:EW], TB[5][:, :, DEC0:EW], ALU.mult).then_inc(y_ready, 1)
                dve.drain()
                dve.sem_inc(out_free, 2)
                with dve.Fori(0, OUT_T // 2) as g:
                    for j in range(2):
                        dve.wait_ge(tile_done, L * TILES + OUT_0 + g * 2 + j + 3)
                        add_tile(bass.ds(g * 2 + j, 1), 2 * j).then_inc(out_free, 1)
                dve.wait_ge(stored, (L + 1) * 48)
                passed(dve)
                dve.drain()
                dve.sem_inc(h_ready, 1)
                norm(L * 3 + 2, "n2", xn_ready)

                def top16(nt, src, spare, n, width, vals, idx):
                    mx, mi, mr = nc.vector.max, nc.vector.max_index, nc.vector.match_replace
                    for q in range(n):
                        mx(vals[0:nt, q, 0:8], src(q))
                    dve.drain()
                    for q in range(n):
                        mi(idx[0:nt, q, 0:8], vals[0:nt, q, 0:8], src(q))
                        last = mr(spare[0:nt, q * width:(q + 1) * width], vals[0:nt, q, 0:8], src(q), NEG)
                    dve.drain()
                    for q in range(n):
                        mx(vals[0:nt, q, 8:16], spare[0:nt, q * width:(q + 1) * width])
                    dve.drain()
                    for q in range(n):
                        mi(idx[0:nt, q, 8:16], vals[0:nt, q, 8:16], spare[0:nt, q * width:(q + 1) * width])
                    dve.drain()

                def route(b, nt):
                    n = L * NBLK + b
                    dve.wait_ge(sc_read, n + 1)
                    passed(dve)
                    top16(nt, lambda q: s2[0:nt, q * NK:(q + 1) * NK], s1, QH, NK, tv, ti.bitcast(U32))
                    copy(tf[0:nt], ti[0:nt].bitcast(U32))
                    tvs = tv[0:nt].rearrange("p (q w) k -> p q w k", w=2)
                    cand = s2[0:nt].rearrange("p (q a b) -> p q a b", q=PH, a=TOPK)
                    shape = [nt, PH, TOPK, TOPK]
                    tt(cand, tvs[:, :, 0, :].unsqueeze(3).to_broadcast(shape),
                       tvs[:, :, 1, :].unsqueeze(2).to_broadcast(shape), ALU.add)
                    dve.drain()
                    top16(nt, lambda q: s2[0:nt, q * 256:(q + 1) * 256], s1, PH, 256, bv, bi.bitcast(U32))
                    mxs = bv[0:nt, :, 0:1]
                    copy(gsum[0:nt], mxs)
                    dve.drain()
                    tt(bv[0:nt], bv[0:nt], gsum[0:nt].unsqueeze(2).to_broadcast([nt, PH, TOPK]), ALU.subtract).then_inc(best_ready, 1)
                    ts(ba[0:nt, 0].bitcast(U32), bi[0:nt].bitcast(U32), 4, None, ALU.logical_shift_right)
                    ts(ba[0:nt, 1].bitcast(U32), bi[0:nt].bitcast(U32), 15, None, ALU.bitwise_and)
                    dve.drain()
                    copy(bf[0:nt], ba[0:nt].bitcast(U32))
                    dve.drain()
                    eq = s2[0:nt].rearrange("p (q k j) -> p q k j", q=PH, k=TOPK)
                    eq3 = s2[0:nt].rearrange("p (q j) -> p q j", q=PH * TOPK)
                    tfs = tf[0:nt].rearrange("p (q w) k -> p q w k", w=2)
                    for w in range(2):
                        b3 = bf[0:nt, w].rearrange("p q k -> p (q k)").unsqueeze(2).to_broadcast([nt, PH * TOPK, TOPK])
                        i3 = iota[0:nt, 0:TOPK].unsqueeze(1).to_broadcast([nt, PH * TOPK, TOPK])
                        tt(eq3, b3, i3, ALU.is_equal)
                        dve.drain()
                        tt(eq, eq, tfs[:, :, w, :].unsqueeze(2).to_broadcast(shape), ALU.mult)
                        dve.drain()
                        nc.vector.tensor_reduce(sel_t[0:nt, 1 + w, :], eq3, AX.X, ALU.add)
                        dve.drain()
                    dve.wait_ge(gexp, n + 1)
                    nc.vector.tensor_reduce(gsum[0:nt], bv[0:nt], AX.X, ALU.add)
                    dve.drain()
                    dve.reciprocal(gsum[0:nt], gsum[0:nt])
                    dve.drain()
                    tt(sel_t[0:nt, 0, :].rearrange("p (q k) -> p q k", q=PH), bv[0:nt],
                       gsum[0:nt].unsqueeze(2).to_broadcast([nt, PH, TOPK]), ALU.mult).then_inc(sel_ready, 1)
                    dve.wait_ge(selT_out, n + 1)
                    passed(dve)
                    with dve.Fori(0, nt // (2 * GT)) as g:
                        for s in range(2):
                            i = L * GROUPS + b * (BLK // GT) + g * 2 + s
                            dve.wait_ge(gmat_done, i + 1)
                            for hot, w in ((oneB, 2), (oneA, 1)):
                                number = sel[:, w, bass.ds(g * (2 * GT) + s * GT, GT)]
                                tt(hot[:, s], iota.unsqueeze(1).to_broadcast([P, GT, P]),
                                   number.unsqueeze(2).to_broadcast([P, GT, P]), ALU.is_equal).then_inc(hot_ready, 1)

                with dve.Fori(0, NB) as b:
                    route(b, BLK)
                route(NB, DEC)

                def high_v(e, half, j):
                    dve.wait_ge(v_in[j % 2], L * (8 * NK) + e * (8 * EC) + 16 * (j // 2) + 16)
                    dve.wait_ge(eo_done, (L * ESTEPS + e + 1) * KD)
                    passed(dve)
                    copy(vh[half * EC + j], vraw[j % 2]).then_inc(vh_ready, 1)

                def weigh(e, half, j):
                    dve.drain()
                    dve.wait_ge(g_in[j], (L * ESTEPS + e + 1) * 32)
                    tt(wf[j % 2], gf[j], gs[j], ALU.mult).then_inc(w_ready, 1)

                def low_w(e, half, j):
                    dve.wait_ge(wh_ready, L * NK + e * EC + j + 1)
                    tt(wtl[half * EC + j], wf[j % 2], wth[half * EC + j].bitcast(F32), ALU.subtract).then_inc(wl_ready, 1)

                prepare = [[(high_v, 0), (high_v, 1)], [(weigh, 0), (weigh, 1)], [(high_v, 2), (low_w, 0)],
                           [(weigh, 2), (low_w, 1)], [(high_v, 3), (weigh, 3)], [(low_w, 2), (low_w, 3)], [], []]

                def add(e, m):
                    dve.wait_ge(eo_done, (L * ESTEPS + e) * KD + m + 1 + 2 * KD)
                    add_tile(m, 4 + m % 2 * 2).then_inc(eo_out, 1)

                def step(e, half):
                    for m in range(KD):
                        add(e, m)
                        for make, j in prepare[m]:
                            make(e + 1, 1 - half, j)

                for part in prepare:
                    for make, j in part:
                        make(0, 0, j)
                with dve.Fori(0, ESTEPS // 2 - 1) as e2:
                    step(e2 * 2, 0)
                    step(e2 * 2 + 1, 1)
                step(ESTEPS - 2, 0)
                for m in range(KD):
                    add(ESTEPS - 1, m)
                dve.drain()
                dve.sem_inc(h_ready, 1)
                norm(L * 3 + 3, "n3", xn_ready)
                dve.drain()
                dve.sem_inc(ple_free, 2)
                with dve.Fori(0, PLE_T // 2) as g:
                    for j in range(2):
                        dve.wait_ge(ple_sig, L * PLE_T + g * 2 + j + 1)
                        tt(cut(pg[j], HALF), halves(4 + 2 * j, HALF), cut(sg[j], HALF), ALU.mult)
                        dve.drain()
                        at = h[:, bass.ds(g * 2 + j, 1), :].rearrange("p a t -> p (a t)")
                        tt(at, at, pg[j], ALU.add).then_inc(ple_free, 1)
                dve.drain()
                dve.sem_inc(layer_free, 1)
            dve.sem_inc(h_ready, 1)
            norm(3 * DEPTH + 1, "fin", y_out_ready)


def kernel(**inputs):
    import concourse.bacc as bacc
    from concourse.bass_utils import run_bass_kernel_spmd

    nc = bacc.Bacc("TRN2", target_bir_lowering=False, num_devices=1)
    arrays = lay_out(inputs)
    args = []
    for name, a in arrays.items():
        args.append(nc.dram_tensor(f"in_{name}", a.shape, mybir.dt.from_np(a.dtype), kind="ExternalInput").ap())
    for name, shape in OUTS.items():
        args.append(nc.dram_tensor(f"out_{name}", shape, F32, kind="ExternalOutput").ap())
    trunk(nc, *args)
    r = run_bass_kernel_spmd(nc, [{f"in_{n}": a for n, a in arrays.items()}], core_ids=[0]).results[0]
    return give_back({n: r[f"out_{n}"] for n in OUTS})


OUTS = {"y": (P, KD, T), "small": (DEPTH, P, NSO), "wkv": (DEPTH, 2, P, NT, HD)}


def lay_out(i):
    i = {k: np.asarray(a) for k, a in i.items()}

    def cols(a, axis=1):
        return np.swapaxes(a.reshape(DEPTH, -1, P), 1, 2)

    x = np.concatenate([i["x_prompt"][0], i["x_sample"][0]], 0).T.reshape(KD, P, T).transpose(1, 0, 2)
    p = np.concatenate([i["p_prompt"][:, 0], i["p_sample"][:, 0]], 1).transpose(0, 2, 1).reshape(DEPTH, 2, P, T).transpose(0, 2, 1, 3)
    small = np.zeros((DEPTH, P, NSM), np.float32)

    def put(name, a):
        small[:, :, SM[name]:SM[name] + a.shape[2]] = a

    put("n1", cols(i["norm1_g"]))
    put("n2", cols(i["norm2_g"]))
    put("n3", cols(i["norm3_g"]))
    put("fin", cols(np.stack([i["final_g"]] * DEPTH)))
    put("cw", cols(i["conv_w"].reshape(DEPTH, -1)))
    for name, key in [("cb", "conv_b"), ("ba", "lru_ba"), ("bx", "lru_bx"), ("lam", "lru_lambda"), ("mu", "rwkv_mu"),
                      ("w0", "rwkv_w0"), ("a0", "rwkv_a0"), ("kk", "rwkv_kk"), ("ka", "rwkv_ka"),
                      ("rk", "rwkv_rk"), ("lnw", "rwkv_ln_w"), ("lnb", "rwkv_ln_b")]:
        put(name, cols(i[key].reshape(DEPTH, -1)))
    put("cst", i["state_conv"][:, 0].reshape(DEPTH, 3, NT, P).transpose(0, 3, 2, 1).reshape(DEPTH, P, 12))
    put("lst", cols(i["state_lru"][:, 0]))
    put("sst", cols(i["state_shift"][:, 0]))
    mixw = np.stack([i["lru_wa"].transpose(0, 2, 1, 3).reshape(DEPTH, P, LW),
                     i["lru_wx"].transpose(0, 2, 1, 3).reshape(DEPTH, P, LW),
                     np.concatenate([i["rwkv_w2"], i["rwkv_a2"]], 1), i["rwkv_g2"]], 2)
    wkv0 = i["state_wkv"][:, 0].reshape(DEPTH, NT, 2, HD, HD).transpose(0, 2, 4, 1, 3).reshape(DEPTH, P, NT, HD)
    keys = i["peer_keys"].reshape(DEPTH, QH, NK, P).transpose(0, 3, 1, 2)
    ut = i["peer_u"].reshape(DEPTH, NK, NK, KD, P).transpose(0, 2, 4, 3, 1)
    wple = np.concatenate([i["ple_gate"], i["ple_w"]], 1)
    out = dict(x=x, p=p, small=small, const=constants(), mixw=mixw, wkv0=wkv0, w_in=i["w_in"], w_out=i["w_out"],
               wq=i["peer_wq"], keys=keys, ut=ut, v=i["peer_v"], wple=wple)
    return {k: np.ascontiguousarray(a) for k, a in out.items()}


def give_back(r):
    y = r["y"].transpose(2, 1, 0).reshape(T, D)
    so, wk = r["small"], r["wkv"]

    def cols(name, w):
        at, n = SO[name]
        return so[:, :, at + n * w:at + n * w + n]

    res = []
    for w in range(2):
        conv = cols("conv", w).reshape(DEPTH, P, NT, 3).transpose(0, 3, 2, 1).reshape(DEPTH, 1, 3, LW)
        lru = cols("lru", w).transpose(0, 2, 1).reshape(DEPTH, 1, LW)
        shift = cols("shift", w).transpose(0, 2, 1).reshape(DEPTH, 1, RCOLS)
        wkv = wk[:, w].reshape(DEPTH, 2, HD, NT, HD).transpose(0, 3, 1, 4, 2).reshape(DEPTH, 1, HEADS, HD, HD)
        res += [conv, lru, shift, wkv]
    return tuple(np.ascontiguousarray(a) for a in [y[None, :SEQ], y[None, SEQ:]] + res)
```
